# Optimizing a Trainium2 kernel written in Bass

```python
import math
import jax
import jax.numpy as jnp
from jax import lax
import numpy as np
import jax, jax.numpy as jnp

D_MODEL = 1024
BATCH = 1
SEQ = 256
DEPTH = 2

HEAD_DIM = 64
N_HEADS_A = 8
N_HEADS_B = 8
N_HEADS_C = 8
N_HEADS_D = 8
MOBA_BLOCK = 256
MOBA_TOPK = 3
MOBA_Q_CHUNK = 32
DILATED_BRANCHES = ((128, 1), (512, 4), (2048, 16))
Q_BLOCK = 128
MLA_Q_RANK = 256
MLA_KV_RANK = 256
MLA_NOPE_DIM = 64
MLA_ROPE_DIM = 32
MLA_V_DIM = 64
ROPE_THETA = 10000.0
REL_BUCKETS = 32
REL_MAX_DIST = 2048
D_FF = 2816
CONV_WIDTH = 3
NORM_EPS = 1e-6
N_EVEN = (DEPTH + 1) // 2
N_ODD = DEPTH // 2
AB_IN = 3 * HEAD_DIM * (N_HEADS_A + N_HEADS_B)
AB_OUT = HEAD_DIM * (N_HEADS_A + N_HEADS_B)
CD_IN = MLA_Q_RANK + MLA_KV_RANK + MLA_ROPE_DIM + 3 * HEAD_DIM * N_HEADS_D
CD_OUT = MLA_V_DIM * N_HEADS_C + HEAD_DIM * N_HEADS_D


def rmsnorm(x, g):
    x32 = x.astype(jnp.float32)
    y = x32 * lax.rsqrt(jnp.mean(x32 * x32, axis=-1, keepdims=True) + NORM_EPS)
    return (y * g.astype(jnp.float32)).astype(x.dtype)

def t5_bucket(dist):
    dist = jnp.maximum(dist, 0)
    max_exact = REL_BUCKETS // 2
    d_f = jnp.maximum(dist, max_exact).astype(jnp.float32)
    large = max_exact + (jnp.log(d_f / max_exact) / math.log(REL_MAX_DIST / max_exact)
                         * (REL_BUCKETS - max_exact)).astype(jnp.int32)
    large = jnp.minimum(large, REL_BUCKETS - 1)
    return jnp.where(dist < max_exact, dist, large)

def split_cols(t, sizes):
    return jnp.split(t, [int(o) for o in np.cumsum(sizes)[:-1]], axis=-1)

def to_heads(t, n_heads):
    b, s, _ = t.shape
    return t.reshape(b, s, n_heads, -1).transpose(0, 2, 1, 3)

def from_heads(t):
    b, h, s, d = t.shape
    return t.transpose(0, 2, 1, 3).reshape(b, s, h * d)

def query_blocks(q, qb):
    b, h, s, d = q.shape
    return q.reshape(b, h, s // qb, qb, d).transpose(2, 0, 1, 3, 4)

def merge_blocks(o):
    n, b, h, qb, d = o.shape
    return o.transpose(1, 2, 0, 3, 4).reshape(b, h, n * qb, d)

def rope_tables(s):
    inv_freq = 1.0 / (ROPE_THETA ** (jnp.arange(0, MLA_ROPE_DIM, 2, dtype=jnp.float32) / MLA_ROPE_DIM))
    ang = jnp.arange(s, dtype=jnp.float32)[:, None] * inv_freq[None, :]
    return jnp.cos(ang), jnp.sin(ang)

def apply_rope(x, cos, sin):
    cos = cos[:, None, :].astype(x.dtype)
    sin = sin[:, None, :].astype(x.dtype)
    x1, x2 = jnp.split(x, 2, axis=-1)
    return jnp.concatenate([x1 * cos - x2 * sin, x1 * sin + x2 * cos], axis=-1)

def moba_attention(q, k, v, bias_table):
    b, h, s, dh = q.shape
    nb = -(-s // MOBA_BLOCK)
    pad = nb * MOBA_BLOCK - s
    kp = jnp.pad(k, ((0, 0), (0, 0), (0, pad), (0, 0)))
    vp = jnp.pad(v, ((0, 0), (0, 0), (0, pad), (0, 0)))
    kb = kp.reshape(b, h, nb, MOBA_BLOCK, dh)
    vb = vp.reshape(b, h, nb, MOBA_BLOCK, dh)
    k_mean = jnp.mean(kb, axis=3)
    scale = dh ** -0.5
    topk = min(MOBA_TOPK, nb)
    head_idx = jnp.arange(h)[:, None, None, None]
    blk_offsets = jnp.arange(MOBA_BLOCK)
    gather_blocks = jax.vmap(jax.vmap(lambda arr, idx: arr[idx]))

    def chunk_fn(args):
        qc, ci = args
        t = ci * MOBA_Q_CHUNK + jnp.arange(MOBA_Q_CHUNK)
        own = t[0] // MOBA_BLOCK
        gate = jnp.einsum('bhqd,bhnd->bhqn', qc, k_mean).astype(jnp.float32)
        past = jnp.arange(nb)[None, :] < (t // MOBA_BLOCK)[:, None]
        gate = jnp.where(past, gate, -jnp.inf)
        _, sel = lax.top_k(gate, topk)
        sel_valid = sel < own
        k_sel = gather_blocks(kb, sel)
        v_sel = gather_blocks(vb, sel)
        pos_sel = sel[..., None] * MOBA_BLOCK + blk_offsets
        logit_sel = (jnp.einsum('bhqd,bhqkld->bhqkl', qc, k_sel).astype(jnp.float32) * scale
                     + bias_table[head_idx, t5_bucket(t[:, None, None] - pos_sel)].astype(jnp.float32))
        logit_sel = jnp.where(sel_valid[..., None], logit_sel, -jnp.inf)
        k_own = lax.dynamic_slice_in_dim(kp, own * MOBA_BLOCK, MOBA_BLOCK, axis=2)
        v_own = lax.dynamic_slice_in_dim(vp, own * MOBA_BLOCK, MOBA_BLOCK, axis=2)
        pos_own = own * MOBA_BLOCK + blk_offsets
        logit_own = (jnp.einsum('bhqd,bhld->bhql', qc, k_own).astype(jnp.float32) * scale
                     + bias_table[:, t5_bucket(t[:, None] - pos_own[None, :])].astype(jnp.float32))
        logit_own = jnp.where(pos_own[None, :] <= t[:, None], logit_own, -jnp.inf)
        logits = jnp.concatenate([logit_sel.reshape(b, h, MOBA_Q_CHUNK, topk * MOBA_BLOCK), logit_own], axis=-1)
        p = jax.nn.softmax(logits, axis=-1)
        p_sel = p[..., :topk * MOBA_BLOCK].reshape(b, h, MOBA_Q_CHUNK, topk, MOBA_BLOCK).astype(v.dtype)
        p_own = p[..., topk * MOBA_BLOCK:].astype(v.dtype)
        return (jnp.einsum('bhqkl,bhqkld->bhqd', p_sel, v_sel)
                + jnp.einsum('bhql,bhld->bhqd', p_own, v_own))

    n_chunks = s // MOBA_Q_CHUNK
    return merge_blocks(lax.map(chunk_fn, (query_blocks(q, MOBA_Q_CHUNK), jnp.arange(n_chunks))))

def dilated_attention(q, k, v, bias_table):
    b, h, s, dh = q.shape
    scale = dh ** -0.5

    def chunk_fn(args):
        qc, ci = args
        t = ci * Q_BLOCK + jnp.arange(Q_BLOCK)
        lses, outs = [], []
        for window, dil in DILATED_BRANCHES:
            dist = dil * jnp.arange(window // dil + 1)
            pos = t[:, None] - dist[None, :]
            valid = pos >= 0
            pos_c = jnp.maximum(pos, 0)
            k_g = k[:, :, pos_c]
            v_g = v[:, :, pos_c]
            logit = (jnp.einsum('bhqd,bhqmd->bhqm', qc, k_g).astype(jnp.float32) * scale
                     + bias_table[:, t5_bucket(dist)][:, None, :].astype(jnp.float32))
            logit = jnp.where(valid, logit, -jnp.inf)
            lse = jax.nn.logsumexp(logit, axis=-1, keepdims=True)
            p = jnp.exp(logit - lse).astype(v.dtype)
            outs.append(jnp.einsum('bhqm,bhqmd->bhqd', p, v_g))
            lses.append(lse)
        w = jax.nn.softmax(jnp.concatenate(lses, axis=-1), axis=-1).astype(v.dtype)
        return jnp.einsum('bhqr,rbhqd->bhqd', w, jnp.stack(outs))

    n_chunks = s // Q_BLOCK
    return merge_blocks(lax.map(chunk_fn, (query_blocks(q, Q_BLOCK), jnp.arange(n_chunks))))

def causal_softmax_attention(q, k, v):
    s = q.shape[2]
    scale = q.shape[-1] ** -0.5
    kpos = jnp.arange(s)

    def block_fn(args):
        qc, bi = args
        t = bi * Q_BLOCK + jnp.arange(Q_BLOCK)
        logits = jnp.einsum('bhqd,bhsd->bhqs', qc, k).astype(jnp.float32) * scale
        logits = jnp.where(kpos[None, :] <= t[:, None], logits, -jnp.inf)
        p = jax.nn.softmax(logits, axis=-1).astype(v.dtype)
        return jnp.einsum('bhqs,bhsd->bhqd', p, v)

    return merge_blocks(lax.map(block_fn, (query_blocks(q, Q_BLOCK), jnp.arange(s // Q_BLOCK))))

def mla_attention(c_q, c_kv, k_rope, q_norm_g, kv_norm_g, w_uq, w_ukv, cos, sin):
    b, s, _ = c_q.shape
    q = (rmsnorm(c_q, q_norm_g) @ w_uq).reshape(b, s, N_HEADS_C, MLA_NOPE_DIM + MLA_ROPE_DIM)
    kv = (rmsnorm(c_kv, kv_norm_g) @ w_ukv).reshape(b, s, N_HEADS_C, MLA_NOPE_DIM + MLA_V_DIM)
    q_nope, q_pe = q[..., :MLA_NOPE_DIM], q[..., MLA_NOPE_DIM:]
    k_nope, v = kv[..., :MLA_NOPE_DIM], kv[..., MLA_NOPE_DIM:]
    q_pe = apply_rope(q_pe, cos, sin)
    k_pe = apply_rope(k_rope[:, :, None, :], cos, sin)
    k_pe = jnp.broadcast_to(k_pe, (b, s, N_HEADS_C, MLA_ROPE_DIM))
    q_full = jnp.concatenate([q_nope, q_pe], axis=-1).transpose(0, 2, 1, 3)
    k_full = jnp.concatenate([k_nope, k_pe], axis=-1).transpose(0, 2, 1, 3)
    return causal_softmax_attention(q_full, k_full, v.transpose(0, 2, 1, 3))

def stick_breaking_attention(q, k, v):
    s = q.shape[2]
    scale = q.shape[-1] ** -0.5
    kpos = jnp.arange(s)

    def block_fn(args):
        qc, bi = args
        t = bi * Q_BLOCK + jnp.arange(Q_BLOCK)
        z = jnp.einsum('bhqd,bhsd->bhqs', qc, k).astype(jnp.float32) * scale
        strict = kpos[None, :] < t[:, None]
        log_keep = jnp.where(strict, jax.nn.log_sigmoid(-z), 0.0)
        rev = lax.cumsum(log_keep, axis=3, reverse=True)
        after = jnp.concatenate([rev[..., 1:], jnp.zeros_like(rev[..., :1])], axis=-1)
        a = jnp.where(strict, jnp.exp(jax.nn.log_sigmoid(z) + after), 0.0).astype(v.dtype)
        return jnp.einsum('bhqs,bhsd->bhqd', a, v)

    return merge_blocks(lax.map(block_fn, (query_blocks(q, Q_BLOCK), jnp.arange(s // Q_BLOCK))))

def even_mixer(h, w_in, w_out, rel_bias):
    proj = h @ w_in
    wa = N_HEADS_A * HEAD_DIM
    wb = N_HEADS_B * HEAD_DIM
    qa, ka, va, qb, kb, vb = split_cols(proj, [wa, wa, wa, wb, wb, wb])
    o_a = moba_attention(to_heads(qa, N_HEADS_A), to_heads(ka, N_HEADS_A), to_heads(va, N_HEADS_A),
                         rel_bias[:N_HEADS_A])
    o_b = dilated_attention(to_heads(qb, N_HEADS_B), to_heads(kb, N_HEADS_B), to_heads(vb, N_HEADS_B),
                            rel_bias[N_HEADS_A:])
    return jnp.concatenate([from_heads(o_a), from_heads(o_b)], axis=-1) @ w_out

def odd_mixer(h, w_in, q_norm_g, kv_norm_g, w_uq, w_ukv, w_out, cos, sin):
    proj = h @ w_in
    wd = N_HEADS_D * HEAD_DIM
    c_q, c_kv, k_rope, qd, kd, vd = split_cols(proj, [MLA_Q_RANK, MLA_KV_RANK, MLA_ROPE_DIM, wd, wd, wd])
    o_c = mla_attention(c_q, c_kv, k_rope, q_norm_g, kv_norm_g, w_uq, w_ukv, cos, sin)
    o_d = stick_breaking_attention(to_heads(qd, N_HEADS_D), to_heads(kd, N_HEADS_D), to_heads(vd, N_HEADS_D))
    return jnp.concatenate([from_heads(o_c), from_heads(o_d)], axis=-1) @ w_out

def conv_ffn(h, w_up, conv_w, conv_b, w_down):
    s = h.shape[1]
    u = h @ w_up
    up = jnp.pad(u, ((0, 0), (CONV_WIDTH - 1, 0), (0, 0)))
    u = sum(conv_w[j] * up[:, j:j + s] for j in range(CONV_WIDTH)) + conv_b
    gate, val = jnp.split(u, 2, axis=-1)
    return (jax.nn.gelu(gate, approximate=True) * val) @ w_down

def first_inputs(seed: int = 0) -> dict:
    key = jax.random.key(seed)
    ks = jax.random.split(key, 24)
    f32 = jnp.float32

    def dense(k, shape, fan_in, gain=1.0):
        return jax.random.normal(k, shape, f32) * (gain * fan_in ** -0.5)

    def gain(k, shape):
        return 1.0 + 0.05 * jax.random.normal(k, shape, f32)

    return {
        'x': jax.random.normal(ks[0], (BATCH, SEQ, D_MODEL), f32),
        'c': jax.random.normal(ks[1], (BATCH, D_MODEL), f32),
        'rel_bias': 0.5 * jax.random.normal(ks[2], (N_HEADS_A + N_HEADS_B, REL_BUCKETS), f32),
        'ada_w': dense(ks[3], (DEPTH, D_MODEL, 6 * D_MODEL), D_MODEL, 0.5),
        'ada_b': 0.02 * jax.random.normal(ks[4], (DEPTH, 6 * D_MODEL), f32),
        'mix_pre_g': gain(ks[5], (DEPTH, D_MODEL)),
        'mix_post_g': gain(ks[6], (DEPTH, D_MODEL)),
        'ffn_pre_g': gain(ks[7], (DEPTH, D_MODEL)),
        'ffn_post_g': gain(ks[8], (DEPTH, D_MODEL)),
        'ab_w_in': dense(ks[9], (N_EVEN, D_MODEL, AB_IN), D_MODEL),
        'ab_w_out': dense(ks[10], (N_EVEN, AB_OUT, D_MODEL), AB_OUT),
        'cd_w_in': dense(ks[11], (N_ODD, D_MODEL, CD_IN), D_MODEL),
        'mla_q_norm_g': gain(ks[12], (N_ODD, MLA_Q_RANK)),
        'mla_kv_norm_g': gain(ks[13], (N_ODD, MLA_KV_RANK)),
        'mla_w_uq': dense(ks[14], (N_ODD, MLA_Q_RANK, N_HEADS_C * (MLA_NOPE_DIM + MLA_ROPE_DIM)), MLA_Q_RANK),
        'mla_w_ukv': dense(ks[15], (N_ODD, MLA_KV_RANK, N_HEADS_C * (MLA_NOPE_DIM + MLA_V_DIM)), MLA_KV_RANK),
        'cd_w_out': dense(ks[16], (N_ODD, CD_OUT, D_MODEL), CD_OUT),
        'ffn_w_up': dense(ks[17], (DEPTH, D_MODEL, 2 * D_FF), D_MODEL),
        'ffn_conv_w': dense(ks[18], (DEPTH, CONV_WIDTH, 2 * D_FF), CONV_WIDTH),
        'ffn_conv_b': 0.02 * jax.random.normal(ks[19], (DEPTH, 2 * D_FF), f32),
        'ffn_w_down': dense(ks[20], (DEPTH, D_FF, D_MODEL), D_FF),
    }

def first_block(x, c, rel_bias, ada_w, ada_b, mix_pre_g, mix_post_g, ffn_pre_g, ffn_post_g,
              ab_w_in, ab_w_out, cd_w_in, mla_q_norm_g, mla_kv_norm_g, mla_w_uq, mla_w_ukv, cd_w_out,
              ffn_w_up, ffn_conv_w, ffn_conv_b, ffn_w_down):
    s = x.shape[1]
    cos, sin = rope_tables(s)
    cond = jax.nn.silu(c)
    for layer in range(DEPTH):
        mod = cond @ ada_w[layer] + ada_b[layer]
        shift_m, scale_m, gate_m, shift_f, scale_f, gate_f = [m[:, None, :] for m in jnp.split(mod, 6, axis=-1)]
        h = rmsnorm(x, mix_pre_g[layer]) * (1.0 + scale_m) + shift_m
        i = layer // 2
        if layer % 2 == 0:
            y = even_mixer(h, ab_w_in[i], ab_w_out[i], rel_bias)
        else:
            y = odd_mixer(h, cd_w_in[i], mla_q_norm_g[i], mla_kv_norm_g[i], mla_w_uq[i], mla_w_ukv[i],
                          cd_w_out[i], cos, sin)
        x = x + gate_m * rmsnorm(y, mix_post_g[layer])
        h = rmsnorm(x, ffn_pre_g[layer]) * (1.0 + scale_f) + shift_f
        y = conv_ffn(h, ffn_w_up[layer], ffn_conv_w[layer], ffn_conv_b[layer], ffn_w_down[layer])
        x = x + gate_f * rmsnorm(y, ffn_post_g[layer])
    return x


N_META = 16
EPS = 1e-6
A_HEADS = 4
A_HEAD_DIM = 64
A_WIDTH = A_HEADS * A_HEAD_DIM
A_DECAY_RANK = 64
A_ICLR_RANK = 64
A_GATE_RANK = 128
A_GN_EPS = 64e-5
A_DECAY_SCALE = 0.6065306597126334
A_COLS = (A_WIDTH, A_WIDTH, A_WIDTH, A_DECAY_RANK, A_DECAY_RANK, A_ICLR_RANK, A_ICLR_RANK, A_GATE_RANK)
A_TOTAL = 3 * A_WIDTH + 2 * A_DECAY_RANK + 2 * A_ICLR_RANK + A_GATE_RANK
B_HEADS = 4
B_QK_DIM = 64
B_V_DIM = 2 * B_QK_DIM
B_WIDTH = B_HEADS * B_V_DIM
B_COLS = (B_HEADS * 2 * B_QK_DIM, B_HEADS * 2 * B_QK_DIM, B_WIDTH)
B_TOTAL = 2 * B_HEADS * 2 * B_QK_DIM + B_WIDTH
C_HEADS = 4
C_DK = 32
C_DV = 64
C_WIDTH = C_HEADS * C_DV
C_GATE_RANK = 16
C_GATE_TEMP = 16.0
C_CHUNK = 64
C_COLS = (C_HEADS * C_DK, C_HEADS * C_DK, C_WIDTH, C_WIDTH, C_GATE_RANK, C_GATE_RANK)
C_TOTAL = 2 * C_HEADS * C_DK + 2 * C_WIDTH + 2 * C_GATE_RANK
IN_COLS = A_TOTAL + B_TOTAL + C_TOTAL
MIX_WIDTH = A_WIDTH + B_WIDTH + C_WIDTH
N_EXPERTS = 16
EC_FACTOR = 2
EXPERT_FF = 1408


def _split(x, sizes):
    idx = np.cumsum(sizes)[:-1].tolist()
    return jnp.split(x, idx, axis=-1)

def rms_norm(x, g, eps=EPS):
    xf = x.astype(jnp.float32)
    y = xf * lax.rsqrt(jnp.mean(xf * xf, axis=-1, keepdims=True) + eps)
    return (y * g.astype(jnp.float32)).astype(x.dtype)

def rotary(x, pos):
    half = x.shape[-1] // 2
    inv = ROPE_THETA ** (-jnp.arange(half, dtype=jnp.float32) / half)
    ang = pos[:, None] * inv[None, :]
    cos, sin = jnp.cos(ang), jnp.sin(ang)
    xf = x.astype(jnp.float32)
    x1, x2 = xf[..., :half], xf[..., half:]
    return jnp.concatenate([x1 * cos - x2 * sin, x2 * cos + x1 * sin], axis=-1).astype(x.dtype)

def centred_shift(p, mu):
    prev = jnp.pad(p, ((0, 0), (1, 0), (0, 0)))[:, :-1]
    nxt = jnp.pad(p, ((0, 0), (0, 1), (0, 0)))[:, 1:]
    return p + mu[0] * (prev - p) + mu[1] * (nxt - p)

def rwkv7_group(p, shift_mu, w0, w_up, a0, a_up, g_up, k_k, k_a, r_k, gn_g, gn_b):
    B, L, _ = p.shape
    f32 = jnp.float32
    p = centred_shift(p, shift_mu)
    r, k, v, wd_f, wd_b, ad_f, ad_b, gd = _split(p, A_COLS)
    heads = lambda t: t.reshape(t.shape[:-1] + (A_HEADS, A_HEAD_DIM))
    wd = jnp.stack([wd_f, wd_b])
    ad = jnp.stack([ad_f, ad_b])
    z_w = w0[:, None, None] + jnp.einsum("dblr,drc->dblc", jnp.tanh(wd), w_up)
    decay = jnp.exp(-A_DECAY_SCALE * jax.nn.sigmoid(z_w.astype(f32)))
    iclr = jax.nn.sigmoid((a0[:, None, None] + jnp.einsum("dblr,drc->dblc", ad, a_up)).astype(f32))
    gate = jnp.einsum("blr,rc->blc", jax.nn.sigmoid(gd), g_up)
    kk = heads((k * k_k).astype(f32))
    kk = kk / jnp.maximum(jnp.sqrt(jnp.sum(kk * kk, axis=-1, keepdims=True)), 1e-12)
    k_dir = heads(k.astype(f32)[None] * (1.0 + (iclr - 1.0) * k_a.astype(f32)))
    r_h, v_h = heads(r.astype(f32)), heads(v.astype(f32))
    both = lambda t: jnp.broadcast_to(t[None], (2,) + t.shape)

    def to_scan(t):
        t = jnp.stack([t[0], t[1][:, ::-1]])
        return jnp.moveaxis(t, 2, 0)

    xs = tuple(to_scan(t) for t in (both(r_h), heads(decay), k_dir, both(v_h), both(kk), both(kk) * heads(iclr)))

    def step(S, inp):
        r_t, w_t, k_t, v_t, kk_t, ka_t = inp
        sa = jnp.einsum("dbhvk,dbhk->dbhv", S, kk_t)
        S = S * w_t[..., None, :] - sa[..., :, None] * ka_t[..., None, :] + v_t[..., :, None] * k_t[..., None, :]
        return S, jnp.einsum("dbhvk,dbhk->dbhv", S, r_t)

    S0 = jnp.zeros((2, B, A_HEADS, A_HEAD_DIM, A_HEAD_DIM), f32)
    _, y = lax.scan(step, S0, xs)
    y = jnp.moveaxis(y, 0, 2)
    o = y[0] + y[1][:, ::-1]
    mu = jnp.mean(o, axis=-1, keepdims=True)
    var = jnp.mean(jnp.square(o - mu), axis=-1, keepdims=True)
    o = ((o - mu) * lax.rsqrt(var + A_GN_EPS)).reshape(B, L, A_WIDTH) * gn_g.astype(f32) + gn_b.astype(f32)
    bonus = jnp.sum(r_h[None] * k_dir * heads(r_k.astype(f32)), axis=-1, keepdims=True) * v_h[None]
    o = o + jnp.sum(bonus, axis=0).reshape(B, L, A_WIDTH)
    return (o * gate.astype(f32)).astype(p.dtype)

def diff_attention_group(p, pos, lam_p, subln_g, lam_init):
    B, L, _ = p.shape
    f32 = jnp.float32
    q, k, v = _split(p, B_COLS)
    q = rotary(q.reshape(B, L, B_HEADS, 2, B_QK_DIM).transpose(0, 2, 3, 1, 4), pos) * (B_QK_DIM ** -0.5)
    k = rotary(k.reshape(B, L, B_HEADS, 2, B_QK_DIM).transpose(0, 2, 3, 1, 4), pos)
    v = v.reshape(B, L, B_HEADS, B_V_DIM).transpose(0, 2, 1, 3)
    lam_p = lam_p.astype(f32)
    lam = jnp.exp(jnp.sum(lam_p[0] * lam_p[1])) - jnp.exp(jnp.sum(lam_p[2] * lam_p[3])) + lam_init

    def attend(qb):
        s = jnp.einsum("bhcqd,bhckd->bhcqk", qb, k).astype(f32)
        pr = jax.nn.softmax(s, axis=-1)
        w = pr[:, :, 0] - lam * pr[:, :, 1]
        return jnp.einsum("bhqk,bhkv->bhqv", w.astype(v.dtype), v)

    o_meta = attend(q[:, :, :, :N_META])
    n_blk = (L - N_META) // Q_BLOCK
    q_real = jnp.moveaxis(q[:, :, :, N_META:].reshape(B, B_HEADS, 2, n_blk, Q_BLOCK, B_QK_DIM), 3, 0)
    o_real = lax.map(attend, q_real)
    o_real = jnp.moveaxis(o_real, 0, 2).reshape(B, B_HEADS, n_blk * Q_BLOCK, B_V_DIM)
    o = jnp.concatenate([o_meta, o_real], axis=2)
    o = rms_norm(o, subln_g) * (1.0 - lam_init)
    return o.transpose(0, 2, 1, 3).reshape(B, L, B_WIDTH).astype(p.dtype)

def gla_chunked(q, k, v, log_a):
    B, H, T, dk = q.shape
    dv = v.shape[-1]
    n = T // C_CHUNK
    f32 = jnp.float32
    ch = lambda t: t.astype(f32).reshape(B, H, n, C_CHUNK, t.shape[-1])
    q, k, v, g = ch(q), ch(k), ch(v), ch(log_a)
    b = jnp.cumsum(g, axis=3)
    b_last = b[:, :, :, -1:, :]
    q_dec = q * jnp.exp(b)
    k_inv = k * jnp.exp(-b)
    k_end = k * jnp.exp(b_last - b)
    mask = jnp.tril(jnp.ones((C_CHUNK, C_CHUNK), dtype=bool))
    att = jnp.where(mask, jnp.einsum("bhntd,bhnsd->bhnts", q_dec, k_inv), 0.0)
    o = jnp.einsum("bhnts,bhnsv->bhntv", att, v)
    kv = jnp.einsum("bhnsd,bhnsv->bhndv", k_end, v)
    dec = jnp.exp(b_last[:, :, :, 0])

    def step(S, inp):
        dec_n, kv_n = inp
        return dec_n[..., None] * S + kv_n, S

    _, S_prev = lax.scan(step, jnp.zeros((B, H, dk, dv), f32), (jnp.moveaxis(dec, 2, 0), jnp.moveaxis(kv, 2, 0)))
    S_prev = jnp.moveaxis(S_prev, 0, 2)
    o = o + jnp.einsum("bhntd,bhndv->bhntv", q_dec, S_prev)
    return o.reshape(B, H, T, dv)

def gla_group(p, gate_up, gate_b, norm_g):
    B, L, _ = p.shape
    q, k, v, g, ad_f, ad_b = _split(p, C_COLS)
    heads_t = lambda t, d: t.reshape(B, L, C_HEADS, d).transpose(0, 2, 1, 3)
    q = heads_t(q, C_DK) * (C_DK ** -0.5)
    k = heads_t(k, C_DK)
    v = heads_t(v, C_DV)
    ad = jnp.stack([ad_f, ad_b])
    z = jnp.einsum("dblr,drc->dblc", ad, gate_up) + gate_b[:, None, None]
    log_a = jax.nn.log_sigmoid(z.astype(jnp.float32)) / C_GATE_TEMP
    la_f, la_b = heads_t(log_a[0], C_DK), heads_t(log_a[1], C_DK)
    pad = C_CHUNK - N_META
    padt = lambda t: jnp.pad(t, ((0, 0), (0, 0), (pad, 0), (0, 0)))
    flip = lambda t: t[:, :, ::-1]
    qp, kp, vp = padt(q), padt(k), padt(v)
    o_f = gla_chunked(qp, kp, vp, padt(la_f))
    o_b = flip(gla_chunked(flip(qp), flip(kp), flip(vp), flip(padt(la_b))))
    o = (o_f + o_b)[:, :, pad:]
    o = rms_norm(o.transpose(0, 2, 1, 3), norm_g).reshape(B, L, C_WIDTH)
    return (o * jax.nn.silu(g.astype(jnp.float32))).astype(p.dtype)

def expert_choice_ffn(u, router, w1, w3, w2):
    B, L, D = u.shape
    cap = EC_FACTOR * L // N_EXPERTS
    aff = jax.nn.softmax(jnp.einsum("bld,de->ble", u, router).astype(jnp.float32), axis=-1)
    gates, idx = lax.top_k(jnp.swapaxes(aff, 1, 2), cap)
    xs = jax.vmap(lambda ub, ib: ub[ib])(u, idx)
    hid = jax.nn.silu(jnp.einsum("becd,edf->becf", xs, w1)) * jnp.einsum("becd,edf->becf", xs, w3)
    ys = jnp.einsum("becf,efd->becd", hid, w2) * gates[..., None].astype(u.dtype)
    return jax.vmap(lambda yb, ib: jnp.zeros((L, D), yb.dtype).at[ib].add(yb))(ys, idx)

def second_inputs(seed: int = 0) -> dict:
    key = jax.random.key(seed)
    ks = iter(jax.random.split(key, 32))
    nrm = lambda shape, scale: jax.random.normal(next(ks), shape, jnp.float32) * scale
    gain = lambda shape: 1.0 + nrm(shape, 0.02)
    D = D_MODEL
    return {
        "x": nrm((BATCH, SEQ, D), 1.0),
        "meta": nrm((N_META, D), 1.0),
        "norm1_g": gain((DEPTH, D)),
        "w_in": nrm((DEPTH, D, IN_COLS), D ** -0.5),
        "rw_shift": jax.random.uniform(next(ks), (DEPTH, 2, A_TOTAL), jnp.float32, 0.0, 0.5),
        "rw_w0": nrm((DEPTH, 2, A_WIDTH), 1.0),
        "rw_w_up": nrm((DEPTH, 2, A_DECAY_RANK, A_WIDTH), A_DECAY_RANK ** -0.5),
        "rw_a0": nrm((DEPTH, 2, A_WIDTH), 0.5),
        "rw_a_up": nrm((DEPTH, 2, A_ICLR_RANK, A_WIDTH), A_ICLR_RANK ** -0.5),
        "rw_g_up": nrm((DEPTH, A_GATE_RANK, A_WIDTH), A_GATE_RANK ** -0.5),
        "rw_k_k": 0.85 + nrm((DEPTH, A_WIDTH), 0.05),
        "rw_k_a": 1.0 + nrm((DEPTH, A_WIDTH), 0.05),
        "rw_r_k": nrm((DEPTH, A_WIDTH), 0.1),
        "rw_gn_g": gain((DEPTH, A_WIDTH)),
        "rw_gn_b": nrm((DEPTH, A_WIDTH), 0.02),
        "df_lam": nrm((DEPTH, 4, B_QK_DIM), 0.1),
        "df_subln_g": gain((DEPTH, B_V_DIM)),
        "gl_gate_up": nrm((DEPTH, 2, C_GATE_RANK, C_HEADS * C_DK), C_GATE_RANK ** -0.5),
        "gl_gate_b": nrm((DEPTH, 2, C_HEADS * C_DK), 0.5),
        "gl_norm_g": gain((DEPTH, C_DV)),
        "w_out": nrm((DEPTH, MIX_WIDTH, D), MIX_WIDTH ** -0.5),
        "norm2_g": gain((DEPTH, D)),
        "router": nrm((DEPTH, D, N_EXPERTS), D ** -0.5),
        "e_w1": nrm((DEPTH, N_EXPERTS, D, EXPERT_FF), D ** -0.5),
        "e_w3": nrm((DEPTH, N_EXPERTS, D, EXPERT_FF), D ** -0.5),
        "e_w2": nrm((DEPTH, N_EXPERTS, EXPERT_FF, D), EXPERT_FF ** -0.5),
        "final_g": gain((D,)),
    }

def second_block(x, meta, norm1_g, w_in, rw_shift, rw_w0, rw_w_up, rw_a0, rw_a_up, rw_g_up, rw_k_k, rw_k_a,
              rw_r_k, rw_gn_g, rw_gn_b, df_lam, df_subln_g, gl_gate_up, gl_gate_b, gl_norm_g, w_out,
              norm2_g, router, e_w1, e_w3, e_w2, final_g):
    B = x.shape[0]
    h = jnp.concatenate([jnp.broadcast_to(meta[None].astype(x.dtype), (B, N_META, D_MODEL)), x], axis=1)
    L = h.shape[1]
    pos = jnp.arange(L, dtype=jnp.float32)
    for l in range(DEPTH):
        lam_init = 0.8 - 0.6 * math.exp(-0.3 * l)
        u = rms_norm(h, norm1_g[l])
        p = jnp.einsum("bld,dp->blp", u, w_in[l])
        p_a, p_b, p_c = _split(p, (A_TOTAL, B_TOTAL, C_TOTAL))
        y_a = rwkv7_group(p_a, rw_shift[l], rw_w0[l], rw_w_up[l], rw_a0[l], rw_a_up[l], rw_g_up[l],
                          rw_k_k[l], rw_k_a[l], rw_r_k[l], rw_gn_g[l], rw_gn_b[l])
        y_b = diff_attention_group(p_b, pos, df_lam[l], df_subln_g[l], lam_init)
        y_c = gla_group(p_c, gl_gate_up[l], gl_gate_b[l], gl_norm_g[l])
        mix = jnp.concatenate([y_a, y_b, y_c], axis=-1).astype(h.dtype)
        h = h + jnp.einsum("blc,cd->bld", mix, w_out[l])
        h = h + expert_choice_ffn(rms_norm(h, norm2_g[l]), router[l], e_w1[l], e_w3[l], e_w2[l])
    return rms_norm(h, final_g)[:, N_META:]


def setup_inputs(seed=0):
    out = dict(first_inputs(seed))
    for name, value in second_inputs(seed + 1).items():
        if name != "x":
            out[name + "_2"] = value
    return out


def reference(
    x, c, rel_bias, ada_w, ada_b, mix_pre_g, mix_post_g, ffn_pre_g, ffn_post_g, ab_w_in,
    ab_w_out, cd_w_in, mla_q_norm_g, mla_kv_norm_g, mla_w_uq, mla_w_ukv, cd_w_out, ffn_w_up,
    ffn_conv_w, ffn_conv_b, ffn_w_down, meta_2, norm1_g_2, w_in_2, rw_shift_2, rw_w0_2,
    rw_w_up_2, rw_a0_2, rw_a_up_2, rw_g_up_2, rw_k_k_2, rw_k_a_2, rw_r_k_2, rw_gn_g_2,
    rw_gn_b_2, df_lam_2, df_subln_g_2, gl_gate_up_2, gl_gate_b_2, gl_norm_g_2, w_out_2,
    norm2_g_2, router_2, e_w1_2, e_w3_2, e_w2_2, final_g_2,
):
    x = first_block(
        x, c, rel_bias, ada_w, ada_b, mix_pre_g, mix_post_g, ffn_pre_g, ffn_post_g, ab_w_in,
        ab_w_out, cd_w_in, mla_q_norm_g, mla_kv_norm_g, mla_w_uq, mla_w_ukv, cd_w_out, ffn_w_up,
        ffn_conv_w, ffn_conv_b, ffn_w_down,
    )
    return second_block(
        x, meta_2, norm1_g_2, w_in_2, rw_shift_2, rw_w0_2, rw_w_up_2, rw_a0_2, rw_a_up_2,
        rw_g_up_2, rw_k_k_2, rw_k_a_2, rw_r_k_2, rw_gn_g_2, rw_gn_b_2, df_lam_2, df_subln_g_2,
        gl_gate_up_2, gl_gate_b_2, gl_norm_g_2, w_out_2, norm2_g_2, router_2, e_w1_2, e_w3_2,
        e_w2_2, final_g_2,
    )


_drawn_inputs = setup_inputs


def setup_inputs(seed=0):
    import zlib

    import numpy as np

    out = dict(_drawn_inputs(seed))
    spreads = {}
    factors = {'mla_q_norm_g': 8.0,
     'ffn_conv_b': 2.738,
     'rw_gn_g_2': 5.429,
     'rw_gn_b_2': 5.88,
     'gl_norm_g_2': 5.336,
     'norm2_g_2': 3.317,
     'final_g_2': 2.76}
    for name, (base, spread) in spreads.items():
        noise = np.random.default_rng([zlib.crc32(name.encode()), seed]).standard_normal(out[name].shape)
        drawn = base * np.exp(spread * noise) if base else spread * noise
        out[name] = jnp.asarray(drawn.astype(out[name].dtype))
    for name, factor in factors.items():
        out[name] = (out[name] * factor).astype(out[name].dtype)
    return out
```

```python
import concourse.bass as bass
from concourse import mybir
from contextlib import ExitStack
import math
import numpy as np

FP32 = mybir.dt.float32
ALU = mybir.AluOpType
ACT = mybir.ActivationFunctionType
AX = mybir.AxisListType

P = 128
D = 1024
KD = D // P
SEQ = 256
META = 16
L = SEQ + META
TILES = ((0, 128), (128, 128), (256, 16))
EPS = 1e-6
NEG = -1e30
DEPTH = 2
F1 = 2816
KF = F1 // P
HD = 64
BUCKETS = 32
SLOT = 4096
NSLOT = 5
RANK = 256
SPAN = 2 * SEQ - 1


class Count:

    def __init__(self, sem):
        self.sem, self.read = sem, {}

    def next(self, who="", n=1):
        self.read[who] = self.read.get(who, 0) + n
        return self.read[who]



def t5_bucket(dist):
    exact = BUCKETS // 2
    d = np.maximum(dist, 0)
    f = np.maximum(d, exact).astype(np.float32)
    large = exact + (np.log(f / np.float32(exact)) / np.float32(math.log(2048 / exact))
                     * np.float32(BUCKETS - exact)).astype(np.int32)
    return np.where(d < exact, d, np.minimum(large, BUCKETS - 1))


def shape_constants():
    c = {}
    i = np.arange(P)
    c["ident"] = np.eye(P)
    c["ones"] = np.ones((P, P))
    c["ones64"] = (i[:, None] // 64 == i[None, :] // 64).astype(float)
    pos = np.arange(SEQ, dtype=np.float32)
    inv = (1.0 / (np.float32(10000.0) ** (np.arange(0, 32, 2, dtype=np.float32) / np.float32(32)))).astype(np.float32)
    ang = pos[None, :] * inv[:, None]
    c["cos_mla"] = np.concatenate([np.ones((64, SEQ)), np.cos(ang), np.cos(ang)])
    c["sin_mla"] = np.concatenate([np.zeros((64, SEQ)), np.sin(ang), np.sin(ang)])
    rot = np.zeros((96, 96))
    for r in range(16):
        rot[80 + r, 64 + r] = -1.0
        rot[64 + r, 80 + r] = 1.0
    c["rot_mla"] = rot
    inv = (np.float32(10000.0) ** (-np.arange(32, dtype=np.float32) / np.float32(32))).astype(np.float32)
    ang = np.arange(L, dtype=np.float32)[None, :] * inv[:, None]
    c["cos_diff"] = np.tile(np.cos(ang), (4, 1))
    c["sin_diff"] = np.tile(np.sin(ang), (4, 1))
    rot = np.zeros((P, P))
    for g in (0, 64):
        for r in range(32):
            rot[g + 32 + r, g + r] = -1.0
            rot[g + r, g + 32 + r] = 1.0
    c["rot_diff"] = rot
    q, k = i[:, None], np.arange(SEQ)[None, :]
    c["causal"] = np.concatenate([np.where(k <= q + 128, 0.0, NEG), np.where(k <= q, 0.0, NEG)], axis=1)
    dist = SEQ - 1 - np.arange(SPAN)
    hot = (t5_bucket(dist)[None, :] == np.arange(BUCKETS)[:, None]) & (dist >= 0)
    times = np.zeros(SPAN)
    for window, dil in ((128, 1), (512, 4), (2048, 16)):
        times += (dist >= 0) & (dist <= window) & (dist % dil == 0)
    c["hot_moba"] = np.concatenate([hot, np.where(dist >= 0, 0.0, NEG)[None, :]])
    c["hot_dil"] = np.concatenate([hot, np.where(times > 0, np.log(np.maximum(times, 1)), NEG)[None, :]])
    q = np.arange(SEQ)[None, :]
    c["strict"] = np.concatenate([i[:, None] < q, i[:, None] + 128 < q], axis=1).astype(float)
    c["later"] = (i[:, None] >= i[None, :]).astype(float)
    c["before"] = (i[:, None] < i[None, :]).astype(float)
    c["slot_no"] = np.tile(np.arange(34)[None, :], (P, 1))
    same = i[:, None] // 16 == i[None, :] // 16
    s, t = i[:, None], i[None, :]
    c["lt_f"], c["le_f"] = (same & (s < t)).astype(float), (same & (s <= t)).astype(float)
    c["lt_b"], c["le_b"] = (same & (s > t)).astype(float), (same & (s >= t)).astype(float)
    c["le_fb"] = np.concatenate([c["le_f"], c["le_b"]], axis=1)
    c["chunk_of"] = (i[:, None] // 16 == np.arange(8)[None, :]).astype(float)
    t = np.arange(L)
    c["go_f"] = np.tile((t % 16 != 0).astype(float)[None, :], (P, 1))
    c["id64"] = (i[:, None] % 64 == np.arange(64)[None, :]).astype(float)
    c["go_b"] = np.tile((t % 16 != 15).astype(float)[None, :], (P, 1))
    return {k: np.asarray(v, np.float32) for k, v in c.items()}


def pack(parts):
    at, n = {}, 0
    for name, a in parts.items():
        at[name] = (n, a.shape[1], a.shape[0])
        n += a.shape[1]
    out = np.zeros((P, n), np.float32)
    for name, a in parts.items():
        out[:a.shape[0], at[name][0]:at[name][0] + a.shape[1]] = a
    return out, at


def vector_parts(w):
    def cols(a):
        a = np.asarray(a)
        a = a.reshape(-1, a.shape[-1])
        return a.reshape(a.shape[0] * (a.shape[1] // P), P).T
    parts = {"c": cols(w["c"]), "ada_b": cols(w["ada_b"])}
    for n in ("mix_pre_g", "mix_post_g", "ffn_pre_g", "ffn_post_g", "mla_q_norm_g", "mla_kv_norm_g",
              "ffn_conv_w", "ffn_conv_b", "norm1_g_2", "rw_shift_2", "rw_w0_2", "rw_a0_2", "rw_k_k_2",
              "rw_k_a_2", "rw_r_k_2", "rw_gn_g_2", "rw_gn_b_2", "df_subln_g_2", "gl_gate_b_2", "norm2_g_2",
              "final_g_2"):
        parts[n] = cols(w[n])
    g = np.asarray(w["gl_norm_g_2"])
    parts["gl_norm_g_2"] = np.concatenate([g, g], axis=1).T
    lam = np.asarray(w["df_lam_2"]).reshape(DEPTH * 4, HD).T
    parts["df_lam_2"] = lam
    table = np.asarray(w["rel_bias"]).T
    parts["rel_bias"] = table
    up = np.asarray(w["gl_gate_up_2"])
    gate = np.zeros((32, DEPTH * 2 * P), np.float32)
    for l in range(DEPTH):
        for d in range(2):
            gate[16 * d:16 * d + 16, (2 * l + d) * P:(2 * l + d + 1) * P] = up[l, d]
    parts["gl_gate_up_2"] = gate
    return parts


def build(nc, A, cat, vat, out, stop=None, dump=None):
    ctx = ExitStack()
    with ctx:
        def sb(name, shape):
            return ctx.enter_context(nc.sbuf_tensor(name, shape, FP32))

        def sem(name):
            return ctx.enter_context(nc.semaphore(name))

        def signal(name):
            return Count(sem(name))

        X = sb("residual", [P, KD, L])
        H = sb("normed", [P, KD, L])
        S = sb("scratch", [P, KD, L])
        ring = sb("weight_ring", [P, NSLOT, SLOT])
        ncst = A["consts"].shape[1]
        nvec = A["vectors"].shape[1]
        cst = sb("constants", [P, ncst])
        vec = sb("vectors", [P, nvec])
        mod = sb("modulation", [P, DEPTH, 6 * KD])
        gain = sb("gain", [P, 2, KD])
        cond = sb("cond", [P, KD])
        rstd = sb("rstd", [P, L])
        small = sb("small", [P, 64])
        AN = (nc.sbuf_bytes_remaining if not callable(nc.sbuf_bytes_remaining) else nc.sbuf_bytes_remaining()) // 4 - 64

        arena = sb("arena", [P, AN])
        banks = [ctx.enter_context(nc.psum_tensor(f"bank{i}", [P, 512], FP32)) for i in range(8)]
        scratch = nc.dram_tensor("bias_rows", (16, P, 512), FP32, kind="Internal").ap()

        def C(name, rows=None):
            a, n, r = cat[name]
            return cst[0:(rows or r), a:a + n]

        def V(name, j=0, n=1, rows=P):
            a = vat[name][0]
            return vec[0:rows, a + j:a + j + n]

        def view(at, *shape):
            n = int(np.prod(shape))
            assert at + n <= AN, (at, n, AN)
            v = arena[:, at:at + n]
            if len(shape) == 2:
                v = v.rearrange("p (a b) -> p a b", a=shape[0])
            if len(shape) == 3:
                v = v.rearrange("p (a b c) -> p a b c", a=shape[0], b=shape[1])
            return v

        loaded = signal("loaded")
        phase_end = sem("phase_end")
        slot_filled = [signal(f"slot{i}_filled") for i in range(NSLOT)]
        slot_used = signal("slot_used")
        vbank_filled, vbank_emptied = signal("vbank_filled"), signal("vbank_emptied")
        abank_filled, abank_emptied = signal("abank_filled"), signal("abank_emptied")
        squares_ready = signal("squares_ready")
        inv_ready = signal("inv_ready")
        rstd_ready = signal("rstd_ready")
        operand_ready = signal("operand_ready")
        aoperand_ready = signal("aoperand_ready")
        logits_ready = signal("logits_ready")
        exp_ready = signal("exp_ready")
        act_ready = signal("act_ready")
        dve_ready = signal("dve_ready")
        rows_ready = signal("rows_ready")
        rows_stored = signal("rows_stored")
        bias_loaded = signal("bias_loaded")
        stored = signal("stored")
        small_loaded = signal("small_loaded")
        pool_ready = signal("pool_ready")

        ends = {}

        class Stop(Exception):
            pass

        def end_phase(eng, name):
            ends[name] = ends.get(name, 0) + 1
            eng.drain().then_inc(phase_end, 1)
            eng.wait_ge(phase_end, 4 * ends[name])
            if ends[name] == stop:
                raise Stop

        plan = []

        def load_plan(W, c0, w, k0, nk):
            plan.append((W[k0 * P:(k0 + nk) * P, c0:c0 + w].rearrange("(k p) n -> p k n", p=P), nk, w))

        nslot = [0]
        slot_read = []

        def read_with_bank(which="v"):
            slot_read.append(((vbank_filled if which == "v" else abank_filled).sem, nfill[which]))

        def read_alone(mm):
            mm.then_inc(slot_used.sem, 1)
            slot_read.append((slot_used.sem, slot_used.next("pe")))


        def next_slot(pe, nk, w):
            i = nslot[0]
            nslot[0] += 1
            assert plan[i][1:] == (nk, w), (i, plan[i][1:], nk, w)
            pe.wait_ge(slot_filled[i % NSLOT].sem, 16 * (i // NSLOT + 1))
            return ring[:, i % NSLOT, 0:nk * w].rearrange("p (k n) -> p k n", k=nk)

        nfill = {"v": 0, "a": 0}

        def fill_bank(pe, which):
            i = nfill[which]
            nfill[which] += 1
            if i >= 4:
                pe.wait_ge((vbank_emptied if which == "v" else abank_emptied).sem, i - 3)
            return banks[(i % 4) + (4 if which == "a" else 0)]

        ntake = {"v": 0, "a": 0}

        def take_bank(eng, which):
            i = ntake[which]
            ntake[which] += 1
            eng.wait_ge((vbank_filled if which == "v" else abank_filled).sem, i + 1)
            return banks[(i % 4) + (4 if which == "a" else 0)]

        FV, EV = vbank_filled.sem, vbank_emptied.sem
        FA, EA = abank_filled.sem, abank_emptied.sem

        def norm_scalar(act, src, nk, T):
            act.activation(S[:, 0:nk, 0:T], src, ACT.Square).then_inc(squares_ready.sem, 1)
            act.wait_ge(inv_ready.sem, inv_ready.next())
            act.activation(rstd[:, 0:T], rstd[:, 0:T], ACT.Sqrt).then_inc(rstd_ready.sem, 1)

        def norm_tensor(pe, nk, T, ones=None):
            pe.wait_ge(squares_ready.sem, squares_ready.next())
            b = fill_bank(pe, "v")
            for k in range(nk):
                mm = pe.matmul(b[:, 0:T], ones if ones is not None else C("ones"), S[:, k, 0:T], start=(k == 0), stop=(k == nk - 1))
            mm.then_inc(FV, 1)

        def norm_vector(dve, width, T, eps=EPS):
            b = take_bank(dve, "v")
            dve.tensor_scalar(rstd[:, 0:T], b[:, 0:T], 1.0 / width, eps, ALU.mult, ALU.add).then_inc(EV, 1)
            dve.drain()
            dve.reciprocal(rstd[:, 0:T], rstd[:, 0:T]).then_inc(inv_ready.sem, 1)
            dve.wait_ge(rstd_ready.sem, rstd_ready.next())

        def groups(width):
            return [(g, min(512, width - g)) for g in range(0, width, 512)]

        def project_plan(W, width, nk, first=0):
            for g, w in groups(width):
                for k0 in range(0, nk, KD):
                    load_plan(W, first + g, w, k0, min(KD, nk - k0))

        def project_tensor(pe, width, nk, rhs, T):
            for g, w in groups(width):
                tiles = [(m, min(P, w - m)) for m in range(0, w, P)]
                b = [None] * len(tiles)
                for k0 in range(0, nk, KD):
                    n = min(KD, nk - k0)
                    W = next_slot(pe, n, w)
                    for i, (m, mw) in enumerate(tiles):
                        if k0 == 0:
                            b[i] = fill_bank(pe, "v")
                        for k in range(k0, k0 + n):
                            mm = pe.matmul(b[i][0:mw, 0:T], W[:, k - k0, m:m + mw], rhs(k),
                                           start=(k == 0), stop=(k == nk - 1))
                        if k0 + n == nk:
                            mm.then_inc(FV, 1)
                    if k0 + n == nk:
                        read_with_bank()
                    else:
                        read_alone(mm)

        def project_vector(dve, width, put):
            for m in range(-(-width // P)):
                b = take_bank(dve, "v")
                put(m, min(P, width - m * P), b).then_inc(EV, 1)

        XB = X[:, :, META:L]

        arow = view(0, DEPTH * 6 * D)

        def ada_plan():
            for l in range(DEPTH):
                project_plan(A["ada_w"][l], 6 * D, KD)

        def ada_tensor(pe):
            pe.wait_ge(aoperand_ready.sem, aoperand_ready.next())
            for l in range(DEPTH):
                for g, w in groups(6 * D):
                    W = next_slot(pe, KD, w)
                    b = fill_bank(pe, "v")
                    for k in range(KD):
                        mm = pe.matmul(b[0:1, 0:w], cond[:, k:k + 1], W[:, k, :], start=(k == 0), stop=(k == KD - 1))
                    mm.then_inc(FV, 1)
                    read_with_bank()
            pe.wait_ge(operand_ready.sem, operand_ready.next())
            b = fill_bank(pe, "v")
            for j in range(DEPTH * 6 * KD):
                mm = pe.matmul(b[:, j:j + 1], arow[0:1, j * P:(j + 1) * P], C("ones")[0:1, 0:1], start=True, stop=True)
            mm.then_inc(FV, 1)

        def ada_scalar(act):
            act.wait_ge(loaded.sem, 16 * 4)
            act.activation(cond[:, :], V("c", 0, KD), ACT.Silu).then_inc(aoperand_ready.sem, 1)

        def ada_vector(dve):
            dve.wait_ge(loaded.sem, 16 * 4)
            for j in range(DEPTH * 12):
                b = take_bank(dve, "v")
                cp = dve.tensor_copy(arow[0:1, j * 512:(j + 1) * 512], b[0:1, 0:512])
                cp.then_inc(EV, 1)
            dve.drain().then_inc(operand_ready.sem, 1)
            b = take_bank(dve, "v")
            dve.tensor_tensor(mod[:, :, :].rearrange("p l j -> p (l j)"), b[:, 0:DEPTH * 6 * KD],
                              V("ada_b", 0, DEPTH * 6 * KD), ALU.add).then_inc(EV, 1)

        def modulation(l, what):
            return mod[:, l, what * KD:(what + 1) * KD]

        def pre_norm_vector(dve, l, g, shift, scale):
            dve.scalar_tensor_tensor(out=gain[:, 0, :], in0=modulation(l, scale), scalar=1.0,
                                     in1=V(g, l * KD, KD), op0=ALU.add, op1=ALU.mult)
            norm_vector(dve, D, SEQ)
            for k in range(KD):
                dve.tensor_tensor(S[:, k, 0:SEQ], XB[:, k, :], rstd[:, 0:SEQ], ALU.mult)
            dve.drain()
            for k in range(KD):
                ins = dve.tensor_scalar(H[:, k, 0:SEQ], S[:, k, 0:SEQ], gain[:, 0, k:k + 1],
                                        modulation(l, shift)[:, k:k + 1], ALU.mult, ALU.add)
            ins.then_inc(operand_ready.sem, 1)

        def post_norm_vector(dve, l, g, gate):
            dve.drain()
            dve.tensor_tensor(gain[:, 0, :], modulation(l, gate), V(g, l * KD, KD), ALU.mult)
            dve.wait_ge(squares_ready.sem, squares_ready.next("dve"))
            norm_vector(dve, D, SEQ)
            for k in range(KD):
                dve.tensor_tensor(H[:, k, 0:SEQ], H[:, k, 0:SEQ], rstd[:, 0:SEQ], ALU.mult)
            dve.drain()
            for k in range(KD):
                dve.scalar_tensor_tensor(out=XB[:, k, :], in0=H[:, k, 0:SEQ], scalar=gain[:, 0, k:k + 1],
                                         in1=XB[:, k, :], op0=ALU.mult, op1=ALU.add)

        hrhs = lambda T: (lambda k: H[:, k, 0:T])

        def attend_tensor(pe, n, q, k, vtok, feed=None):
            Lg, PT = att_l, att_pt
            for i in range(n + 2):
                if i < n:
                    b = fill_bank(pe, "v")
                    for jj in range(2):
                        qt = q(i)[:, (1 - jj) * P:(2 - jj) * P]
                        mm = pe.matmul(b[:, jj * SEQ:(jj + 1) * SEQ], qt, k(i), start=True, stop=True)
                    mm.then_inc(FV, 1)
                if 1 <= i <= n:
                    h = i - 1
                    pe.wait_ge(operand_ready.sem, operand_ready.next())
                    b = fill_bank(pe, "a")
                    for kt in range(2):
                        for jj in range(2):
                            mm = pe.transpose(b[:, kt * SEQ + (1 - jj) * P:kt * SEQ + (2 - jj) * P],
                                              Lg[:, h % 2, jj * SEQ + kt * P:jj * SEQ + (kt + 1) * P], C("ident"))
                    mm.then_inc(FA, 1)
                if i >= 2:
                    h = i - 2
                    pe.wait_ge(aoperand_ready.sem, aoperand_ready.next())
                    b = fill_bank(pe, "v")
                    o = b[64 * (h % 2):64 * (h % 2) + 64, 0:SEQ]
                    pe.matmul(o, vtok(h, 0), PT[:, h % 2, 0:SEQ], start=True, stop=False)
                    pe.matmul(o, vtok(h, 1), PT[:, h % 2, SEQ:2 * SEQ], start=False, stop=True).then_inc(FV, 1)

        def attend_vector(dve, n, scale, bias, put):
            Lg = att_l
            for i in range(n + 2):
                if i < n:
                    b = take_bank(dve, "v")
                    mx = small[:, 8 * (i % 2):8 * (i % 2) + 2]
                    dve.scalar_tensor_tensor(out=Lg[:, i % 2, :], in0=b[:, :], scalar=scale, in1=bias(i),
                                             op0=ALU.mult, op1=ALU.add).then_inc(EV, 1)
                    dve.drain()
                    dve.tensor_reduce(mx, Lg[:, i % 2, :].rearrange("p (j k) -> p j k", j=2), AX.X, ALU.max)
                    dve.drain()
                    dve.tensor_scalar(mx, mx, -1.0, None, ALU.mult).then_inc(logits_ready.sem, 1)
                if 1 <= i <= n:
                    h = i - 1
                    sm = small[:, 8 * (h % 2) + 2:8 * (h % 2) + 4]
                    rc = small[:, 8 * (h % 2) + 4:8 * (h % 2) + 6]
                    dve.wait_ge(exp_ready.sem, exp_ready.next())
                    dve.reciprocal(rc, sm)
                    dve.drain()
                    for jj in range(2):
                        ins = dve.tensor_scalar(Lg[:, h % 2, jj * SEQ:(jj + 1) * SEQ],
                                                Lg[:, h % 2, jj * SEQ:(jj + 1) * SEQ], rc[:, jj:jj + 1], None, ALU.mult)
                    ins.then_inc(operand_ready.sem, 1)
                if i >= 2:
                    h = i - 2
                    b = take_bank(dve, "v")
                    r = slice(64 * (h % 2), 64 * (h % 2) + 64)
                    dve.tensor_copy(put(h), b[r, 0:SEQ]).then_inc(EV, 1)

        def attend_scalar(act, n):
            Lg, PT = att_l, att_pt
            for i in range(n + 1):
                if i < n:
                    act.wait_ge(logits_ready.sem, logits_ready.next())
                    for jj in range(2):
                        ins = act.activation(Lg[:, i % 2, jj * SEQ:(jj + 1) * SEQ], Lg[:, i % 2, jj * SEQ:(jj + 1) * SEQ],
                                             ACT.Exp, bias=small[:, 8 * (i % 2) + jj:8 * (i % 2) + jj + 1],
                                             accum_out=small[:, 8 * (i % 2) + 2 + jj:8 * (i % 2) + 3 + jj])
                    ins.then_inc(exp_ready.sem, 1)
                if i >= 1:
                    h = i - 1
                    b = take_bank(act, "a")
                    act.activation(PT[:, h % 2, :], b[:, :], ACT.Copy).then_inc(EA, 1)
                    act.drain().then_inc(aoperand_ready.sem, 1)

        def turn_values_tensor(pe, n):
            pe.wait_ge(operand_ready.sem, operand_ready.next())
            for m in range(n):
                b = fill_bank(pe, "a")
                for t in range(2):
                    mm = pe.transpose(b[:, t * P:(t + 1) * P], S[:, m, t * P:(t + 1) * P], C("ident"))
                mm.then_inc(FA, 1)

        def turn_values_scalar(act, n):
            for m in range(n):
                b = take_bank(act, "a")
                act.activation(att_v[:, :, m * P:(m + 1) * P], b[:, 0:2 * P].rearrange("p (t f) -> p t f", t=2),
                               ACT.Copy).then_inc(EA, 1)
            act.drain().then_inc(aoperand_ready.sem, 1)

        att_q = view(0, 8, SEQ)
        att_k = view(8 * SEQ, 8, SEQ)
        att_v = view(16 * SEQ, 2, D)
        att_l = view(24 * SEQ, 2, 2 * SEQ)
        att_pt = view(28 * SEQ, 2, 2 * SEQ)
        att_b = view(32 * SEQ, 16, 2 * SEQ)
        table = sb("bias_table", [BUCKETS + 1, 16])
        row_at = S[:, :, :].rearrange("p a b -> p (a b)")

        def bias_vector(dve):
            dve.memset(table[:, :], 1.0)
            dve.drain()
            dve.tensor_copy(table[0:BUCKETS, :], V("rel_bias", 0, 16, rows=BUCKETS)).then_inc(operand_ready.sem, 1)
            for h in range(16):
                b = take_bank(dve, "v")
                if h >= 4:
                    dve.wait_ge(rows_stored.sem, 16 * (h - 3))
                dve.tensor_copy(row_at[:, (h % 4) * 512:(h % 4) * 512 + SPAN], b[:, 0:SPAN]).then_inc(EV, 1)
                dve.drain().then_inc(rows_ready.sem, 1)

        def bias_tensor(pe):
            pe.wait_ge(operand_ready.sem, operand_ready.next())
            for h in range(16):
                b = fill_bank(pe, "v")
                pe.matmul(b[:, 0:SPAN], table[:, h:h + 1].to_broadcast([BUCKETS + 1, P]),
                          C("hot_moba" if h < 8 else "hot_dil"), start=True, stop=True).then_inc(FV, 1)

        def bias_pool(pool):
            for h in range(16):
                pool.wait_ge(rows_ready.sem, rows_ready.next())
                pool.dma_start(scratch[h, :, 0:SPAN], row_at[:, (h % 4) * 512:(h % 4) * 512 + SPAN])\
                    .then_inc(rows_stored.sem, 16)
                pool.wait_ge(rows_stored.sem, 16 * (h + 1))
                skew = bass.AP(tensor=scratch.tensor, offset=scratch.offset + h * P * 512 + P - 1,
                               ap=[[511, P], [P, 2], [1, SEQ]])
                pool.dma_start(att_b[:, h, :].rearrange("p (j k) -> p j k", j=2), skew).then_inc(bias_loaded.sem, 16)
            pool.wait_ge(bias_loaded.sem, 16 * 16)

        def even_put(dve):
            def put(m, rows, b):
                part, i = m // 4, m % 4
                half, kind = part // 3, part % 3
                if kind == 2:
                    return dve.tensor_copy(S[:, half * 4 + i, 0:SEQ], b[:, 0:SEQ])
                return dve.tensor_copy((att_q, att_k)[kind][:, half * 4 + i, :], b[:, 0:SEQ])
            return put

        def head_rows(buf):
            return lambda h: buf[64 * (h % 2):64 * (h % 2) + 64, h // 2, :]

        hid = view(0, KF, SEQ)
        conv = view(KF * SEQ, 4, SEQ)

        def ffn_plan(l):
            for g, w in groups(F1):
                load_plan(A["ffn_w_up"][l], g, w, 0, KD)
                load_plan(A["ffn_w_up"][l], F1 + g, w, 0, KD)
            project_plan(A["ffn_w_down"][l], D, KF)

        def ffn_tensor(pe):
            pe.wait_ge(operand_ready.sem, operand_ready.next())
            for g, w in groups(F1):
                W = [next_slot(pe, KD, w), next_slot(pe, KD, w)]
                for m in range(0, w, P):
                    for part in range(2):
                        b = fill_bank(pe, "v")
                        for k in range(KD):
                            mm = pe.matmul(b[:, 0:SEQ], W[part][:, k, m:m + P], H[:, k, 0:SEQ],
                                           start=(k == 0), stop=(k == KD - 1))
                        mm.then_inc(FV, 1)
                read_with_bank()
                read_with_bank()
            pe.wait_ge(operand_ready.sem, operand_ready.next())
            project_tensor(pe, D, KF, lambda k: hid[:, k, :], SEQ)

        def ffn_scalar(act, l):
            for i in range(KF):
                for part in range(2):
                    m = part * KF + i
                    n = ffn_taken[0]
                    ffn_taken[0] += 1
                    act.wait_ge(vbank_filled.sem, ntake_ffn(n))
                    if i >= 2:
                        act.wait_ge(dve_ready.sem, dve_ready_at(i, l))
                    act.activation(conv[:, 2 * (i % 2) + part, :], banks[(ntake_ffn(n) - 1) % 4][:, 0:SEQ], ACT.Identity,
                                   bias=V("ffn_conv_b", l * 44 + m),
                                   scale=V("ffn_conv_w", (l * 3 + 2) * 44 + m)).then_inc(act_ready.sem, 1)
                if i >= 1:
                    gelu_scalar(act, i - 1, l)
            gelu_scalar(act, KF - 1, l)

        def gelu_scalar(act, i, l):
            act.wait_ge(logits_ready.sem, logits_ready.next())
            act.activation(conv[:, 2 * (i % 2), :], conv[:, 2 * (i % 2), :], ACT.Gelu_apprx_tanh)\
                .then_inc(exp_ready.sem, 1)

        ffn_taken = [0]
        ffn_first = {}

        def ntake_ffn(n):
            l, j = divmod(n, 2 * KF)
            return ffn_first[l] + j + 1

        def dve_ready_at(i, l):
            return l * KF + i - 1

        def ffn_vector(dve, l):
            def product(i):
                dve.wait_ge(exp_ready.sem, exp_ready.next())
                dve.tensor_tensor(hid[:, i, :], conv[:, 2 * (i % 2), :], conv[:, 2 * (i % 2) + 1, :], ALU.mult)\
                    .then_inc(dve_ready.sem, 1)
            for i in range(KF):
                for part in range(2):
                    m = part * KF + i
                    b = take_bank(dve, "v")
                    c = conv[:, 2 * (i % 2) + part, :]
                    dve.wait_ge(act_ready.sem, act_ready.next())
                    dve.scalar_tensor_tensor(out=c[:, 1:SEQ], in0=b[:, 0:SEQ - 1], scalar=V("ffn_conv_w", (l * 3 + 1) * 44 + m),
                                             in1=c[:, 1:SEQ], op0=ALU.mult, op1=ALU.add)
                    dve.drain()
                    dve.scalar_tensor_tensor(out=c[:, 2:SEQ], in0=b[:, 0:SEQ - 2], scalar=V("ffn_conv_w", l * 3 * 44 + m),
                                             in1=c[:, 2:SEQ], op0=ALU.mult, op1=ALU.add).then_inc(EV, 1)
                dve.drain().then_inc(logits_ready.sem, 1)
                if i >= 1:
                    product(i - 1)
            product(KF - 1)
            dve.drain().then_inc(operand_ready.sem, 1)
            project_vector(dve, D, lambda m, rows, b: dve.tensor_copy(H[:, m, 0:SEQ], b[:, 0:SEQ]))
            dve.drain().then_inc(dve_done_y.sem, 1)

        dve_done_y = signal("y_ready")

        NR = 96
        cq = view(0, 4, SEQ)
        krope = view(4 * SEQ, SEQ)
        qfull = view(5 * SEQ, 8, SEQ)
        kfull = view(13 * SEQ, 8, SEQ)
        stick_q = view(64 * SEQ, 4, SEQ)
        odd_v = view(32 * SEQ, 2, D)
        stick_k = view(40 * SEQ, 4, SEQ)
        odd_o = view(44 * SEQ, 8, SEQ)
        stick_z = view(52 * SEQ, 3, 2 * SEQ)
        stick_t = view(58 * SEQ, 2, 2 * SEQ)
        rope_t = view(62 * SEQ, 2, SEQ)

        def odd_plan():
            W = A["cd_w_in"][0]
            load_plan(W, 0, 512, 0, KD)
            load_plan(W, 512, 32, 0, KD)
            for g in range(2):
                load_plan(A["mla_w_uq"][0], g * 4 * NR, 4 * NR, 0, 2)
            for g in range(2):
                load_plan(A["mla_w_ukv"][0], g * 512, 512, 0, 2)
            project_plan(W, 1536, KD, 544)
            project_plan(A["cd_w_out"][0], D, KD)

        def odd_tensor(pe):
            pe.wait_ge(operand_ready.sem, operand_ready.next())
            project_tensor(pe, 512, KD, hrhs(SEQ), SEQ)
            W = next_slot(pe, KD, 32)
            b = fill_bank(pe, "v")
            for k in range(KD):
                mm = pe.matmul(b[64:96, 0:SEQ], W[:, k, :], H[:, k, 0:SEQ], start=(k == 0), stop=(k == KD - 1))
            mm.then_inc(FV, 1)
            read_with_bank()
            pe.wait_ge(operand_ready.sem, operand_ready.next())
            b = fill_bank(pe, "v")
            pe.matmul(b[64:96, 0:SEQ], C("rot_mla")[64:96, 64:96], krope[64:96, :], start=True, stop=True).then_inc(FV, 1)
            norm_tensor(pe, 2, SEQ)
            norm_tensor(pe, 2, SEQ)
            pe.wait_ge(operand_ready.sem, operand_ready.next())
            for g in range(2):
                W = next_slot(pe, 2, 4 * NR)
                for h in range(4):
                    b = fill_bank(pe, "v")
                    for k in range(2):
                        mm = pe.matmul(b[0:NR, 0:SEQ], W[:, k, h * NR:(h + 1) * NR], cq[:, k, :], start=(k == 0), stop=(k == 1))
                    mm.then_inc(FV, 1)
                read_with_bank()
            pe.wait_ge(operand_ready.sem, operand_ready.next())
            for h in range(8):
                b = fill_bank(pe, "v")
                pe.matmul(b[0:NR, 0:SEQ], C("rot_mla"), qfull[0:NR, h, :], start=True, stop=True).then_inc(FV, 1)
            for g in range(2):
                W = next_slot(pe, 2, 512)
                W4 = W.rearrange("p k (h f) -> p k h f", h=4)
                for h in range(4):
                    b = fill_bank(pe, "v")
                    for k in range(2):
                        mm = pe.matmul(b[0:HD, 0:SEQ], W[:, k, h * P:h * P + HD], cq[:, 2 + k, :], start=(k == 0), stop=(k == 1))
                    mm.then_inc(FV, 1)
                for t in range(2):
                    b = fill_bank(pe, "v")
                    for k in range(2):
                        mm = pe.matmul(b[:, 0:SEQ].rearrange("p (h f) -> p h f", h=4), cq[:, 2 + k, t * P:(t + 1) * P],
                                       W4[:, k, :, HD:P], start=(k == 0), stop=(k == 1))
                    mm.then_inc(FV, 1)
                read_with_bank()
            project_tensor(pe, 1536, KD, hrhs(SEQ), SEQ)
            turn_values_tensor(pe, 4)
            pe.wait_ge(aoperand_ready.sem, aoperand_ready.next())
            attend_tensor(pe, 8, lambda h: qfull[0:NR, h, :], lambda h: kfull[0:NR, h, :],
                          lambda h, t: odd_v[:, t, h * HD:(h + 1) * HD])
            stick_tensor(pe)
            pe.wait_ge(operand_ready.sem, operand_ready.next())
            project_tensor(pe, D, KD, lambda k: odd_o[:, k, :], SEQ)

        def odd_vector(dve):
            project_vector(dve, 512, lambda m, rows, b: dve.tensor_copy(cq[:, m, :], b[:, 0:SEQ]))
            b = take_bank(dve, "v")
            r = slice(64, 96)
            dve.tensor_copy(krope[r, :], b[r, 0:SEQ]).then_inc(EV, 1)
            dve.drain().then_inc(operand_ready.sem, 1)
            b = take_bank(dve, "v")
            dve.tensor_tensor(rope_t[r, 0, :], b[r, 0:SEQ], C("sin_mla")[r, :], ALU.mult).then_inc(EV, 1)
            dve.tensor_tensor(krope[r, :], krope[r, :], C("cos_mla")[r, :], ALU.mult)
            dve.drain()
            for h in range(8):
                dve.tensor_tensor(kfull[r, h, :], krope[r, :], rope_t[r, 0, :], ALU.add)
            for part, g in ((0, "mla_q_norm_g"), (1, "mla_kv_norm_g")):
                dve.drain().then_inc(latent_ready.sem, 1)
                norm_vector(dve, RANK, SEQ)
                for k in range(2):
                    dve.scalar_tensor_tensor(out=cq[:, 2 * part + k, :], in0=cq[:, 2 * part + k, :], scalar=V(g, k),
                                             in1=rstd[:, 0:SEQ], op0=ALU.mult, op1=ALU.mult)
            dve.drain().then_inc(operand_ready.sem, 1)
            for h in range(8):
                b = take_bank(dve, "v")
                dve.tensor_copy(qfull[0:NR, h, :], b[0:NR, 0:SEQ]).then_inc(EV, 1)
            dve.drain().then_inc(operand_ready.sem, 1)
            for h in range(8):
                b = take_bank(dve, "v")
                t = rope_t[0:NR, h % 2, :]
                dve.tensor_tensor(t, b[0:NR, 0:SEQ], C("sin_mla"), ALU.mult).then_inc(EV, 1)
                dve.tensor_tensor(qfull[0:NR, h, :], qfull[0:NR, h, :], C("cos_mla"), ALU.mult)
                dve.drain()
                dve.tensor_tensor(qfull[0:NR, h, :], qfull[0:NR, h, :], t, ALU.add)
            for g in range(2):
                for h in range(4 * g, 4 * g + 4):
                    b = take_bank(dve, "v")
                    dve.tensor_copy(kfull[0:HD, h, :], b[0:HD, 0:SEQ]).then_inc(EV, 1)
                for t in range(2):
                    b = take_bank(dve, "v")
                    dve.tensor_copy(odd_v[:, t, g * SEQ:(g + 1) * SEQ], b[:, 0:SEQ]).then_inc(EV, 1)

            def put(m, rows, b):
                if m < 4:
                    return dve.tensor_scalar(stick_q[:, m, :], b[:, 0:SEQ], HD ** -0.5, None, ALU.mult)
                if m < 8:
                    return dve.tensor_copy(stick_k[:, m - 4, :], b[:, 0:SEQ])
                return dve.tensor_copy(S[:, m - 8, 0:SEQ], b[:, 0:SEQ])
            project_vector(dve, 1536, put)
            dve.drain().then_inc(operand_ready.sem, 1)
            attend_vector(dve, 8, NR ** -0.5, lambda h: C("causal"), head_rows(odd_o))
            stick_vector(dve)
            dve.drain().then_inc(operand_ready.sem, 1)
            project_vector(dve, D, lambda m, rows, b: dve.tensor_copy(H[:, m, 0:SEQ], b[:, 0:SEQ]))
            dve.drain().then_inc(dve_done_y.sem, 1)

        def odd_scalar(act):
            for part in range(2):
                act.wait_ge(latent_ready.sem, latent_ready.next())
                norm_scalar(act, cq[:, 2 * part:2 * part + 2, :], 2, SEQ)
            for m in range(4):
                b = take_bank(act, "a")
                act.activation(odd_v[:, :, 512 + m * P:512 + (m + 1) * P], b[:, 0:2 * P].rearrange("p (t f) -> p t f", t=2),
                               ACT.Copy).then_inc(EA, 1)
            act.drain().then_inc(aoperand_ready.sem, 1)
            attend_scalar(act, 8)
            stick_scalar(act)

        latent_ready = signal("latent_ready")
        score_ready = signal("score_ready")
        log_ready = signal("log_ready")
        rest_ready = signal("rest_ready")
        share_ready = signal("share_ready")

        def stick_tensor(pe):
            qh, kh = head_rows(stick_q), head_rows(stick_k)
            for i in range(8 + 2):
                if i < 8:
                    b = fill_bank(pe, "v")
                    for kt in range(2):
                        mm = pe.matmul(b[:, kt * SEQ:(kt + 1) * SEQ], kh(i)[:, kt * P:(kt + 1) * P], qh(i), start=True, stop=True)
                    mm.then_inc(FV, 1)
                if 1 <= i <= 8:
                    t = stick_t[:, (i - 1) % 2, :]
                    pe.wait_ge(operand_ready.sem, operand_ready.next())
                    b = fill_bank(pe, "v")
                    pe.matmul(b[:, 0:SEQ], C("later"), t[:, 0:SEQ], start=True, stop=False)
                    pe.matmul(b[:, 0:SEQ], C("ones"), t[:, SEQ:], start=False, stop=True)
                    pe.matmul(b[:, SEQ:], C("later"), t[:, SEQ:], start=True, stop=True).then_inc(FV, 1)
                if i >= 2:
                    h = i - 2
                    pe.wait_ge(operand_ready.sem, operand_ready.next())
                    b = fill_bank(pe, "v")
                    for kt in range(2):
                        mm = pe.matmul(b[64 * (h % 2):64 * (h % 2) + 64, 0:SEQ], odd_v[:, kt, 512 + h * HD:512 + (h + 1) * HD],
                                       stick_z[:, h % 3, kt * SEQ:(kt + 1) * SEQ], start=(kt == 0), stop=(kt == 1))
                    mm.then_inc(FV, 1)

        def stick_vector(dve):
            for i in range(8 + 2):
                if i < 8:
                    b = take_bank(dve, "v")
                    dve.tensor_tensor(stick_z[:, i % 3, :], b[:, :], C("strict"), ALU.mult).then_inc(EV, 1)
                    dve.drain().then_inc(score_ready.sem, 1)
                if 1 <= i <= 8:
                    t, z = stick_t[:, (i - 1) % 2, :], stick_z[:, (i - 1) % 3, :]
                    dve.wait_ge(log_ready.sem, log_ready.next())
                    dve.scalar_tensor_tensor(out=t, in0=z, scalar=0.0, in1=t, op0=ALU.max, op1=ALU.add)
                    dve.drain()
                    dve.tensor_tensor(t, t, C("strict"), ALU.mult).then_inc(operand_ready.sem, 1)
                if i >= 2:
                    z = stick_z[:, (i - 2) % 3, :]
                    dve.wait_ge(share_ready.sem, share_ready.next())
                    dve.tensor_tensor(z, z, C("strict"), ALU.mult).then_inc(operand_ready.sem, 1)
                if 1 <= i <= 8:
                    z = stick_z[:, (i - 1) % 3, :]
                    b = take_bank(dve, "v")
                    dve.tensor_tensor(z, z, b[:, :], ALU.subtract).then_inc(EV, 1)
                    dve.drain().then_inc(rest_ready.sem, 1)
                if i >= 2:
                    h = i - 2
                    b = take_bank(dve, "v")
                    dve.tensor_copy(odd_o[64 * (h % 2):64 * (h % 2) + 64, 4 + h // 2, :],
                                    b[64 * (h % 2):64 * (h % 2) + 64, 0:SEQ]).then_inc(EV, 1)

        def stick_scalar(act):
            for i in range(8 + 1):
                if i < 8:
                    t = stick_t[:, i % 2, :]
                    act.wait_ge(score_ready.sem, score_ready.next())
                    act.activation(t, stick_z[:, i % 3, :], ACT.Abs)
                    act.drain()
                    act.activation(t, t, ACT.Exp, scale=-1.0)
                    act.drain()
                    act.activation(t, t, ACT.Ln, bias=1.0).then_inc(log_ready.sem, 1)
                if i >= 1:
                    act.wait_ge(rest_ready.sem, rest_ready.next())
                    z = stick_z[:, (i - 1) % 3, :]
                    act.activation(z, z, ACT.Exp).then_inc(share_ready.sem, 1)

        Q = L
        NIN = A["w_in_2"].shape[2]
        MIN = -(-NIN // P)
        proj = view(0, MIN, L)
        A_T, B_T, C_T = 0, 9, 21
        CH = 16
        NCH = L // CH

        for_scalar = signal("for_scalar")
        from_scalar = signal("from_scalar")

        def gain_norm_vector(dve, g, l, n=KD):
            norm_vector(dve, D, L)
            for k in range(KD):
                dve.scalar_tensor_tensor(out=H[:, k, :], in0=X[:, k, :], scalar=V(g, l * KD + k), in1=rstd[:, :],
                                         op0=ALU.mult, op1=ALU.mult)
            dve.drain().then_inc(operand_ready.sem, 1)

        def second_in_plan(l):
            project_plan(A["w_in_2"][l], NIN, KD)

        def second_in_tensor(pe):
            norm_tensor(pe, KD, L)
            pe.wait_ge(operand_ready.sem, operand_ready.next())
            project_tensor(pe, NIN, KD, lambda k: H[:, k, :], L)

        def second_in_vector(dve, l):
            gain_norm_vector(dve, "norm1_g_2", l)
            project_vector(dve, NIN, lambda m, rows, b: dve.tensor_copy(proj[0:rows, m, :], b[0:rows, 0:L]))

        DB = MIN * Q
        diff_v = view(DB, 3, 512)
        diff_e = view(DB + 1536, 2, 2, L)
        diff_t = view(DB + 1536 + 4 * L, 2, 3 * P)
        diff_r = view(DB + 1536 + 4 * L + 6 * P, 2, L)
        UNITS = [(h, t) for h in range(4) for t in range(3)]

        def diff_tensor(pe):
            for m in range(8):
                b = fill_bank(pe, "v")
                pe.matmul(b[:, 0:L], C("rot_diff"), proj[:, B_T + m, :], start=True, stop=True).then_inc(FV, 1)
            for t, (t0, n) in enumerate(TILES):
                b = fill_bank(pe, "a")
                for m in range(4):
                    mm = pe.transpose(b[0:n, m * P:(m + 1) * P], proj[:, B_T + 8 + m, t0:t0 + n], C("ident"))
                mm.then_inc(FA, 1)
            pe.wait_ge(operand_ready.sem, operand_ready.next())
            b = fill_bank(pe, "v")
            pe.matmul(b[:, 0:2], C("ones")[0:HD, :], small[0:HD, 32:34], start=True, stop=True).then_inc(FV, 1)
            for i in range(len(UNITS) + 2):
                if i < len(UNITS):
                    h, t = UNITS[i]
                    t0, n = TILES[t]
                    for c in range(2):
                        r = slice(64 * c, 64 * c + 64)
                        b = fill_bank(pe, "v")
                        pe.matmul(b[0:n, 0:L], proj[r, B_T + h, t0:t0 + n], proj[r, B_T + 4 + h, :], start=True, stop=True)\
                            .then_inc(FV, 1)
                if 1 <= i <= len(UNITS):
                    h, t = UNITS[i - 1]
                    n = TILES[t][1]
                    pe.wait_ge(operand_ready.sem, operand_ready.next())
                    b = fill_bank(pe, "a")
                    for kt, (k0, kn) in enumerate(TILES):
                        mm = pe.transpose(b[0:kn, kt * P:kt * P + n], diff_e[0:n, (i - 1) % 2, 0, k0:k0 + kn],
                                          C("ident")[0:n, 0:n])
                    mm.then_inc(FA, 1)
                if i >= 2:
                    h, t = UNITS[i - 2]
                    n = TILES[t][1]
                    pe.wait_ge(aoperand_ready.sem, aoperand_ready.next())
                    b = fill_bank(pe, "v")
                    for kt, (k0, kn) in enumerate(TILES):
                        mm = pe.matmul(b[:, 0:n], diff_v[0:kn, kt, h * P:(h + 1) * P],
                                       diff_t[0:kn, i % 2, kt * P:kt * P + n], start=(kt == 0), stop=(kt == 2))
                    mm.then_inc(FV, 1)
            for h in range(4):
                norm_tensor(pe, 1, L)

        def diff_vector(dve, l):
            lam_init = 0.8 - 0.6 * math.exp(-0.3 * l)
            for m in range(8):
                b = take_bank(dve, "v")
                dve.tensor_tensor(diff_r[:, m % 2, :], b[:, 0:L], C("sin_diff"), ALU.mult).then_inc(EV, 1)
                dve.tensor_tensor(proj[:, B_T + m, :], proj[:, B_T + m, :], C("cos_diff"), ALU.mult)
                dve.drain()
                dve.tensor_tensor(proj[:, B_T + m, :], proj[:, B_T + m, :], diff_r[:, m % 2, :], ALU.add)
            for j in range(2):
                dve.tensor_tensor(small[0:HD, 32 + j:33 + j], V("df_lam_2", 4 * l + 2 * j, 1, HD),
                                  V("df_lam_2", 4 * l + 2 * j + 1, 1, HD), ALU.mult)
            dve.drain().then_inc(operand_ready.sem, 1)
            b = take_bank(dve, "v")
            dve.tensor_copy(small[:, 34:36], b[:, 0:2]).then_inc(EV, 1)
            dve.drain().then_inc(for_scalar.sem, 1)
            dve.wait_ge(from_scalar.sem, from_scalar.next())
            dve.tensor_tensor(small[:, 36:37], small[:, 35:36], small[:, 34:35], ALU.subtract)
            dve.drain()
            dve.tensor_scalar(small[:, 36:37], small[:, 36:37], -lam_init, None, ALU.add)
            dve.drain()
            for i in range(len(UNITS) + 2):
                if i < len(UNITS):
                    h, t = UNITS[i]
                    n = TILES[t][1]
                    o = 8 * (i % 2)
                    for c in range(2):
                        b = take_bank(dve, "v")
                        dve.tensor_copy(diff_e[0:n, i % 2, c, :], b[0:n, 0:L]).then_inc(EV, 1)
                    dve.drain()
                    dve.tensor_reduce(small[0:n, o:o + 2], diff_e[0:n, i % 2, :, :], AX.X, ALU.max)
                    dve.drain()
                    dve.tensor_scalar(small[0:n, o:o + 2], small[0:n, o:o + 2], -HD ** -0.5, None, ALU.mult)\
                        .then_inc(logits_ready.sem, 1)
                if 1 <= i <= len(UNITS):
                    h, t = UNITS[i - 1]
                    n = TILES[t][1]
                    o = 8 * ((i - 1) % 2)
                    e = diff_e[0:n, (i - 1) % 2, :, :]
                    dve.wait_ge(exp_ready.sem, exp_ready.next())
                    dve.reciprocal(small[0:n, o + 4:o + 6], small[0:n, o + 2:o + 4])
                    dve.drain()
                    dve.tensor_scalar(small[0:n, o + 6:o + 7], small[0:n, o + 5:o + 6], small[0:n, 36:37], None, ALU.mult)
                    dve.tensor_scalar(e[:, 0, :], e[:, 0, :], small[0:n, o + 4:o + 5], None, ALU.mult)
                    dve.drain()
                    dve.scalar_tensor_tensor(out=e[:, 0, :], in0=e[:, 1, :], scalar=small[0:n, o + 6:o + 7], in1=e[:, 0, :],
                                             op0=ALU.mult, op1=ALU.add).then_inc(operand_ready.sem, 1)
                if i >= 2:
                    h, t = UNITS[i - 2]
                    t0, n = TILES[t]
                    b = take_bank(dve, "v")
                    dve.tensor_copy(H[:, 2 + h, t0:t0 + n], b[:, 0:n]).then_inc(EV, 1)
            for h in range(4):
                dve.drain().then_inc(latent_ready.sem, 1)
                norm_vector(dve, P, L)
                dve.tensor_tensor(H[:, 2 + h, :], H[:, 2 + h, :], rstd[:, :], ALU.mult)
                dve.drain()
                dve.tensor_scalar(H[:, 2 + h, :], H[:, 2 + h, :], V("df_subln_g_2", l), 1.0 - lam_init, ALU.mult, ALU.mult)

        def diff_scalar(act):
            for t, (t0, n) in enumerate(TILES):
                b = take_bank(act, "a")
                act.activation(diff_v[0:n, t, :], b[0:n, :], ACT.Copy).then_inc(EA, 1)
            act.wait_ge(for_scalar.sem, for_scalar.next())
            act.activation(small[:, 34:36], small[:, 34:36], ACT.Exp).then_inc(from_scalar.sem, 1)
            for i in range(len(UNITS) + 1):
                if i < len(UNITS):
                    n = TILES[UNITS[i][1]][1]
                    o = 8 * (i % 2)
                    act.wait_ge(logits_ready.sem, logits_ready.next())
                    for c in range(2):
                        e = diff_e[0:n, i % 2, c, :]
                        ins = act.activation(e, e, ACT.Exp, bias=small[0:n, o + c:o + c + 1], scale=HD ** -0.5,
                                             accum_out=small[0:n, o + 2 + c:o + 3 + c])
                    ins.then_inc(exp_ready.sem, 1)
                if i >= 1:
                    n = TILES[UNITS[i - 1][1]][1]
                    b = take_bank(act, "a")
                    for kt, (k0, kn) in enumerate(TILES):
                        ins = act.activation(diff_t[0:kn, (i - 1) % 2, kt * P:kt * P + n], b[0:kn, kt * P:kt * P + n], ACT.Copy)
                    ins.then_inc(EA, 1)
                    act.drain().then_inc(aoperand_ready.sem, 1)
            for h in range(4):
                act.wait_ge(latent_ready.sem, latent_ready.next())
                norm_scalar(act, H[:, 2 + h:3 + h, :], 1, L)

        G0 = MIN * Q
        gl = [view(G0 + 5 * Q * d, 5, L) for d in range(2)]
        gl_dc = view(G0 + 10 * Q, 2, NCH)
        gl_kt = view(G0 + 10 * Q + 40, 2, 3 * P)
        gl_v = view(G0 + 10 * Q + 40 + 6 * P, 3, 256)
        gl_ve = view(G0 + 10 * Q + 40 + 12 * P, 4, 8, HD)
        gl_st = view(G0 + 10 * Q + 40 + 12 * P + 2048, 2, NCH, HD)
        gl_at = view(G0 + 10 * Q + 40 + 12 * P + 2048 + 2 * NCH * HD, 4, 2, P)

        def ends_of(x, d):
            c = x.rearrange("p (c t) -> p c t", t=CH)
            return c[:, :, CH - 1:CH] if d == 0 else c[:, :, 0:1]

        def cumsum(dve, out, x, d):
            if d == 0:
                return dve.tensor_tensor_scan(out, C("go_f"), x, 0.0, ALU.mult, ALU.add)
            return dve.tensor_tensor_scan(out[:, ::-1], C("go_b")[:, ::-1], x[:, ::-1], 0.0, ALU.mult, ALU.add)

        def gla_tensor(pe, l):
            for d in range(2):
                b = fill_bank(pe, "v")
                pe.matmul(b[:, 0:L], V("gl_gate_up_2", (2 * l + d) * P, P, 32), proj[0:32, C_T + 6, :], start=True, stop=True)\
                    .then_inc(FV, 1)
            for t, (t0, n) in enumerate(TILES):
                b = fill_bank(pe, "v")
                for m in range(2):
                    mm = pe.transpose(b[0:n, m * P:(m + 1) * P], proj[:, C_T + 2 + m, t0:t0 + n], C("ident"))
                mm.then_inc(FV, 1)
            for d in range(2):
                pe.wait_ge(operand_ready.sem, operand_ready.next())
                b = fill_bank(pe, "v")
                for t, (t0, n) in enumerate(TILES):
                    mm = pe.transpose(b[0:n, t * P:(t + 1) * P], gl[d][:, 3, t0:t0 + n], C("ident"))
                mm.then_inc(FV, 1)
            for t, (t0, n) in enumerate(TILES):
                nc_ = n // CH
                pe.wait_ge(operand_ready.sem, operand_ready.next())
                for d in range(2):
                    b = fill_bank(pe, "v")
                    for h in range(4):
                        mm = pe.matmul(b[32 * h:32 * h + 32, 0:nc_ * HD], gl_kt[0:n, d, t * P + 32 * h:t * P + 32 * h + 32],
                                       gl_ve[0:n, h, 0:nc_, :], start=True, stop=True, tile_position=(0, 32 * h))
                    mm.then_inc(FV, 1)
            pe.wait_ge(operand_ready.sem, operand_ready.next())
            for t, (t0, n) in enumerate(TILES):
                for h in range(4):
                    r = slice(32 * h, 32 * h + 32)
                    b = fill_bank(pe, "v")
                    for d in range(2):
                        mm = pe.matmul(b[0:n, d * P:d * P + n], gl[d][r, 2, t0:t0 + n], gl[d][r, 1, t0:t0 + n],
                                       start=True, stop=True, tile_position=(32 * h, 0))
                    mm.then_inc(FV, 1)
                pe.wait_ge(operand_ready.sem, operand_ready.next())
                for j in range(2):
                    b = fill_bank(pe, "v")
                    for h in (2 * j, 2 * j + 1):
                        rr = 64 * (h % 2)
                        parts = []
                        for d in range(2):
                            parts.append((0, n, gl_v[0:n, t, h * HD:(h + 1) * HD], gl_at[0:n, h, d, 0:n], (0, rr)))
                        for d in range(2):
                            for c in range(t0 // CH, (t0 + n) // CH):
                                prev = c - 1 if d == 0 else c + 1
                                if 0 <= prev < NCH:
                                    parts.append((c * CH - t0, CH, gl_st[32 * h:32 * h + 32, d, prev, :],
                                                  gl[d][32 * h:32 * h + 32, 1, c * CH:(c + 1) * CH], (32 * h, rr)))
                        for i, (a, w, lhs, rhs, tp) in enumerate(parts):
                            if i == 2 and n <= 32:
                                pe.drain()
                            mm = pe.matmul(b[rr:rr + 64, a:a + w], lhs, rhs, start=(i == 0), stop=(i == len(parts) - 1),
                                           skip_group_check=True, tile_position=tp)
                    mm.then_inc(FV, 1)
            for m in range(2):
                norm_tensor(pe, 1, L, C("ones64"))

        def gla_vector(dve, l):
            for d in range(2):
                b = take_bank(dve, "v")
                dve.tensor_scalar(gl[d][:, 0, :], b[:, 0:L], V("gl_gate_b_2", 2 * l + d), None, ALU.add).then_inc(EV, 1)
                dve.drain().then_inc(for_scalar.sem, 1)
            for t, (t0, n) in enumerate(TILES):
                b = take_bank(dve, "v")
                dve.tensor_copy(gl_v[0:n, t, :], b[0:n, 0:256]).then_inc(EV, 1)
            for d in range(2):
                z, tmp = gl[d][:, 0, :], gl[d][:, 4, :]
                dve.wait_ge(from_scalar.sem, from_scalar.next())
                dve.scalar_tensor_tensor(out=tmp, in0=z, scalar=0.0, in1=tmp, op0=ALU.min, op1=ALU.subtract)
                dve.drain()
                dve.tensor_scalar(tmp, tmp, 1.0 / 16.0, None, ALU.mult)
                dve.drain()
                cumsum(dve, z, tmp, d)
                dve.drain()
                dve.tensor_tensor(gl[d][:, 3, :].rearrange("p (c t) -> p c t", t=CH),
                                  ends_of(z, d).to_broadcast([P, NCH, CH]), z.rearrange("p (c t) -> p c t", t=CH),
                                  ALU.subtract)
                dve.drain().then_inc(for_scalar.sem, 1)
            for d in range(2):
                g = gl[d]
                dve.wait_ge(from_scalar.sem, from_scalar.next())
                dve.tensor_copy(gl_dc[:, d, :], ends_of(g[:, 1, :], d).rearrange("p c o -> p (c o)"))
                dve.drain()
                dve.scalar_tensor_tensor(out=g[:, 1, :], in0=g[:, 1, :], scalar=32 ** -0.5, in1=proj[:, C_T, :],
                                         op0=ALU.mult, op1=ALU.mult)
                dve.tensor_tensor(g[:, 2, :], g[:, 2, :], proj[:, C_T + 1, :], ALU.mult)
                dve.tensor_tensor(g[:, 3, :], g[:, 3, :], proj[:, C_T + 1, :], ALU.mult)
                dve.drain().then_inc(operand_ready.sem, 1)
                b = take_bank(dve, "v")
                dve.tensor_copy(gl_kt[:, d, 0:2 * P], b[:, 0:2 * P])
                dve.tensor_copy(gl_kt[0:16, d, 2 * P:3 * P], b[0:16, 2 * P:3 * P]).then_inc(EV, 1)
            for t, (t0, n) in enumerate(TILES):
                nc_ = n // CH
                dve.drain()
                for h in range(4):
                    dve.tensor_tensor(gl_ve[0:n, h, 0:nc_, :],
                                      gl_v[0:n, t, h * HD:(h + 1) * HD].unsqueeze(1).to_broadcast([n, nc_, HD]),
                                      C("chunk_of")[0:n, 0:nc_].unsqueeze(2).to_broadcast([n, nc_, HD]), ALU.mult)
                dve.drain().then_inc(operand_ready.sem, 1)
                for d in range(2):
                    b = take_bank(dve, "v")
                    dve.tensor_copy(gl_st[:, d, t0 // CH:t0 // CH + nc_, :],
                                    b[:, 0:nc_ * HD].rearrange("p (c v) -> p c v", v=HD)).then_inc(EV, 1)
            dve.drain()
            for i in range(1, NCH):
                for d in range(2):
                    c, prev = (i, i - 1) if d == 0 else (NCH - 1 - i, NCH - i)
                    dve.scalar_tensor_tensor(out=gl_st[:, d, c, :], in0=gl_st[:, d, prev, :], scalar=gl_dc[:, d, c:c + 1],
                                             in1=gl_st[:, d, c, :], op0=ALU.mult, op1=ALU.add)
                dve.drain()
            dve.drain().then_inc(operand_ready.sem, 1)
            for t, (t0, n) in enumerate(TILES):
                for h in range(4):
                    b = take_bank(dve, "v")
                    dve.tensor_tensor(gl_at[0:n, h, :, 0:n], b[0:n, 0:2 * P].rearrange("p (d t) -> p d t", d=2)[:, :, 0:n],
                                      C("le_fb")[0:n, :].rearrange("p (d t) -> p d t", d=2)[:, :, 0:n],
                                      ALU.mult).then_inc(EV, 1)
                dve.drain().then_inc(operand_ready.sem, 1)
                for j in range(2):
                    b = take_bank(dve, "v")
                    dve.tensor_copy(H[:, 6 + j, t0:t0 + n], b[:, 0:n]).then_inc(EV, 1)
            for m in range(2):
                dve.drain().then_inc(latent_ready.sem, 1)
                norm_vector(dve, HD, L)
                dve.tensor_tensor(H[:, 6 + m, :], H[:, 6 + m, :], rstd[:, :], ALU.mult)
                dve.drain()
                dve.scalar_tensor_tensor(out=H[:, 6 + m, :], in0=H[:, 6 + m, :], scalar=V("gl_norm_g_2", l),
                                         in1=proj[:, C_T + 4 + m, :], op0=ALU.mult, op1=ALU.mult)

        def gla_scalar(act):
            for d in range(2):
                t = gl[d][:, 4, :]
                act.wait_ge(for_scalar.sem, for_scalar.next())
                act.activation(t, gl[d][:, 0, :], ACT.Abs)
                act.drain()
                act.activation(t, t, ACT.Exp, scale=-1.0)
                act.drain()
                act.activation(t, t, ACT.Ln, bias=1.0).then_inc(from_scalar.sem, 1)
            for d in range(2):
                g = gl[d]
                act.wait_ge(for_scalar.sem, for_scalar.next())
                act.activation(g[:, 1, :], g[:, 0, :], ACT.Exp)
                act.activation(g[:, 2, :], g[:, 0, :], ACT.Exp, scale=-1.0)
                act.activation(g[:, 3, :], g[:, 3, :], ACT.Exp)
                act.drain().then_inc(from_scalar.sem, 1)
            act.activation(proj[:, C_T + 4:C_T + 6, :], proj[:, C_T + 4:C_T + 6, :], ACT.Silu)
            act.drain()
            for m in range(2):
                act.wait_ge(latent_ready.sem, latent_ready.next())
                norm_scalar(act, H[:, 6 + m:7 + m, :], 1, L)

        raw = view(0, 9, L)
        sh = view(9 * Q, 9, L)
        kk, rw_o, ksum, rtmp = view(0, 2, L), view(2 * Q, 2, L), view(4 * Q, 2, L), view(6 * Q, 2, L)
        kdir, ka, lwa, bR, Kb, Bb = [view((18 + 2 * i) * Q, 2, L) for i in range(6)]
        R0 = 30 * Q
        rv = view(R0, 3, 256)
        kht, bht = view(R0 + 768, 256), view(R0 + 1024, 256)
        rve, rbe, rpe = [view(R0 + 1280 + 1024 * i, 2, 8, HD) for i in range(3)]
        rF = view(R0 + 4352, 2, NCH, HD)
        rS = view(R0 + 4352 + 2 * NCH * HD, 2, NCH, HD)
        M0 = R0 + 4352 + 4 * NCH * HD
        s_flat = S[:, :, :].rearrange("p a b -> p (a b)")
        mT, mM, mM2, mM2T = [s_flat[:, 512 * i:512 * (i + 1)].rearrange("p (h t) -> p h t", h=4) for i in range(4)]
        nT, LkT, LbT, Z = [view(M0 + 512 * i, 4, P) for i in range(4)]
        rdc = view(M0 + 2048, 2, NCH)

        def rwkv_plan(l):
            for w in ("rw_w_up_2", "rw_a_up_2"):
                plan.append((A[w][l].rearrange("d r c -> (d r) c").unsqueeze(1), 1, 256))
            plan.append((A["rw_g_up_2"][l].unsqueeze(1), 1, 256))

        def rwkv_tensor(pe, l):
            pe.wait_ge(operand_ready.sem, operand_ready.next())
            for j in range(2):
                b = fill_bank(pe, "v")
                pe.matmul(b[:, 0:L], C("ones64"), S[:, j, :], start=True, stop=True).then_inc(FV, 1)
            for t, (t0, n) in enumerate(TILES):
                b = fill_bank(pe, "v")
                for j in range(2):
                    mm = pe.transpose(b[0:n, j * P:(j + 1) * P], sh[:, 4 + j, t0:t0 + n], C("ident"))
                mm.then_inc(FV, 1)
            W = [next_slot(pe, 1, 256) for _ in range(3)]
            pe.wait_ge(aoperand_ready.sem, aoperand_ready.next())
            for d in range(2):
                dr = slice(64 * d, 64 * d + 64)
                for part in range(2):
                    for j in range(2):
                        b = fill_bank(pe, "v")
                        pe.matmul(b[:, 0:L], W[part][dr, 0, j * P:(j + 1) * P], sh[dr, 6 + part, :], start=True, stop=True)\
                            .then_inc(FV, 1)
                pe.wait_ge(operand_ready.sem, operand_ready.next())
                for t in range(3):
                    rwkv_tile_tensor(pe, d, t)
                for i in range(1, NCH):
                    c, prev = (i, i - 1) if d == 0 else (NCH - 1 - i, NCH - i)
                    pe.wait_ge(operand_ready.sem, operand_ready.next())
                    b = fill_bank(pe, "v")
                    for h in range(4):
                        r, j = slice(64 * (h % 2), 64 * (h % 2) + 64), h // 2
                        mm = pe.matmul(b[r, j * HD:(j + 1) * HD], rF[r, j, c, :], rS[r, j, prev, :], start=True, stop=True)
                    mm.then_inc(FV, 1)
                pe.wait_ge(operand_ready.sem, operand_ready.next())
                for t, (t0, n) in enumerate(TILES):
                    pairs = inter_chunks(d, t0, n)
                    if not pairs:
                        continue
                    b = fill_bank(pe, "v")
                    for c, prev in pairs:
                        for h in range(4):
                            r, j = slice(64 * (h % 2), 64 * (h % 2) + 64), h // 2
                            a = j * P + c * CH - t0
                            mm = pe.matmul(b[r, a:a + CH], rS[r, j, prev, :], bR[r, j, c * CH:(c + 1) * CH], start=True, stop=True)
                    mm.then_inc(FV, 1)
            for j in range(2):
                b = fill_bank(pe, "v")
                pe.matmul(b[:, 0:L], W[2][:, 0, j * P:(j + 1) * P], sh[:, 8, :], start=True, stop=True).then_inc(FV, 1)
            for _ in range(3):
                read_with_bank()
            pe.wait_ge(operand_ready.sem, operand_ready.next())
            for src in (rw_o, rtmp):
                for j in range(2):
                    b = fill_bank(pe, "v")
                    pe.matmul(b[:, 0:L], C("ones64"), src[:, j, :], start=True, stop=True).then_inc(FV, 1)
            for j in range(2):
                norm_tensor(pe, 1, L, C("ones64"))

        def inter_chunks(d, t0, n):
            out = [(c, c - 1 if d == 0 else c + 1) for c in range(t0 // CH, (t0 + n) // CH)]
            return [(c, p) for c, p in out if 0 <= p < NCH]

        def rwkv_tile_tensor(pe, d, t):
            t0, n = TILES[t]
            tok = slice(t0, t0 + n)
            nc_ = n // CH
            b = fill_bank(pe, "v")
            for i, src in enumerate((lwa, kdir)):
                for j in range(2):
                    mm = pe.transpose(b[0:n, i * 256 + j * P:i * 256 + (j + 1) * P], src[:, j, tok], C("ident"))
            mm.then_inc(FV, 1)
            b = fill_bank(pe, "v")
            for j in range(2):
                mm = pe.transpose(b[0:n, j * P:(j + 1) * P], ka[:, j, tok], C("ident"))
            mm.then_inc(FV, 1)
            for pp in range(2):
                r = slice(64 * pp, 64 * pp + 64)
                for pairs in (((Bb, lwa), (lwa, Bb)), ((Kb, lwa), (Kb, bR)), ((Bb, bR),)):
                    b = fill_bank(pe, "v")
                    for i, (x, y) in enumerate(pairs):
                        for j in range(2):
                            a = (2 * i + j) * P
                            mm = pe.matmul(b[0:n, a:a + n], x[r, j, tok], y[r, j, tok], start=True, stop=True)
                    mm.then_inc(FV, 1)
            pe.wait_ge(operand_ready.sem, operand_ready.next())

            def per_head(lhs, rhs, w):
                b = fill_bank(pe, "v")
                for h in range(4):
                    mm = pe.matmul(b[0:n, h * w:h * w + (n if rhs is not Z and w == P else w)], lhs(h), rhs_of(rhs, h, w), start=True, stop=True)
                mm.then_inc(FV, 1)

            def rhs_of(rhs, h, w):
                if rhs is Z:
                    return Z[0:n, h, :]
                if rhs is rv:
                    return rv[0:n, t, h * HD:(h + 1) * HD]
                return rhs[0:n, h, 0:n]
            m = lambda x: (lambda h: x[0:n, h, 0:n])
            per_head(m(nT), rv, HD)
            per_head(m(mT), mM, P)
            per_head(m(mM), mT, P)
            pe.wait_ge(operand_ready.sem, operand_ready.next())
            per_head(m(mM2T), mM2, P)
            per_head(m(mM2), mM2T, P)
            pe.wait_ge(operand_ready.sem, operand_ready.next())
            per_head(m(mM), nT, P)
            for power in (None, nT, mM2T, mT):
                pe.wait_ge(operand_ready.sem, operand_ready.next())
                per_head(m(mM2 if power is None else power), Z, P)
            pe.wait_ge(operand_ready.sem, operand_ready.next())
            b = fill_bank(pe, "v")
            for h in range(4):
                rr, j = 64 * (h % 2), h // 2
                mm = pe.matmul(b[rr:rr + 64, j * P:j * P + n], Z[0:n, h, 0:HD], LbT[0:n, h, 0:n], start=True, stop=True)
            mm.then_inc(FV, 1)
            b = fill_bank(pe, "v")
            for h in range(4):
                rr, j = 64 * (h % 2), h // 2
                o = b[rr:rr + 64, j * P:j * P + n]
                pe.matmul(o, rv[0:n, t, h * HD:(h + 1) * HD], LkT[0:n, h, 0:n], start=True, stop=False)
                mm = pe.matmul(o, Z[0:n, h, HD:P], LbT[0:n, h, 0:n], start=False, stop=True)
            mm.then_inc(FV, 1)
            for j in range(2):
                pe.wait_ge(operand_ready.sem, operand_ready.next())
                b = fill_bank(pe, "v")
                for hh in range(2):
                    mm = pe.matmul(b[64 * hh:64 * hh + 64, 0:nc_ * HD], Z[0:n, 2 * j + hh, 0:HD], rbe[0:n, hh, 0:nc_, :],
                                   start=True, stop=True)
                mm.then_inc(FV, 1)
                b = fill_bank(pe, "v")
                for hh in range(2):
                    h = 2 * j + hh
                    o = b[64 * hh:64 * hh + 64, 0:nc_ * HD]
                    pe.matmul(o, kht[0:n, h * HD:(h + 1) * HD], rve[0:n, hh, 0:nc_, :], start=True, stop=False)
                    mm = pe.matmul(o, bht[0:n, h * HD:(h + 1) * HD], rpe[0:n, hh, 0:nc_, :], start=False, stop=True)
                mm.then_inc(FV, 1)

        def rwkv_tile_vector(dve, d, t):
            t0, n = TILES[t]
            tok = slice(t0, t0 + n)
            nc_ = n // CH
            lt, lt_t, le = ("lt_f", "lt_b", "le_f") if d == 0 else ("lt_b", "lt_f", "le_b")
            b = take_bank(dve, "v")
            dve.tensor_copy(Z[0:n, :, 0:HD], b[0:n, 0:256].rearrange("p (h k) -> p h k", h=4))
            dve.tensor_copy(kht[0:n, :], b[0:n, 256:512]).then_inc(EV, 1)
            b = take_bank(dve, "v")
            dve.tensor_copy(bht[0:n, :], b[0:n, 0:256]).then_inc(EV, 1)

            def masked(b, at, out, pp, mask, sign=1.0):
                return dve.scalar_tensor_tensor(out=out[0:n, pp::2, 0:n],
                                                in0=b[0:n, at:at + 256].rearrange("p (j t) -> p j t", j=2)[:, :, 0:n],
                                                scalar=sign, in1=C(mask)[0:n, 0:n].unsqueeze(1).to_broadcast([n, 2, n]),
                                                op0=ALU.mult, op1=ALU.mult)
            for pp in range(2):
                b = take_bank(dve, "v")
                masked(b, 0, mT, pp, lt)
                masked(b, 256, mM, pp, lt_t).then_inc(EV, 1)
                b = take_bank(dve, "v")
                masked(b, 0, nT, pp, lt)
                masked(b, 256, LkT, pp, le).then_inc(EV, 1)
                b = take_bank(dve, "v")
                masked(b, 0, LbT, pp, le, -1.0).then_inc(EV, 1)
            dve.drain().then_inc(operand_ready.sem, 1)

            def copy4(out, w=P):
                b = take_bank(dve, "v")
                dve.tensor_copy(out[0:n, :, 0:n], b[0:n, :].rearrange("p (h t) -> p h t", h=4)[:, :, 0:n]).then_inc(EV, 1)
            b = take_bank(dve, "v")
            dve.tensor_copy(Z[0:n, :, HD:P], b[0:n, 0:256].rearrange("p (h v) -> p h v", h=4)).then_inc(EV, 1)
            copy4(mM2)
            copy4(mM2T)
            dve.drain().then_inc(operand_ready.sem, 1)
            copy4(mM)
            copy4(nT)
            dve.drain().then_inc(operand_ready.sem, 1)
            copy4(mM2)
            for sign in (ALU.add, ALU.add, ALU.add, ALU.subtract):
                dve.drain().then_inc(operand_ready.sem, 1)
                b = take_bank(dve, "v")
                dve.tensor_tensor(Z[0:n, :, :], Z[0:n, :, :], b[0:n, :].rearrange("p (h t) -> p h t", h=4), sign)\
                    .then_inc(EV, 1)
            dve.drain().then_inc(operand_ready.sem, 1)
            b = take_bank(dve, "v")
            two = lambda b: b[:, 0:256].rearrange("p (j t) -> p j t", j=2)[:, :, 0:n]
            dve.tensor_tensor(bR[:, :, tok], bR[:, :, tok], two(b), ALU.add).then_inc(EV, 1)
            b = take_bank(dve, "v")
            if d == 0:
                dve.tensor_copy(rw_o[:, :, tok], two(b)).then_inc(EV, 1)
            else:
                dve.tensor_tensor(rw_o[:, :, tok], rw_o[:, :, tok], two(b), ALU.add).then_inc(EV, 1)
            for j in range(2):
                chunk = C("chunk_of")[0:n, 0:nc_].unsqueeze(2).to_broadcast([n, nc_, HD])
                for hh in range(2):
                    h = 2 * j + hh
                    for out, src in ((rve, rv[0:n, t, h * HD:(h + 1) * HD]), (rbe, bht[0:n, h * HD:(h + 1) * HD]),
                                     (rpe, Z[0:n, h, HD:P])):
                        dve.tensor_tensor(out[0:n, hh, 0:nc_, :], src.unsqueeze(1).to_broadcast([n, nc_, HD]), chunk, ALU.mult)
                dve.tensor_tensor(rF[:, j, t0 // CH:t0 // CH + nc_, :], C("id64").unsqueeze(1).to_broadcast([P, nc_, HD]),
                                  rdc[:, j, t0 // CH:t0 // CH + nc_].unsqueeze(2).to_broadcast([P, nc_, HD]), ALU.mult)
                dve.drain().then_inc(operand_ready.sem, 1)
                b = take_bank(dve, "v")
                f = rF[:, j, t0 // CH:t0 // CH + nc_, :]
                dve.tensor_tensor(f, f, b[:, 0:nc_ * HD].rearrange("p (c k) -> p c k", k=HD), ALU.add).then_inc(EV, 1)
                b = take_bank(dve, "v")
                dve.tensor_copy(rS[:, j, t0 // CH:t0 // CH + nc_, :], b[:, 0:nc_ * HD].rearrange("p (c v) -> p c v", v=HD))\
                    .then_inc(EV, 1)

        def rwkv_vector(dve, l):
            mu = lambda s: V("rw_shift_2", (2 * l + s) * 9, 9)
            c0 = small[:, 40:49]
            oka = small[:, 49:51]
            dve.tensor_tensor(c0, mu(0), mu(1), ALU.add)
            dve.tensor_scalar(oka, V("rw_k_a_2", 2 * l, 2), -1.0, 1.0, ALU.mult, ALU.add)
            dve.drain()
            dve.tensor_scalar(c0, c0, -1.0, 1.0, ALU.mult, ALU.add)
            dve.drain()
            for m in range(9):
                dve.tensor_scalar(sh[:, m, :], raw[:, m, :], c0[:, m:m + 1], None, ALU.mult)
            dve.drain()
            for m in range(9):
                dve.scalar_tensor_tensor(out=sh[:, m, 1:], in0=raw[:, m, 0:L - 1], scalar=mu(0)[:, m:m + 1], in1=sh[:, m, 1:],
                                         op0=ALU.mult, op1=ALU.add)
            dve.drain()
            for m in range(9):
                dve.scalar_tensor_tensor(out=sh[:, m, 0:L - 1], in0=raw[:, m, 1:], scalar=mu(1)[:, m:m + 1],
                                         in1=sh[:, m, 0:L - 1], op0=ALU.mult, op1=ALU.add)
            dve.drain().then_inc(for_scalar.sem, 1)
            for j in range(2):
                dve.tensor_scalar(kk[:, j, :], sh[:, 2 + j, :], V("rw_k_k_2", 2 * l + j), None, ALU.mult)
            dve.drain()
            dve.tensor_tensor(S[:, 0:2, :], kk, kk, ALU.mult)
            dve.drain().then_inc(operand_ready.sem, 1)
            for j in range(2):
                b = take_bank(dve, "v")
                dve.tensor_scalar(rtmp[:, j, :], b[:, 0:L], 1e-24, None, ALU.max).then_inc(EV, 1)
            dve.drain().then_inc(for_scalar.sem, 1)
            for t, (t0, n) in enumerate(TILES):
                b = take_bank(dve, "v")
                dve.tensor_copy(rv[0:n, t, :], b[0:n, 0:256]).then_inc(EV, 1)
            dve.wait_ge(from_scalar.sem, from_scalar.next())
            dve.reciprocal(rtmp, rtmp)
            dve.drain()
            dve.tensor_tensor(kk, kk, rtmp, ALU.mult)
            dve.drain()
            for d in range(2):
                for out, g in ((lwa, "rw_w0_2"), (ka, "rw_a0_2")):
                    for j in range(2):
                        b = take_bank(dve, "v")
                        dve.tensor_scalar(out[:, j, :], b[:, 0:L], V(g, (2 * l + d) * 2 + j), None, ALU.add).then_inc(EV, 1)
                dve.drain().then_inc(for_scalar.sem, 1)
                dve.wait_ge(from_scalar.sem, from_scalar.next())
                for j in range(2):
                    dve.tensor_scalar(kdir[:, j, :], ka[:, j, :], V("rw_k_a_2", 2 * l + j), oka[:, j:j + 1], ALU.mult, ALU.add)
                dve.tensor_scalar(lwa, lwa, -0.6065306597126334, None, ALU.mult)
                dve.drain()
                dve.tensor_tensor(kdir, kdir, sh[:, 2:4, :], ALU.mult)
                dve.tensor_tensor(ka, ka, kk, ALU.mult)
                for j in range(2):
                    cumsum(dve, bR[:, j, :], lwa[:, j, :], d)
                dve.drain()
                if d == 0:
                    dve.tensor_copy(ksum, kdir)
                else:
                    dve.tensor_tensor(ksum, ksum, kdir, ALU.add)
                dve.tensor_tensor(lwa, bR, lwa, ALU.subtract)
                for j in range(2):
                    dve.tensor_tensor(rtmp[:, j, :].rearrange("p (c t) -> p c t", t=CH),
                                      ends_of(bR[:, j, :], d).to_broadcast([P, NCH, CH]),
                                      bR[:, j, :].rearrange("p (c t) -> p c t", t=CH), ALU.subtract)
                dve.drain().then_inc(for_scalar.sem, 1)
                dve.wait_ge(from_scalar.sem, from_scalar.next())
                for j in range(2):
                    dve.tensor_copy(rdc[:, j, :], ends_of(bR[:, j, :], d).rearrange("p c o -> p (c o)"))
                dve.tensor_tensor(lwa, lwa, kk, ALU.mult)
                dve.tensor_tensor(Bb, Kb, ka, ALU.mult)
                dve.drain()
                dve.tensor_tensor(Kb, Kb, kdir, ALU.mult)
                dve.tensor_tensor(bR, bR, sh[:, 0:2, :], ALU.mult)
                dve.drain()
                dve.tensor_tensor(kdir, kdir, rtmp, ALU.mult)
                for j in range(2):
                    dve.scalar_tensor_tensor(out=ka[:, j, :], in0=ka[:, j, :], scalar=-1.0, in1=rtmp[:, j, :], op0=ALU.mult,
                                             op1=ALU.mult)
                dve.drain().then_inc(operand_ready.sem, 1)
                for t in range(3):
                    rwkv_tile_vector(dve, d, t)
                for i in range(1, NCH):
                    c = i if d == 0 else NCH - 1 - i
                    dve.drain().then_inc(operand_ready.sem, 1)
                    b = take_bank(dve, "v")
                    dve.tensor_tensor(rS[:, :, c, :], rS[:, :, c, :], b[:, 0:2 * HD].rearrange("p (j v) -> p j v", j=2), ALU.add)\
                        .then_inc(EV, 1)
                dve.drain().then_inc(operand_ready.sem, 1)
                for t, (t0, n) in enumerate(TILES):
                    pairs = inter_chunks(d, t0, n)
                    if not pairs:
                        continue
                    lo, hi = min(c for c, _ in pairs) * CH, max(c for c, _ in pairs) * CH + CH
                    b = take_bank(dve, "v")
                    dve.tensor_tensor(rw_o[:, :, lo:hi], rw_o[:, :, lo:hi],
                                      b[:, 0:256].rearrange("p (j t) -> p j t", j=2)[:, :, lo - t0:hi - t0], ALU.add)\
                        .then_inc(EV, 1)
                    dve.drain()
            for j in range(2):
                b = take_bank(dve, "v")
                dve.tensor_copy(kdir[:, j, :], b[:, 0:L]).then_inc(EV, 1)
            for j in range(2):
                dve.scalar_tensor_tensor(out=rtmp[:, j, :], in0=sh[:, j, :], scalar=V("rw_r_k_2", 2 * l + j), in1=ksum[:, j, :],
                                         op0=ALU.mult, op1=ALU.mult)
            dve.drain().then_inc(operand_ready.sem, 1)
            for j in range(2):
                b = take_bank(dve, "v")
                dve.scalar_tensor_tensor(out=rw_o[:, j, :], in0=b[:, 0:L], scalar=-1.0 / HD, in1=rw_o[:, j, :],
                                         op0=ALU.mult, op1=ALU.add).then_inc(EV, 1)
            for j in range(2):
                b = take_bank(dve, "v")
                dve.tensor_tensor(ka[:, j, :], b[:, 0:L], sh[:, 4 + j, :], ALU.mult).then_inc(EV, 1)
            for j in range(2):
                dve.drain().then_inc(latent_ready.sem, 1)
                norm_vector(dve, HD, L, 64e-5)
                dve.tensor_tensor(rw_o[:, j, :], rw_o[:, j, :], rstd[:, :], ALU.mult)
                dve.drain()
                dve.tensor_scalar(rw_o[:, j, :], rw_o[:, j, :], V("rw_gn_g_2", 2 * l + j), V("rw_gn_b_2", 2 * l + j),
                                  ALU.mult, ALU.add)
                dve.drain()
                dve.tensor_tensor(rw_o[:, j, :], rw_o[:, j, :], ka[:, j, :], ALU.add)
                dve.drain()
                dve.tensor_tensor(H[:, j, :], rw_o[:, j, :], kdir[:, j, :], ALU.mult)

        def rwkv_scalar(act):
            act.wait_ge(for_scalar.sem, for_scalar.next())
            act.activation(sh[:, 6, :], sh[:, 6, :], ACT.Tanh)
            act.activation(sh[:, 8, :], sh[:, 8, :], ACT.Sigmoid)
            act.drain().then_inc(aoperand_ready.sem, 1)
            act.wait_ge(for_scalar.sem, for_scalar.next())
            act.activation(rtmp, rtmp, ACT.Sqrt).then_inc(from_scalar.sem, 1)
            for d in range(2):
                act.wait_ge(for_scalar.sem, for_scalar.next())
                act.activation(lwa, lwa, ACT.Sigmoid)
                act.activation(ka, ka, ACT.Sigmoid)
                act.drain().then_inc(from_scalar.sem, 1)
                act.wait_ge(for_scalar.sem, for_scalar.next())
                act.activation(Kb, bR, ACT.Exp, scale=-1.0)
                act.activation(lwa, lwa, ACT.Exp)
                act.activation(rtmp, rtmp, ACT.Exp)
                act.drain()
                act.activation(bR, bR, ACT.Exp)
                act.drain().then_inc(from_scalar.sem, 1)
            for j in range(2):
                act.wait_ge(latent_ready.sem, latent_ready.next())
                norm_scalar(act, rw_o[:, j:j + 1, :], 1, L)

        def mix_out_tensor(pe):
            project_tensor(pe, D, KD, lambda k: H[:, k, :], L)

        def mix_out_vector(dve):
            project_vector(dve, D, lambda m, rows, b: dve.tensor_tensor(X[:, m, :], X[:, m, :], b[:, 0:L], ALU.add))

        NE, CAP, FE = 16, 34, A["e_w1_2"].shape[3]
        KE = FE // P
        PAIRS = NE // 2
        xs = view(0, KD, NE * 64)
        gT = view(8192, PAIRS, L)
        T0 = 8192 + PAIRS * L
        utok = view(T0, 3, D)
        hot = view(T0 + 3072, 3, NE, 64)
        E0 = T0 + 6144
        aff, cum, mask = [view(E0 + 48 * i, 3, NE) for i in range(3)]
        affT, work = view(E0 + 144, L), view(E0 + 144 + L, L)
        top8 = view(E0 + 144 + 2 * L, 8)
        ghot = view(E0 + 152 + 2 * L, NE, 64)
        hs, hid2 = view(T0, FE), view(T0 + FE, FE)
        hidT = view(T0 + 2 * FE, KE, P)
        ys = view(T0 + 3 * FE, 4, D)
        CHUNKS = ((0, 512), (512, 512), (1024, 384))
        KSPLIT = ((0, 4), (4, 4), (8, 3))
        silu_ready = signal("silu_ready")

        def moe_plan(l):
            load_plan(A["router_2"][l], 0, NE, 0, KD)
            for p in range(PAIRS):
                for w in ("e_w1_2", "e_w3_2"):
                    for k in range(0, KD, 2):
                        for e in (2 * p, 2 * p + 1):
                            load_plan(A[w][l, e], 0, FE, k, 2)
                for k0, nk in KSPLIT:
                    for e in (2 * p, 2 * p + 1):
                        load_plan(A["e_w2_2"][l, e], 0, D, k0, nk)

        def moe_tensor(pe):
            norm_tensor(pe, KD, L)
            pe.wait_ge(operand_ready.sem, operand_ready.next())
            W = next_slot(pe, KD, NE)
            b = fill_bank(pe, "v")
            for t, (t0, n) in enumerate(TILES):
                for k in range(KD):
                    mm = pe.matmul(b[0:n, t * NE:(t + 1) * NE], H[:, k, t0:t0 + n], W[:, k, :], start=(k == 0), stop=(k == KD - 1))
            mm.then_inc(FV, 1)
            read_with_bank()
            for t, (t0, n) in enumerate(TILES):
                for half in range(2):
                    b = fill_bank(pe, "a")
                    for m in range(4):
                        mm = pe.transpose(b[0:n, m * P:(m + 1) * P], H[:, 4 * half + m, t0:t0 + n], C("ident"))
                    mm.then_inc(FA, 1)
            pe.wait_ge(operand_ready.sem, operand_ready.next())
            b = fill_bank(pe, "v")
            for t, (t0, n) in enumerate(TILES):
                mm = pe.transpose(b[0:NE, t0:t0 + n], aff[0:n, t, :], C("ident")[0:n, 0:n])
            mm.then_inc(FV, 1)
            pe.wait_ge(operand_ready.sem, operand_ready.next())
            b = fill_bank(pe, "v")
            for t, (t0, n) in enumerate(TILES):
                mm = pe.transpose(b[0:n, t * NE:(t + 1) * NE], work[0:NE, t0:t0 + n], C("ident")[0:NE, 0:NE])
            mm.then_inc(FV, 1)
            pe.wait_ge(operand_ready.sem, operand_ready.next())
            b = fill_bank(pe, "v")
            for t, (t0, n) in enumerate(TILES):
                o = b[0:n, t * NE:(t + 1) * NE]
                for s_ in range(t):
                    pe.matmul(o, C("ones")[:, 0:n], mask[:, s_, :], start=(s_ == 0), stop=False)
                mm = pe.matmul(o, C("before")[0:n, 0:n], mask[0:n, t, :], start=(t == 0), stop=True)
            mm.then_inc(FV, 1)
            for t, (t0, n) in enumerate(TILES):
                pe.wait_ge(operand_ready.sem, operand_ready.next())
                for half in range(2):
                    b = fill_bank(pe, "v")
                    for q in range(4):
                        p = 4 * half + q
                        mm = pe.transpose(b[:, q * P:q * P + n], ghot[0:n, 2 * p:2 * p + 2, :].rearrange("p e s -> p (e s)"),
                                          C("ident")[0:n, 0:n])
                    mm.then_inc(FV, 1)
            pe.wait_ge(aoperand_ready.sem, aoperand_ready.next())
            for k in range(KD):
                for half in range(2):
                    b = fill_bank(pe, "v")
                    o = b[:, :].rearrange("p (e s) -> p e s", s=64)[:, :, 0:CAP]
                    for t, (t0, n) in enumerate(TILES):
                        mm = pe.matmul(o, utok[0:n, t, k * P:(k + 1) * P], hot[0:n, t, 8 * half:8 * half + 8, 0:CAP],
                                       start=(t == 0), stop=(t == 2))
                    mm.then_inc(FV, 1)
            pe.wait_ge(operand_ready.sem, operand_ready.next())
            for p in range(PAIRS):
                for which in ("a", "v"):
                    b = [fill_bank(pe, which) for _ in CHUNKS]
                    for k0 in range(0, KD, 2):
                        W = [next_slot(pe, 2, FE) for _ in range(2)]
                        for k in range(2):
                            for ci, (c0, cw) in enumerate(CHUNKS):
                                for e in range(2):
                                    x = xs[:, k0 + k, (2 * p + e) * 64:(2 * p + e + 1) * 64]
                                    mm = pe.matmul(b[ci][64 * e:64 * e + 64, 0:cw], x, W[e][:, k, c0:c0 + cw],
                                                   start=(k0 + k == 0), stop=(k0 + k == KD - 1))
                                    last = k == 1 and ci == len(CHUNKS) - 1
                                    if last and e == 0:
                                        read_alone(mm)
                                if k0 + k == KD - 1:
                                    mm.then_inc(FA if which == "a" else FV, 1)
                        if k0 + 2 < KD:
                            read_alone(mm)
                        else:
                            read_with_bank(which)
                pe.wait_ge(operand_ready.sem, operand_ready.next())
                for f0, nf in KSPLIT:
                    b = fill_bank(pe, "a")
                    for f in range(nf):
                        mm = pe.transpose(b[:, f * P:(f + 1) * P], hid2[:, (f0 + f) * P:(f0 + f + 1) * P], C("ident"))
                    mm.then_inc(FA, 1)
                pe.wait_ge(aoperand_ready.sem, aoperand_ready.next())
                b = [fill_bank(pe, "v") for _ in range(2)]
                for f0, nf in KSPLIT:
                    W = [next_slot(pe, nf, D) for _ in range(2)]
                    for f in range(nf):
                        for c in range(2):
                            for e in range(2):
                                mm = pe.matmul(b[c][64 * e:64 * e + 64, :], hidT[:, f0 + f, 64 * e:64 * e + 64],
                                               W[e][:, f, c * 512:(c + 1) * 512], start=(f0 + f == 0), stop=(f0 + f == KE - 1))
                                if f == nf - 1 and c == 1 and e == 0:
                                    read_alone(mm)
                            if f0 + f == KE - 1:
                                mm.then_inc(FV, 1)
                    if f0 + nf < KE:
                        read_alone(mm)
                    else:
                        read_with_bank("v")
                if p % 4 == 3:
                    pe.wait_ge(operand_ready.sem, operand_ready.next())
                    for m in range(KD):
                        b = fill_bank(pe, "v")
                        for q in range(4):
                            mm = pe.matmul(b[:, 0:L], ys[:, q, m * P:(m + 1) * P], gT[:, p - 3 + q, :], start=(q == 0), stop=(q == 3))
                        mm.then_inc(FV, 1)

        def moe_vector(dve, l):
            gain_norm_vector(dve, "norm2_g_2", l)
            dve.memset(hot.rearrange("p t e s -> p (t e s)"), 0.0)
            dve.memset(ghot.rearrange("p e s -> p (e s)"), 0.0)
            dve.memset(xs.rearrange("p k s -> p (k s)"), 0.0)
            dve.memset(aff.rearrange("p t e -> p (t e)"), 0.0)
            dve.drain()
            b = take_bank(dve, "v")
            for t, (t0, n) in enumerate(TILES):
                ins = dve.tensor_copy(aff[0:n, t, :], b[0:n, t * NE:(t + 1) * NE])
            ins.then_inc(EV, 1)
            dve.drain()
            mx, sm = small[:, 52:55], small[:, 56:59]
            bc = lambda x: x.unsqueeze(2).to_broadcast([P, 3, NE])
            dve.tensor_reduce(mx, aff, AX.X, ALU.max)
            dve.drain()
            dve.tensor_tensor(aff, aff, bc(mx), ALU.subtract)
            dve.drain().then_inc(for_scalar.sem, 1)
            dve.wait_ge(from_scalar.sem, from_scalar.next())
            dve.tensor_reduce(sm, aff, AX.X, ALU.add)
            dve.drain()
            dve.reciprocal(sm, sm)
            dve.drain()
            dve.tensor_tensor(aff, aff, bc(sm), ALU.mult)
            dve.drain().then_inc(operand_ready.sem, 1)
            b = take_bank(dve, "v")
            w = work[0:NE, :]
            dve.tensor_copy(w, b[0:NE, 0:L]).then_inc(EV, 1)
            dve.drain()
            for i in range(0, CAP, 8):
                dve.max(out=top8[0:NE, :], in_=w)
                dve.drain()
                if CAP - i < 8:
                    dve.memset(top8[0:NE, CAP - i:8], -1.0)
                    dve.drain()
                dve.match_replace(out=w, in_to_replace=top8[0:NE, :], in_values=w, imm_value=-1.0)
                dve.drain()
            dve.tensor_scalar(w, w, 0.0, None, ALU.is_lt)
            dve.drain().then_inc(operand_ready.sem, 1)
            b = take_bank(dve, "v")
            for t, (t0, n) in enumerate(TILES):
                ins = dve.tensor_copy(mask[0:n, t, :], b[0:n, t * NE:(t + 1) * NE])
            ins.then_inc(EV, 1)
            dve.drain().then_inc(operand_ready.sem, 1)
            b = take_bank(dve, "v")
            for t, (t0, n) in enumerate(TILES):
                ins = dve.scalar_tensor_tensor(out=cum[0:n, t, :], in0=mask[0:n, t, :], scalar=-1000.0,
                                               in1=b[0:n, t * NE:(t + 1) * NE], op0=ALU.mult, op1=ALU.add)
            ins.then_inc(EV, 1)
            dve.drain()
            for t, (t0, n) in enumerate(TILES):
                dve.tensor_scalar(cum[0:n, t, :], cum[0:n, t, :], 1000.0, None, ALU.add)
            dve.drain()
            for t, (t0, n) in enumerate(TILES):
                if t:
                    pass
                ht = hot[0:n, t, :, 0:CAP]
                dve.tensor_tensor(ht, C("slot_no")[0:n, :].unsqueeze(1).to_broadcast([n, NE, CAP]),
                                  cum[0:n, t, :].unsqueeze(2).to_broadcast([n, NE, CAP]), ALU.is_equal)
                dve.drain()
                dve.tensor_tensor(ghot[0:n, :, 0:CAP], ht, aff[0:n, t, :].unsqueeze(2).to_broadcast([n, NE, CAP]), ALU.mult)
                dve.drain().then_inc(operand_ready.sem, 1)
                for half in range(2):
                    b = take_bank(dve, "v")
                    dve.tensor_copy(gT[:, 4 * half:4 * half + 4, t0:t0 + n],
                                    b[:, :].rearrange("p (q t) -> p q t", q=4)[:, :, 0:n]).then_inc(EV, 1)
            for k in range(KD):
                for half in range(2):
                    b = take_bank(dve, "v")
                    dve.tensor_copy(xs[:, k, 512 * half:512 * half + 512].rearrange("p (e s) -> p e s", s=64)[:, :, 0:CAP],
                                    b[:, :].rearrange("p (e s) -> p e s", s=64)[:, :, 0:CAP]).then_inc(EV, 1)
            dve.drain().then_inc(operand_ready.sem, 1)
            for p in range(PAIRS):
                for c0, cw in CHUNKS:
                    dve.wait_ge(silu_ready.sem, silu_ready.next())
                    b = take_bank(dve, "v")
                    dve.tensor_tensor(hid2[:, c0:c0 + cw], hs[:, c0:c0 + cw], b[:, 0:cw], ALU.mult).then_inc(EV, 1)
                dve.drain().then_inc(operand_ready.sem, 1)
                for c in range(2):
                    b = take_bank(dve, "v")
                    dve.tensor_copy(ys[:, p % 4, c * 512:(c + 1) * 512], b[:, :]).then_inc(EV, 1)
                if p % 4 == 3:
                    dve.drain().then_inc(operand_ready.sem, 1)
                    for m in range(KD):
                        b = take_bank(dve, "v")
                        dve.tensor_tensor(X[:, m, :], X[:, m, :], b[:, 0:L], ALU.add).then_inc(EV, 1)
                        dve.drain()

        def moe_scalar(act):
            norm_scalar(act, X[:, :, :], KD, L)
            for t, (t0, n) in enumerate(TILES):
                for half in range(2):
                    b = take_bank(act, "a")
                    act.activation(utok[0:n, t, 512 * half:512 * half + 512], b[0:n, :], ACT.Copy).then_inc(EA, 1)
            act.drain().then_inc(aoperand_ready.sem, 1)
            act.wait_ge(for_scalar.sem, for_scalar.next())
            act.activation(aff, aff, ACT.Exp).then_inc(from_scalar.sem, 1)
            for p in range(PAIRS):
                for c0, cw in CHUNKS:
                    b = take_bank(act, "a")
                    act.activation(hs[:, c0:c0 + cw], b[:, 0:cw], ACT.Silu).then_inc(EA, 1)
                    act.drain().then_inc(silu_ready.sem, 1)
                for f0, nf in KSPLIT:
                    b = take_bank(act, "a")
                    act.activation(hidT[:, f0:f0 + nf, :], b[:, 0:nf * P].rearrange("p (f s) -> p f s", s=P), ACT.Copy)\
                        .then_inc(EA, 1)
                act.drain().then_inc(aoperand_ready.sem, 1)

        def make_plan():
            ada_plan()
            project_plan(A["ab_w_in"][0], 3072, KD)
            project_plan(A["ab_w_out"][0], D, KD)
            ffn_plan(0)
            odd_plan()
            ffn_plan(1)
            for l in range(DEPTH):
                second_in_plan(l)
                rwkv_plan(l)
                project_plan(A["w_out_2"][l], D, KD)
                moe_plan(l)
        make_plan()

        block = ctx.enter_context(nc.Block())

        def guarded(f):
            try:
                f()
            except Stop:
                pass

        @block.tensor
        def _(pe):
            def prog():
                ada_tensor(pe)
                end_phase(pe, "pe")
                bias_tensor(pe)
                end_phase(pe, "pe")
                norm_tensor(pe, KD, SEQ)
                pe.wait_ge(operand_ready.sem, operand_ready.next())
                project_tensor(pe, 3072, KD, hrhs(SEQ), SEQ)
                turn_values_tensor(pe, 8)
                pe.wait_ge(aoperand_ready.sem, aoperand_ready.next())
                attend_tensor(pe, 16, head_rows(att_q), head_rows(att_k),
                              lambda h, t: att_v[:, t, h * HD:(h + 1) * HD])
                pe.wait_ge(operand_ready.sem, operand_ready.next())
                project_tensor(pe, D, KD, lambda k: att_q[:, k, :], SEQ)
                norm_tensor(pe, KD, SEQ)
                end_phase(pe, "pe")
                norm_tensor(pe, KD, SEQ)
                ffn_tensor(pe)
                norm_tensor(pe, KD, SEQ)
                end_phase(pe, "pe")
                norm_tensor(pe, KD, SEQ)
                odd_tensor(pe)
                norm_tensor(pe, KD, SEQ)
                end_phase(pe, "pe")
                norm_tensor(pe, KD, SEQ)
                ffn_tensor(pe)
                norm_tensor(pe, KD, SEQ)
                end_phase(pe, "pe")
                for l in range(DEPTH):
                    second_in_tensor(pe)
                    end_phase(pe, "pe")
                    diff_tensor(pe)
                    end_phase(pe, "pe")
                    gla_tensor(pe, l)
                    end_phase(pe, "pe")
                    rwkv_tensor(pe, l)
                    end_phase(pe, "pe")
                    mix_out_tensor(pe)
                    end_phase(pe, "pe")
                    moe_tensor(pe)
                    end_phase(pe, "pe")
                norm_tensor(pe, KD, L)
                end_phase(pe, "pe")
            guarded(prog)

        @block.vector
        def _(dve):
            def prog():
                ada_vector(dve)
                end_phase(dve, "dve")
                bias_vector(dve)
                end_phase(dve, "dve")
                pre_norm_vector(dve, 0, "mix_pre_g", 0, 1)
                project_vector(dve, 3072, even_put(dve))
                dve.drain().then_inc(operand_ready.sem, 1)
                attend_vector(dve, 16, 0.125, lambda h: att_b[:, h, :], head_rows(att_q))
                dve.drain().then_inc(operand_ready.sem, 1)
                project_vector(dve, D, lambda m, rows, b: dve.tensor_copy(H[:, m, 0:SEQ], b[:, 0:SEQ]))
                dve.drain().then_inc(dve_done_y.sem, 1)
                post_norm_vector(dve, 0, "mix_post_g", 2)
                end_phase(dve, "dve")
                pre_norm_vector(dve, 0, "ffn_pre_g", 3, 4)
                ffn_first[0] = ntake["v"]
                ffn_vector(dve, 0)
                post_norm_vector(dve, 0, "ffn_post_g", 5)
                end_phase(dve, "dve")
                pre_norm_vector(dve, 1, "mix_pre_g", 0, 1)
                odd_vector(dve)
                post_norm_vector(dve, 1, "mix_post_g", 2)
                end_phase(dve, "dve")
                pre_norm_vector(dve, 1, "ffn_pre_g", 3, 4)
                ffn_first[1] = ntake["v"]
                ffn_vector(dve, 1)
                post_norm_vector(dve, 1, "ffn_post_g", 5)
                end_phase(dve, "dve")
                for l in range(DEPTH):
                    second_in_vector(dve, l)
                    end_phase(dve, "dve")
                    diff_vector(dve, l)
                    end_phase(dve, "dve")
                    gla_vector(dve, l)
                    end_phase(dve, "dve")
                    rwkv_vector(dve, l)
                    end_phase(dve, "dve")
                    mix_out_vector(dve)
                    end_phase(dve, "dve")
                    moe_vector(dve, l)
                    end_phase(dve, "dve")
                gain_norm_vector(dve, "final_g_2", 0)
                end_phase(dve, "dve")
            guarded(prog)

        @block.scalar
        def _(act):
            def prog():
                ada_scalar(act)
                end_phase(act, "act")
                end_phase(act, "act")
                norm_scalar(act, XB, KD, SEQ)
                turn_values_scalar(act, 8)
                attend_scalar(act, 16)
                act.wait_ge(dve_done_y.sem, dve_done_y.next())
                norm_scalar(act, H[:, :, 0:SEQ], KD, SEQ)
                end_phase(act, "act")
                norm_scalar(act, XB, KD, SEQ)
                ffn_scalar(act, 0)
                act.wait_ge(dve_done_y.sem, dve_done_y.next())
                norm_scalar(act, H[:, :, 0:SEQ], KD, SEQ)
                end_phase(act, "act")
                norm_scalar(act, XB, KD, SEQ)
                odd_scalar(act)
                act.wait_ge(dve_done_y.sem, dve_done_y.next())
                norm_scalar(act, H[:, :, 0:SEQ], KD, SEQ)
                end_phase(act, "act")
                norm_scalar(act, XB, KD, SEQ)
                ffn_scalar(act, 1)
                act.wait_ge(dve_done_y.sem, dve_done_y.next())
                norm_scalar(act, H[:, :, 0:SEQ], KD, SEQ)
                end_phase(act, "act")
                for l in range(DEPTH):
                    norm_scalar(act, X[:, :, :], KD, L)
                    end_phase(act, "act")
                    diff_scalar(act)
                    end_phase(act, "act")
                    gla_scalar(act)
                    end_phase(act, "act")
                    rwkv_scalar(act)
                    end_phase(act, "act")
                    pass
                    end_phase(act, "act")
                    moe_scalar(act)
                    end_phase(act, "act")
                norm_scalar(act, X[:, :, :], KD, L)
                end_phase(act, "act")
            guarded(prog)

        @block.gpsimd
        def _(pool):
            def prog():
                end_phase(pool, "pool")
                bias_pool(pool)
                for _ in range(5 + 6 * DEPTH + 1):
                    end_phase(pool, "pool")
            guarded(prog)

        @block.sync
        def _(sp):
            sp.dma_start(cst[:, :], A["consts"]).then_inc(loaded.sem, 16)
            sp.dma_start(vec[:, :], A["vectors"]).then_inc(loaded.sem, 16)
            sp.dma_start(X[:, :, META:L], A["xt"]).then_inc(loaded.sem, 16)
            sp.dma_start(X[:, :, 0:META], A["metat"]).then_inc(loaded.sem, 16)
            for i, (src, nk, w) in enumerate(plan[:nslot[0]]):
                if i >= NSLOT:
                    sp.wait_ge(*slot_read[i - NSLOT])
                sp.dma_start(ring[:, i % NSLOT, 0:nk * w].rearrange("p (k n) -> p k n", k=nk), src)\
                    .then_inc(slot_filled[i % NSLOT].sem, 16)
            sp.wait_ge(phase_end, 4 * ends["dve"])
            src = H if stop is None else X
            if dump == "H":
                src = H
            if dump and dump.startswith("arena"):
                a0, nn, tt = [int(v) for v in dump[5:].split(",")]
                sp.dma_start(out[:, 0:nn, 0:tt], view(a0, nn, tt)).then_inc(stored.sem, 16)
                sp.wait_ge(stored.sem, 16)
                return
            sp.dma_start(out, src[:, :, :]).then_inc(stored.sem, 16)
            sp.wait_ge(stored.sem, 16)


SHARED = ["ada_w", "ab_w_in", "ab_w_out", "cd_w_in", "mla_w_uq", "mla_w_ukv", "cd_w_out", "ffn_w_up", "ffn_w_down",
          "w_in_2", "rw_w_up_2", "rw_a_up_2", "rw_g_up_2", "w_out_2", "router_2", "e_w1_2", "e_w3_2", "e_w2_2"]


def kernel(_stop=None, _dump=None, **inputs):
    import concourse.bacc as _bacc
    from concourse.bass_utils import run_bass_kernel_spmd as _run

    nc = _bacc.Bacc("TRN2", target_bir_lowering=False, num_devices=1)
    consts, cat = pack(shape_constants())
    vectors, vat = pack(vector_parts(inputs))
    arrays = {"consts": consts, "vectors": vectors}
    x = np.asarray(inputs["x"])[0]
    arrays["xt"] = np.ascontiguousarray(x.T.reshape(KD, P, SEQ).transpose(1, 0, 2))
    meta = np.asarray(inputs["meta_2"])
    arrays["metat"] = np.ascontiguousarray(meta.T.reshape(KD, P, META).transpose(1, 0, 2))
    for n in SHARED:
        arrays[n] = np.ascontiguousarray(inputs[n])
    A = {n: nc.dram_tensor(f"in_{n}", a.shape, FP32, kind="ExternalInput").ap() for n, a in arrays.items()}
    out = nc.dram_tensor("out_0", (P, KD, L), FP32, kind="ExternalOutput").ap()
    build(nc, A, cat, vat, out, _stop, _dump)
    r = _run(nc, [{f"in_{n}": a for n, a in arrays.items()}], core_ids=[0])
    got = r.results[0]["out_0"]
    return np.ascontiguousarray(got[:, :, META:L].transpose(2, 1, 0).reshape(1, SEQ, D))
```

```python
import concourse.bass as bass
from concourse import mybir
from contextlib import ExitStack
import math
import numpy as np

FP32 = mybir.dt.float32
ALU = mybir.AluOpType
ACT = mybir.ActivationFunctionType
AX = mybir.AxisListType

P = 128
D = 1024
KD = D // P
SEQ = 256
META = 16
L = SEQ + META
TILES = ((0, 128), (128, 128), (256, 16))
EPS = 1e-6
NEG = -1e30
DEPTH = 2
F1 = 2816
KF = F1 // P
HD = 64
BUCKETS = 32
SLOT = 4096
NSLOT = 5
RANK = 256
SPAN = 2 * SEQ - 1


class Count:

    def __init__(self, sem):
        self.sem, self.read = sem, {}

    def next(self, who="", n=1):
        self.read[who] = self.read.get(who, 0) + n
        return self.read[who]



def t5_bucket(dist):
    exact = BUCKETS // 2
    d = np.maximum(dist, 0)
    f = np.maximum(d, exact).astype(np.float32)
    large = exact + (np.log(f / np.float32(exact)) / np.float32(math.log(2048 / exact))
                     * np.float32(BUCKETS - exact)).astype(np.int32)
    return np.where(d < exact, d, np.minimum(large, BUCKETS - 1))


def shape_constants():
    c = {}
    i = np.arange(P)
    c["ident"] = np.eye(P)
    c["ones"] = np.ones((P, P))
    c["ones64"] = (i[:, None] // 64 == i[None, :] // 64).astype(float)
    pos = np.arange(SEQ, dtype=np.float32)
    inv = (1.0 / (np.float32(10000.0) ** (np.arange(0, 32, 2, dtype=np.float32) / np.float32(32)))).astype(np.float32)
    ang = pos[None, :] * inv[:, None]
    c["cos_mla"] = np.concatenate([np.ones((64, SEQ)), np.cos(ang), np.cos(ang)])
    c["sin_mla"] = np.concatenate([np.zeros((64, SEQ)), np.sin(ang), np.sin(ang)])
    rot = np.zeros((96, 96))
    for r in range(16):
        rot[80 + r, 64 + r] = -1.0
        rot[64 + r, 80 + r] = 1.0
    c["rot_mla"] = rot
    inv = (np.float32(10000.0) ** (-np.arange(32, dtype=np.float32) / np.float32(32))).astype(np.float32)
    ang = np.arange(L, dtype=np.float32)[None, :] * inv[:, None]
    c["cos_diff"] = np.tile(np.cos(ang), (4, 1))
    c["sin_diff"] = np.tile(np.sin(ang), (4, 1))
    rot = np.zeros((P, P))
    for g in (0, 64):
        for r in range(32):
            rot[g + 32 + r, g + r] = -1.0
            rot[g + r, g + 32 + r] = 1.0
    c["rot_diff"] = rot
    q, k = i[:, None], np.arange(SEQ)[None, :]
    c["causal"] = np.concatenate([np.where(k <= q + 128, 0.0, NEG), np.where(k <= q, 0.0, NEG)], axis=1)
    dist = SEQ - 1 - np.arange(SPAN)
    hot = (t5_bucket(dist)[None, :] == np.arange(BUCKETS)[:, None]) & (dist >= 0)
    times = np.zeros(SPAN)
    for window, dil in ((128, 1), (512, 4), (2048, 16)):
        times += (dist >= 0) & (dist <= window) & (dist % dil == 0)
    c["hot_moba"] = np.concatenate([hot, np.where(dist >= 0, 0.0, NEG)[None, :]])
    c["hot_dil"] = np.concatenate([hot, np.where(times > 0, np.log(np.maximum(times, 1)), NEG)[None, :]])
    q = np.arange(SEQ)[None, :]
    c["strict"] = np.concatenate([i[:, None] < q, i[:, None] + 128 < q], axis=1).astype(float)
    c["later"] = (i[:, None] >= i[None, :]).astype(float)
    c["before"] = (i[:, None] < i[None, :]).astype(float)
    c["slot_no"] = np.tile(np.arange(34)[None, :], (P, 1))
    same = i[:, None] // 16 == i[None, :] // 16
    s, t = i[:, None], i[None, :]
    c["lt_f"], c["lt_b"] = (same & (s < t)).astype(float), (same & (s > t)).astype(float)
    c["le_fb"] = np.concatenate([same & (s <= t), same & (s >= t)], axis=1).astype(float)
    c["half_of"] = (i[:, None] // 16 % 2 == np.arange(2)[None, :]).astype(float)
    c["chunk_of"] = (i[:, None] // 16 == np.arange(8)[None, :]).astype(float)
    t = np.arange(L)
    c["go_f"] = np.tile((t % 16 != 0).astype(float)[None, :], (P, 1))
    c["go_b"] = np.tile((t % 16 != 15).astype(float)[None, :], (P, 1))
    return {k: np.asarray(v, np.float32) for k, v in c.items()}


def pack(parts):
    at, n = {}, 0
    for name, a in parts.items():
        at[name] = (n, a.shape[1], a.shape[0])
        n += a.shape[1]
    out = np.zeros((P, n), np.float32)
    for name, a in parts.items():
        out[:a.shape[0], at[name][0]:at[name][0] + a.shape[1]] = a
    return out, at


def vector_parts(w):
    def cols(a):
        a = np.asarray(a)
        a = a.reshape(-1, a.shape[-1])
        return a.reshape(a.shape[0] * (a.shape[1] // P), P).T
    parts = {"c": cols(w["c"]), "ada_b": cols(w["ada_b"])}
    for n in ("mix_pre_g", "mix_post_g", "ffn_pre_g", "ffn_post_g", "mla_q_norm_g", "mla_kv_norm_g",
              "ffn_conv_w", "ffn_conv_b", "norm1_g_2", "rw_shift_2", "rw_w0_2", "rw_a0_2", "rw_k_k_2",
              "rw_k_a_2", "rw_r_k_2", "rw_gn_g_2", "rw_gn_b_2", "df_subln_g_2", "gl_gate_b_2", "norm2_g_2",
              "final_g_2"):
        parts[n] = cols(w[n])
    g = np.asarray(w["gl_norm_g_2"])
    parts["gl_norm_g_2"] = np.concatenate([g, g], axis=1).T
    lam = np.asarray(w["df_lam_2"]).reshape(DEPTH * 4, HD).T
    parts["df_lam_2"] = lam
    table = np.asarray(w["rel_bias"]).T
    parts["rel_bias"] = table
    up = np.asarray(w["gl_gate_up_2"])
    gate = np.zeros((32, DEPTH * 2 * P), np.float32)
    for l in range(DEPTH):
        for d in range(2):
            gate[16 * d:16 * d + 16, (2 * l + d) * P:(2 * l + d + 1) * P] = up[l, d]
    parts["gl_gate_up_2"] = gate
    return parts


def build(nc, A, cat, vat, out, stop=None, dump=None):
    ctx = ExitStack()
    with ctx:
        def sb(name, shape):
            return ctx.enter_context(nc.sbuf_tensor(name, shape, FP32))

        def sem(name):
            return ctx.enter_context(nc.semaphore(name))

        def signal(name):
            return Count(sem(name))

        X = sb("residual", [P, KD, L])
        H = sb("normed", [P, KD, L])
        S = sb("scratch", [P, KD, L])
        ring = sb("weight_ring", [P, NSLOT, SLOT])
        ncst = A["consts"].shape[1]
        nvec = A["vectors"].shape[1]
        cst = sb("constants", [P, ncst])
        vec = sb("vectors", [P, nvec])
        mod = sb("modulation", [P, DEPTH, 6 * KD])
        gain = sb("gain", [P, 2, KD])
        rstd = sb("rstd", [P, L])
        cond = sb("cond", [P, KD, 32])
        small = sb("small", [P, 64])
        AN = (nc.sbuf_bytes_remaining if not callable(nc.sbuf_bytes_remaining) else nc.sbuf_bytes_remaining()) // 4 - 64

        arena = sb("arena", [P, AN])
        banks = [ctx.enter_context(nc.psum_tensor(f"bank{i}", [P, 512], FP32)) for i in range(8)]
        scratch = nc.dram_tensor("bias_rows", (16, P, 512), FP32, kind="Internal").ap()

        cat["le_f"] = (cat["le_fb"][0], P, P)
        cat["le_b"] = (cat["le_fb"][0] + P, P, P)

        def C(name, rows=None):
            a, n, r = cat[name]
            return cst[0:(rows or r), a:a + n]

        def V(name, j=0, n=1, rows=P):
            a = vat[name][0]
            return vec[0:rows, a + j:a + j + n]

        def view(at, *shape):
            n = int(np.prod(shape))
            assert at + n <= AN, (at, n, AN)
            v = arena[:, at:at + n]
            if len(shape) == 2:
                v = v.rearrange("p (a b) -> p a b", a=shape[0])
            if len(shape) == 3:
                v = v.rearrange("p (a b c) -> p a b c", a=shape[0], b=shape[1])
            return v

        loaded = signal("loaded")
        phase_end = sem("phase_end")
        slot_filled = [signal(f"slot{i}_filled") for i in range(NSLOT)]
        slot_used = signal("slot_used")
        vbank_filled, vbank_emptied = signal("vbank_filled"), signal("vbank_emptied")
        abank_filled, abank_emptied = signal("abank_filled"), signal("abank_emptied")
        squares_ready = signal("squares_ready")
        inv_ready = signal("inv_ready")
        rstd_ready = signal("rstd_ready")
        operand_ready = signal("operand_ready")
        aoperand_ready = signal("aoperand_ready")
        logits_ready = signal("logits_ready")
        exp_ready = signal("exp_ready")
        act_ready = signal("act_ready")
        dve_ready = signal("dve_ready")
        rows_ready = signal("rows_ready")
        rows_stored = [signal(f"rows_stored{g}") for g in range(4)]
        bias_loaded = signal("bias_loaded")
        stored = signal("stored")
        small_loaded = signal("small_loaded")
        pool_ready = signal("pool_ready")

        for_scalar = signal("for_scalar")
        from_scalar = signal("from_scalar")

        ends = {}

        class Stop(Exception):
            pass

        def end_phase(eng, name):
            ends[name] = ends.get(name, 0) + 1
            eng.drain().then_inc(phase_end, 1)
            eng.wait_ge(phase_end, 4 * ends[name])
            if ends[name] == stop:
                raise Stop

        plan = []

        def load_plan(W, c0, w, k0, nk):
            plan.append((W[k0 * P:(k0 + nk) * P, c0:c0 + w].rearrange("(k p) n -> p k n", p=P), nk, w))

        nslot = [0]
        slot_read = {}
        open_slots = []

        def read_with_bank(which="v", at=0):
            slot_read[open_slots.pop(at)] = ((vbank_filled if which == "v" else abank_filled).sem, nfill[which])

        def read_alone(mm):
            mm.then_inc(slot_used.sem, 1)
            slot_read[open_slots.pop(0)] = (slot_used.sem, slot_used.next("pe"))

        def next_slot(pe, nk, w):
            i = nslot[0]
            nslot[0] += 1
            open_slots.append(i)
            assert plan[i][1:] == (nk, w), (i, plan[i][1:], nk, w)
            pe.wait_ge(slot_filled[i % NSLOT].sem, 16 * (i // NSLOT + 1))
            return ring[:, i % NSLOT, 0:nk * w].rearrange("p (k n) -> p k n", k=nk)

        nfill = {"v": 0, "a": 0}

        def fill_bank(pe, which):
            i = nfill[which]
            nfill[which] += 1
            if i >= 4:
                pe.wait_ge((vbank_emptied if which == "v" else abank_emptied).sem, i - 3)
            return banks[(i % 4) + (4 if which == "a" else 0)]

        ntake = {"v": 0, "a": 0}

        def take_bank(eng, which):
            i = ntake[which]
            ntake[which] += 1
            eng.wait_ge((vbank_filled if which == "v" else abank_filled).sem, i + 1)
            return banks[(i % 4) + (4 if which == "a" else 0)]

        FV, EV = vbank_filled.sem, vbank_emptied.sem
        FA, EA = abank_filled.sem, abank_emptied.sem

        def norm_scalar(act, src, nk, T):
            act.activation(S[:, 0:nk, 0:T], src, ACT.Square).then_inc(squares_ready.sem, 1)
            act.wait_ge(inv_ready.sem, inv_ready.next())
            act.activation(rstd[:, 0:T], rstd[:, 0:T], ACT.Sqrt).then_inc(rstd_ready.sem, 1)

        def norm_tensor(pe, nk, T, ones=None):
            pe.wait_ge(squares_ready.sem, squares_ready.next())
            b = fill_bank(pe, "v")
            for k in range(nk):
                mm = pe.matmul(b[:, 0:T], ones if ones is not None else C("ones"), S[:, k, 0:T], start=(k == 0), stop=(k == nk - 1))
            mm.then_inc(FV, 1)

        def norm_vector(dve, width, T, eps=EPS):
            b = take_bank(dve, "v")
            dve.tensor_scalar(rstd[:, 0:T], b[:, 0:T], 1.0 / width, eps, ALU.mult, ALU.add).then_inc(EV, 1)
            dve.drain()
            dve.reciprocal(rstd[:, 0:T], rstd[:, 0:T]).then_inc(inv_ready.sem, 1)
            dve.wait_ge(rstd_ready.sem, rstd_ready.next())

        def groups(width):
            return [(g, min(512, width - g)) for g in range(0, width, 512)]

        def project_plan(W, width, nk, first=0):
            for g, w in groups(width):
                for k0 in range(0, nk, KD):
                    load_plan(W, first + g, w, k0, min(KD, nk - k0))

        def project_tensor(pe, width, nk, rhs, T):
            for g, w in groups(width):
                tiles = [(m, min(P, w - m)) for m in range(0, w, P)]
                b = [None] * len(tiles)
                for k0 in range(0, nk, KD):
                    n = min(KD, nk - k0)
                    W = next_slot(pe, n, w)
                    for i, (m, mw) in enumerate(tiles):
                        if k0 == 0:
                            b[i] = fill_bank(pe, "v")
                        for k in range(k0, k0 + n):
                            mm = pe.matmul(b[i][0:mw, 0:T], W[:, k - k0, m:m + mw], rhs(k),
                                           start=(k == 0), stop=(k == nk - 1))
                        if k0 + n == nk:
                            mm.then_inc(FV, 1)
                    if k0 + n == nk:
                        read_with_bank()
                    else:
                        read_alone(mm)

        def project_vector(dve, width, put):
            for m in range(-(-width // P)):
                b = take_bank(dve, "v")
                put(m, min(P, width - m * P), b).then_inc(EV, 1)

        XB = X[:, :, META:L]

        flat = S[:, :, :].rearrange("p a b -> p (a b)")
        arow = [flat[:, 512 * i:512 * (i + 1)] for i in range(2)]
        AG = 6 * D // 512
        astep = {"pe": 0, "dve": 0}

        def ada_plan(i):
            load_plan(A["ada_w"][i // AG], (i % AG) * 512, 512, 0, KD)

        def ada_tensor(pe, more=True, first=False):
            i = astep["pe"]
            if more:
                astep["pe"] += 1
                W = next_slot(pe, KD, 512)
                b = fill_bank(pe, "v")
                for k in range(KD):
                    g = k % 4
                    mm = pe.matmul(b[32 * g:32 * g + 32, :], cond[:, k, :], W[:, k, :], start=(k < 4), stop=(k >= 4),
                                   tile_position=(0, 32 * g))
                mm.then_inc(FV, 1)
                read_with_bank("v", -1)
            if not first:
                pe.wait_ge(row_ready.sem, row_ready.next())
                b = fill_bank(pe, "v")
                for j in range(4):
                    mm = pe.matmul(b[:, j:j + 1], arow[(i - 1) % 2][:, j * P:(j + 1) * P], C("ones")[:, 0:1], start=True, stop=True)
                mm.then_inc(FV, 1)

        def ada_vector(dve, more=True, first=False):
            i = astep["dve"]
            if more:
                astep["dve"] += 1
                b = take_bank(dve, "v")
                dve.tensor_copy(arow[i % 2], b[:, :]).then_inc(EV, 1)
                dve.drain().then_inc(row_ready.sem, 1)
            if not first:
                b = take_bank(dve, "v")
                l, g = divmod(i - 1, AG)
                dve.tensor_tensor(mod[:, l, 4 * g:4 * g + 4], b[:, 0:4], V("ada_b", l * 6 * KD + 4 * g, 4), ALU.add)\
                    .then_inc(EV, 1)

        row_ready = signal("row_ready")

        def start_tensor(pe):
            bias_tensor(pe)
            pe.wait_ge(aoperand_ready.sem, aoperand_ready.next())
            for i in range(4):
                ada_tensor(pe, first=(i == 0))
            ada_tensor(pe, more=False)

        def start_vector(dve):
            dve.wait_ge(loaded.sem, 16 * 4)
            dve.memset(cond[:, :, :], 0.0)
            dve.drain().then_inc(for_scalar.sem, 1)
            bias_vector(dve)
            for i in range(4):
                ada_vector(dve, first=(i == 0))
            ada_vector(dve, more=False)

        def start_scalar(act):
            act.wait_ge(for_scalar.sem, for_scalar.next())
            act.activation(cond[:, :, 0], V("c", 0, KD), ACT.Silu).then_inc(aoperand_ready.sem, 1)

        def modulation(l, what):
            return mod[:, l, what * KD:(what + 1) * KD]

        def pre_norm_vector(dve, l, g, shift, scale):
            dve.scalar_tensor_tensor(out=gain[:, 0, :], in0=modulation(l, scale), scalar=1.0,
                                     in1=V(g, l * KD, KD), op0=ALU.add, op1=ALU.mult)
            norm_vector(dve, D, SEQ)
            for k in range(KD):
                dve.tensor_tensor(S[:, k, 0:SEQ], XB[:, k, :], rstd[:, 0:SEQ], ALU.mult)
            dve.drain()
            for k in range(KD):
                ins = dve.tensor_scalar(H[:, k, 0:SEQ], S[:, k, 0:SEQ], gain[:, 0, k:k + 1],
                                        modulation(l, shift)[:, k:k + 1], ALU.mult, ALU.add)
            ins.then_inc(operand_ready.sem, 1)

        def post_norm_vector(dve, l, g, gate):
            dve.drain()
            dve.tensor_tensor(gain[:, 0, :], modulation(l, gate), V(g, l * KD, KD), ALU.mult)
            dve.wait_ge(squares_ready.sem, squares_ready.next("dve"))
            norm_vector(dve, D, SEQ)
            for k in range(KD):
                dve.tensor_tensor(H[:, k, 0:SEQ], H[:, k, 0:SEQ], rstd[:, 0:SEQ], ALU.mult)
            dve.drain()
            for k in range(KD):
                dve.scalar_tensor_tensor(out=XB[:, k, :], in0=H[:, k, 0:SEQ], scalar=gain[:, 0, k:k + 1],
                                         in1=XB[:, k, :], op0=ALU.mult, op1=ALU.add)

        hrhs = lambda T: (lambda k: H[:, k, 0:T])

        HALVES = (slice(0, SEQ), slice(SEQ, SEQ + P))

        def attend_tensor(pe, n, q, k, vtok, beside=None):
            for i in range(n + 3):
                if i < n:
                    b = fill_bank(pe, "v")
                    pe.matmul(b[:, HALVES[0]], q(i)[:, P:2 * P], k(i), start=True, stop=True)
                    pe.matmul(b[:, HALVES[1]], q(i)[:, 0:P], k(i)[:, 0:P], start=True, stop=True).then_inc(FV, 1)
                if 2 <= i < n + 2:
                    x = att_l[:, (i - 2) % 3, :]
                    pe.wait_ge(operand_ready.sem, operand_ready.next())
                    b = fill_bank(pe, "a")
                    for j, a in enumerate((SEQ, 0, P)):
                        mm = pe.transpose(b[:, j * P:(j + 1) * P], x[:, a:a + P], C("ident"))
                    mm.then_inc(FA, 1)
                if i >= 3:
                    h = i - 3
                    x = att_pt[:, h % 2, :]
                    pe.wait_ge(aoperand_ready.sem, aoperand_ready.next())
                    b = fill_bank(pe, "v")
                    r = slice(64 * (h % 2), 64 * (h % 2) + 64)
                    pe.matmul(b[r, 0:SEQ], vtok(h, 0), x[:, 0:SEQ], start=True, stop=False)
                    pe.matmul(b[r, P:SEQ], vtok(h, 1), x[:, SEQ:SEQ + P], start=False, stop=True).then_inc(FV, 1)
                if beside:
                    beside(i)

        def attend_vector(dve, n, scale, bias, put, beside=None):
            for i in range(n + 3):
                if i < n:
                    o = 8 * (i % 3)
                    x = att_l[:, i % 3, :]
                    b = take_bank(dve, "v")
                    dve.scalar_tensor_tensor(out=x, in0=b[:, 0:SEQ + P], scalar=scale, in1=bias(i)[:, 0:SEQ + P],
                                             op0=ALU.mult, op1=ALU.add).then_inc(EV, 1)
                    dve.drain()
                    for j, c in enumerate(HALVES):
                        dve.tensor_reduce(small[:, o + j:o + j + 1], x[:, c], AX.X, ALU.max)
                    dve.drain()
                    dve.tensor_scalar(small[:, o:o + 2], small[:, o:o + 2], -1.0, None, ALU.mult).then_inc(logits_ready.sem, 1)
                if 1 <= i <= n:
                    o = 8 * ((i - 1) % 3)
                    x = att_l[:, (i - 1) % 3, :]
                    dve.wait_ge(exp_ready.sem, exp_ready.next())
                    dve.reciprocal(small[:, o + 4:o + 6], small[:, o + 2:o + 4])
                    dve.drain()
                    for j, c in enumerate(HALVES):
                        ins = dve.tensor_scalar(x[:, c], x[:, c], small[:, o + 4 + j:o + 5 + j], None, ALU.mult)
                    ins.then_inc(operand_ready.sem, 1)
                if i >= 3:
                    h = i - 3
                    b = take_bank(dve, "v")
                    dve.tensor_copy(put(h), b[64 * (h % 2):64 * (h % 2) + 64, 0:SEQ]).then_inc(EV, 1)
                if beside:
                    beside(i)

        def attend_scalar(act, n):
            for i in range(n + 2):
                if i < n:
                    o = 8 * (i % 3)
                    act.wait_ge(logits_ready.sem, logits_ready.next())
                    for j, c in enumerate(HALVES):
                        x = att_l[:, i % 3, c]
                        ins = act.activation(x, x, ACT.Exp, bias=small[:, o + j:o + j + 1],
                                             accum_out=small[:, o + 2 + j:o + 3 + j])
                    ins.then_inc(exp_ready.sem, 1)
                if i >= 2:
                    b = take_bank(act, "a")
                    act.activation(att_pt[:, i % 2, :], b[:, 0:SEQ + P], ACT.Copy).then_inc(EA, 1)
                    act.drain().then_inc(aoperand_ready.sem, 1)

        def turn_values_tensor(pe, n):
            pe.wait_ge(operand_ready.sem, operand_ready.next())
            for m in range(n):
                b = fill_bank(pe, "a")
                for t in range(2):
                    mm = pe.transpose(b[:, t * P:(t + 1) * P], S[:, m, t * P:(t + 1) * P], C("ident"))
                mm.then_inc(FA, 1)

        def turn_values_scalar(act, n):
            for m in range(n):
                b = take_bank(act, "a")
                act.activation(att_v[:, :, m * P:(m + 1) * P], b[:, 0:2 * P].rearrange("p (t f) -> p t f", t=2),
                               ACT.Copy).then_inc(EA, 1)
            act.drain().then_inc(aoperand_ready.sem, 1)

        att_q = view(0, 8, SEQ)
        att_k = view(8 * SEQ, 8, SEQ)
        att_v = view(16 * SEQ, 2, D)
        att_l = view(24 * SEQ, 3, SEQ + P)
        att_pt = view(29 * SEQ, 2, SEQ + P)
        att_b = view(32 * SEQ, 16, 2 * SEQ)
        table = sb("bias_table", [BUCKETS + 1, 16])

        def bias_vector(dve):
            dve.memset(table[:, :], 1.0)
            dve.drain()
            dve.tensor_copy(table[0:BUCKETS, :], V("rel_bias", 0, 16, rows=BUCKETS)).then_inc(operand_ready.sem, 1)
            for h in range(16):
                b = take_bank(dve, "v")
                dve.tensor_copy(att_b[:, h, 0:SPAN], b[:, 0:SPAN]).then_inc(EV, 1)
                if h % 4 == 3:
                    dve.drain().then_inc(rows_ready.sem, 1)

        def bias_tensor(pe):
            pe.wait_ge(operand_ready.sem, operand_ready.next())
            for h in range(16):
                b = fill_bank(pe, "v")
                pe.matmul(b[:, 0:SPAN], table[:, h:h + 1].to_broadcast([BUCKETS + 1, P]),
                          C("hot_moba" if h < 8 else "hot_dil"), start=True, stop=True).then_inc(FV, 1)

        def bias_pool(pool):
            for g in range(4):
                pool.wait_ge(rows_ready.sem, rows_ready.next())
                pool.dma_start(scratch[4 * g:4 * g + 4, :, 0:SPAN].rearrange("h p s -> p h s"),
                               att_b[:, 4 * g:4 * g + 4, 0:SPAN]).then_inc(rows_stored[g].sem, 16)
            for g in range(4):
                pool.wait_ge(rows_stored[g].sem, 16)
                for h in range(4 * g, 4 * g + 4):
                    skew = bass.AP(tensor=scratch.tensor, offset=scratch.offset + h * P * 512 + P - 1,
                                   ap=[[511, P], [P, 2], [1, SEQ]])
                    pool.dma_start(att_b[:, h, :].rearrange("p (j k) -> p j k", j=2), skew).then_inc(bias_loaded.sem, 16)
            pool.wait_ge(bias_loaded.sem, 16 * 16)

        def even_put(dve):
            def put(m, rows, b):
                part, i = m // 4, m % 4
                half, kind = part // 3, part % 3
                if kind == 2:
                    return dve.tensor_copy(S[:, half * 4 + i, 0:SEQ], b[:, 0:SEQ])
                return dve.tensor_copy((att_q, att_k)[kind][:, half * 4 + i, :], b[:, 0:SEQ])
            return put

        def even_ada(step, eng):
            def beside(i):
                if i % 2 == 1 and i <= 15:
                    step(eng, first=(i == 1))
                if i == 17:
                    step(eng, more=False)
            return beside

        def head_rows(buf):
            return lambda h: buf[64 * (h % 2):64 * (h % 2) + 64, h // 2, :]

        hid = view(0, KF, SEQ)
        conv = view(KF * SEQ, 4, SEQ)

        def ffn_plan(l):
            for g, w in groups(F1):
                load_plan(A["ffn_w_up"][l], g, w, 0, KD)
                load_plan(A["ffn_w_up"][l], F1 + g, w, 0, KD)
                for i in range(g // P, (g + w) // P):
                    if l == 0 and ada_beside(i):
                        ada_plan(AG + sum(ada_beside(j) for j in range(i)))
            project_plan(A["ffn_w_down"][l], D, KF)

        def ada_beside(i):
            return i % 2 == 0 or i == KF - 1

        def ffn_tensor(pe, l):
            pe.wait_ge(operand_ready.sem, operand_ready.next())
            for g, w in groups(F1):
                W = [next_slot(pe, KD, w), next_slot(pe, KD, w)]
                for m in range(0, w, P):
                    for part in range(2):
                        b = fill_bank(pe, "v")
                        for k in range(KD):
                            mm = pe.matmul(b[:, 0:SEQ], W[part][:, k, m:m + P], H[:, k, 0:SEQ],
                                           start=(k == 0), stop=(k == KD - 1))
                        mm.then_inc(FV, 1)
                    if m + P == w:
                        read_with_bank()
                        read_with_bank()
                    if l == 0 and ada_beside((g + m) // P):
                        ada_tensor(pe, first=(g + m == 0))
            if l == 0:
                ada_tensor(pe, more=False)
            pe.wait_ge(operand_ready.sem, operand_ready.next())
            project_tensor(pe, D, KF, lambda k: hid[:, k, :], SEQ)

        def ffn_scalar(act, l):
            for i in range(KF):
                for part in range(2):
                    m = part * KF + i
                    n = ffn_taken[0]
                    ffn_taken[0] += 1
                    act.wait_ge(vbank_filled.sem, ntake_ffn(n))
                    if i >= 2:
                        act.wait_ge(dve_ready.sem, dve_ready_at(i, l))
                    act.activation(conv[:, 2 * (i % 2) + part, :], banks[(ntake_ffn(n) - 1) % 4][:, 0:SEQ], ACT.Identity,
                                   bias=V("ffn_conv_b", l * 44 + m),
                                   scale=V("ffn_conv_w", (l * 3 + 2) * 44 + m)).then_inc(act_ready.sem, 1)
                if i >= 1:
                    gelu_scalar(act, i - 1, l)
            gelu_scalar(act, KF - 1, l)

        def gelu_scalar(act, i, l):
            act.wait_ge(logits_ready.sem, logits_ready.next())
            act.activation(conv[:, 2 * (i % 2), :], conv[:, 2 * (i % 2), :], ACT.Gelu_apprx_tanh)\
                .then_inc(exp_ready.sem, 1)

        ffn_taken = [0]
        ffn_first = {}

        def ntake_ffn(n):
            l, j = divmod(n, 2 * KF)
            before = 0
            if l == 0:
                steps = sum(ada_beside(i) for i in range(j // 2))
                before = max(2 * steps - 1, 0)
            return ffn_first[l] + j + before + 1

        def dve_ready_at(i, l):
            return l * KF + i - 1

        def ffn_vector(dve, l):
            def product(i):
                dve.wait_ge(exp_ready.sem, exp_ready.next())
                dve.tensor_tensor(hid[:, i, :], conv[:, 2 * (i % 2), :], conv[:, 2 * (i % 2) + 1, :], ALU.mult)\
                    .then_inc(dve_ready.sem, 1)
            for i in range(KF):
                for part in range(2):
                    m = part * KF + i
                    b = take_bank(dve, "v")
                    c = conv[:, 2 * (i % 2) + part, :]
                    dve.wait_ge(act_ready.sem, act_ready.next())
                    dve.scalar_tensor_tensor(out=c[:, 1:SEQ], in0=b[:, 0:SEQ - 1], scalar=V("ffn_conv_w", (l * 3 + 1) * 44 + m),
                                             in1=c[:, 1:SEQ], op0=ALU.mult, op1=ALU.add)
                    dve.drain()
                    dve.scalar_tensor_tensor(out=c[:, 2:SEQ], in0=b[:, 0:SEQ - 2], scalar=V("ffn_conv_w", l * 3 * 44 + m),
                                             in1=c[:, 2:SEQ], op0=ALU.mult, op1=ALU.add).then_inc(EV, 1)
                dve.drain().then_inc(logits_ready.sem, 1)
                if i >= 1:
                    product(i - 1)
                if l == 0 and ada_beside(i):
                    ada_vector(dve, first=(i == 0))
            product(KF - 1)
            if l == 0:
                ada_vector(dve, more=False)
            dve.drain().then_inc(operand_ready.sem, 1)
            project_vector(dve, D, lambda m, rows, b: dve.tensor_copy(H[:, m, 0:SEQ], b[:, 0:SEQ]))
            dve.drain().then_inc(dve_done_y.sem, 1)

        dve_done_y = signal("y_ready")

        NR = 96
        cq = view(0, 4, SEQ)
        krope = view(4 * SEQ, SEQ)
        qfull = view(5 * SEQ, 8, SEQ)
        kfull = view(13 * SEQ, 8, SEQ)
        stick_q = view(64 * SEQ, 4, SEQ)
        odd_v = view(32 * SEQ, 2, D)
        stick_k = view(40 * SEQ, 4, SEQ)
        odd_o = view(44 * SEQ, 8, SEQ)
        stick_z = view(52 * SEQ, 3, 2 * SEQ)
        stick_t = view(58 * SEQ, 2, 2 * SEQ)
        rope_t = view(62 * SEQ, 2, SEQ)

        def odd_plan():
            W = A["cd_w_in"][0]
            load_plan(W, 0, 512, 0, KD)
            load_plan(W, 512, 32, 0, KD)
            for g in range(2):
                load_plan(A["mla_w_uq"][0], g * 4 * NR, 4 * NR, 0, 2)
            for g in range(2):
                load_plan(A["mla_w_ukv"][0], g * 512, 512, 0, 2)
            project_plan(W, 1536, KD, 544)
            project_plan(A["cd_w_out"][0], D, KD)

        def odd_tensor(pe):
            pe.wait_ge(operand_ready.sem, operand_ready.next())
            project_tensor(pe, 512, KD, hrhs(SEQ), SEQ)
            W = next_slot(pe, KD, 32)
            b = fill_bank(pe, "v")
            for k in range(KD):
                mm = pe.matmul(b[64:96, 0:SEQ], W[:, k, :], H[:, k, 0:SEQ], start=(k == 0), stop=(k == KD - 1))
            mm.then_inc(FV, 1)
            read_with_bank()
            pe.wait_ge(operand_ready.sem, operand_ready.next())
            b = fill_bank(pe, "v")
            pe.matmul(b[64:96, 0:SEQ], C("rot_mla")[64:96, 64:96], krope[64:96, :], start=True, stop=True).then_inc(FV, 1)
            norm_tensor(pe, 2, SEQ)
            norm_tensor(pe, 2, SEQ)
            pe.wait_ge(operand_ready.sem, operand_ready.next())
            for g in range(2):
                W = next_slot(pe, 2, 4 * NR)
                for h in range(4):
                    b = fill_bank(pe, "v")
                    for k in range(2):
                        mm = pe.matmul(b[0:NR, 0:SEQ], W[:, k, h * NR:(h + 1) * NR], cq[:, k, :], start=(k == 0), stop=(k == 1))
                    mm.then_inc(FV, 1)
                read_with_bank()
            pe.wait_ge(operand_ready.sem, operand_ready.next())
            for h in range(8):
                b = fill_bank(pe, "v")
                pe.matmul(b[0:NR, 0:SEQ], C("rot_mla"), qfull[0:NR, h, :], start=True, stop=True).then_inc(FV, 1)
            for g in range(2):
                W = next_slot(pe, 2, 512)
                W4 = W.rearrange("p k (h f) -> p k h f", h=4)
                for h in range(4):
                    b = fill_bank(pe, "v")
                    for k in range(2):
                        mm = pe.matmul(b[0:HD, 0:SEQ], W[:, k, h * P:h * P + HD], cq[:, 2 + k, :], start=(k == 0), stop=(k == 1))
                    mm.then_inc(FV, 1)
                for t in range(2):
                    b = fill_bank(pe, "v")
                    for k in range(2):
                        mm = pe.matmul(b[:, 0:SEQ].rearrange("p (h f) -> p h f", h=4), cq[:, 2 + k, t * P:(t + 1) * P],
                                       W4[:, k, :, HD:P], start=(k == 0), stop=(k == 1))
                    mm.then_inc(FV, 1)
                read_with_bank()
            project_tensor(pe, 1536, KD, hrhs(SEQ), SEQ)
            turn_values_tensor(pe, 4)
            pe.wait_ge(aoperand_ready.sem, aoperand_ready.next())
            attend_tensor(pe, 8, lambda h: qfull[0:NR, h, :], lambda h: kfull[0:NR, h, :],
                          lambda h, t: odd_v[:, t, h * HD:(h + 1) * HD])
            stick_tensor(pe)
            pe.wait_ge(operand_ready.sem, operand_ready.next())
            project_tensor(pe, D, KD, lambda k: odd_o[:, k, :], SEQ)

        def odd_vector(dve):
            project_vector(dve, 512, lambda m, rows, b: dve.tensor_copy(cq[:, m, :], b[:, 0:SEQ]))
            b = take_bank(dve, "v")
            r = slice(64, 96)
            dve.tensor_copy(krope[r, :], b[r, 0:SEQ]).then_inc(EV, 1)
            dve.drain().then_inc(operand_ready.sem, 1)
            b = take_bank(dve, "v")
            dve.tensor_tensor(rope_t[r, 0, :], b[r, 0:SEQ], C("sin_mla")[r, :], ALU.mult).then_inc(EV, 1)
            dve.tensor_tensor(krope[r, :], krope[r, :], C("cos_mla")[r, :], ALU.mult)
            dve.drain()
            for h in range(8):
                dve.tensor_tensor(kfull[r, h, :], krope[r, :], rope_t[r, 0, :], ALU.add)
            for part, g in ((0, "mla_q_norm_g"), (1, "mla_kv_norm_g")):
                dve.drain().then_inc(latent_ready.sem, 1)
                norm_vector(dve, RANK, SEQ)
                for k in range(2):
                    dve.scalar_tensor_tensor(out=cq[:, 2 * part + k, :], in0=cq[:, 2 * part + k, :], scalar=V(g, k),
                                             in1=rstd[:, 0:SEQ], op0=ALU.mult, op1=ALU.mult)
            dve.drain().then_inc(operand_ready.sem, 1)
            for h in range(8):
                b = take_bank(dve, "v")
                dve.tensor_copy(qfull[0:NR, h, :], b[0:NR, 0:SEQ]).then_inc(EV, 1)
            dve.drain().then_inc(operand_ready.sem, 1)
            for h in range(8):
                b = take_bank(dve, "v")
                t = rope_t[0:NR, h % 2, :]
                dve.tensor_tensor(t, b[0:NR, 0:SEQ], C("sin_mla"), ALU.mult).then_inc(EV, 1)
                dve.tensor_tensor(qfull[0:NR, h, :], qfull[0:NR, h, :], C("cos_mla"), ALU.mult)
                dve.drain()
                dve.tensor_tensor(qfull[0:NR, h, :], qfull[0:NR, h, :], t, ALU.add)
            for g in range(2):
                for h in range(4 * g, 4 * g + 4):
                    b = take_bank(dve, "v")
                    dve.tensor_copy(kfull[0:HD, h, :], b[0:HD, 0:SEQ]).then_inc(EV, 1)
                for t in range(2):
                    b = take_bank(dve, "v")
                    dve.tensor_copy(odd_v[:, t, g * SEQ:(g + 1) * SEQ], b[:, 0:SEQ]).then_inc(EV, 1)

            def put(m, rows, b):
                if m < 4:
                    return dve.tensor_scalar(stick_q[:, m, :], b[:, 0:SEQ], HD ** -0.5, None, ALU.mult)
                if m < 8:
                    return dve.tensor_copy(stick_k[:, m - 4, :], b[:, 0:SEQ])
                return dve.tensor_copy(S[:, m - 8, 0:SEQ], b[:, 0:SEQ])
            project_vector(dve, 1536, put)
            dve.drain().then_inc(operand_ready.sem, 1)
            attend_vector(dve, 8, NR ** -0.5, lambda h: C("causal"), head_rows(odd_o))
            stick_vector(dve)
            dve.drain().then_inc(operand_ready.sem, 1)
            project_vector(dve, D, lambda m, rows, b: dve.tensor_copy(H[:, m, 0:SEQ], b[:, 0:SEQ]))
            dve.drain().then_inc(dve_done_y.sem, 1)

        def odd_scalar(act):
            for part in range(2):
                act.wait_ge(latent_ready.sem, latent_ready.next())
                norm_scalar(act, cq[:, 2 * part:2 * part + 2, :], 2, SEQ)
            for m in range(4):
                b = take_bank(act, "a")
                act.activation(odd_v[:, :, 512 + m * P:512 + (m + 1) * P], b[:, 0:2 * P].rearrange("p (t f) -> p t f", t=2),
                               ACT.Copy).then_inc(EA, 1)
            act.drain().then_inc(aoperand_ready.sem, 1)
            attend_scalar(act, 8)
            stick_scalar(act)

        latent_ready = signal("latent_ready")
        score_ready = signal("score_ready")
        log_ready = signal("log_ready")
        rest_ready = signal("rest_ready")
        share_ready = signal("share_ready")

        def stick_tensor(pe):
            qh, kh = head_rows(stick_q), head_rows(stick_k)
            for i in range(8 + 2):
                if i < 8:
                    b = fill_bank(pe, "v")
                    for kt in range(2):
                        mm = pe.matmul(b[:, kt * SEQ:(kt + 1) * SEQ], kh(i)[:, kt * P:(kt + 1) * P], qh(i), start=True, stop=True)
                    mm.then_inc(FV, 1)
                if 1 <= i <= 8:
                    t = stick_t[:, (i - 1) % 2, :]
                    pe.wait_ge(operand_ready.sem, operand_ready.next())
                    b = fill_bank(pe, "v")
                    pe.matmul(b[:, 0:SEQ], C("later"), t[:, 0:SEQ], start=True, stop=False)
                    pe.matmul(b[:, 0:SEQ], C("ones"), t[:, SEQ:], start=False, stop=True)
                    pe.matmul(b[:, SEQ:], C("later"), t[:, SEQ:], start=True, stop=True).then_inc(FV, 1)
                if i >= 2:
                    h = i - 2
                    pe.wait_ge(operand_ready.sem, operand_ready.next())
                    b = fill_bank(pe, "v")
                    for kt in range(2):
                        mm = pe.matmul(b[64 * (h % 2):64 * (h % 2) + 64, 0:SEQ], odd_v[:, kt, 512 + h * HD:512 + (h + 1) * HD],
                                       stick_z[:, h % 3, kt * SEQ:(kt + 1) * SEQ], start=(kt == 0), stop=(kt == 1))
                    mm.then_inc(FV, 1)

        def stick_vector(dve):
            for i in range(8 + 2):
                if i < 8:
                    b = take_bank(dve, "v")
                    dve.tensor_tensor(stick_z[:, i % 3, :], b[:, :], C("strict"), ALU.mult).then_inc(EV, 1)
                    dve.drain().then_inc(score_ready.sem, 1)
                if 1 <= i <= 8:
                    t, z = stick_t[:, (i - 1) % 2, :], stick_z[:, (i - 1) % 3, :]
                    dve.wait_ge(log_ready.sem, log_ready.next())
                    dve.scalar_tensor_tensor(out=t, in0=z, scalar=0.0, in1=t, op0=ALU.max, op1=ALU.add)
                    dve.drain()
                    dve.tensor_tensor(t, t, C("strict"), ALU.mult).then_inc(operand_ready.sem, 1)
                if i >= 2:
                    z = stick_z[:, (i - 2) % 3, :]
                    dve.wait_ge(share_ready.sem, share_ready.next())
                    dve.tensor_tensor(z, z, C("strict"), ALU.mult).then_inc(operand_ready.sem, 1)
                if 1 <= i <= 8:
                    z = stick_z[:, (i - 1) % 3, :]
                    b = take_bank(dve, "v")
                    dve.tensor_tensor(z, z, b[:, :], ALU.subtract).then_inc(EV, 1)
                    dve.drain().then_inc(rest_ready.sem, 1)
                if i >= 2:
                    h = i - 2
                    b = take_bank(dve, "v")
                    dve.tensor_copy(odd_o[64 * (h % 2):64 * (h % 2) + 64, 4 + h // 2, :],
                                    b[64 * (h % 2):64 * (h % 2) + 64, 0:SEQ]).then_inc(EV, 1)

        def stick_scalar(act):
            for i in range(8 + 1):
                if i < 8:
                    t = stick_t[:, i % 2, :]
                    act.wait_ge(score_ready.sem, score_ready.next())
                    act.activation(t, stick_z[:, i % 3, :], ACT.Abs)
                    act.drain()
                    act.activation(t, t, ACT.Exp, scale=-1.0)
                    act.drain()
                    act.activation(t, t, ACT.Ln, bias=1.0).then_inc(log_ready.sem, 1)
                if i >= 1:
                    act.wait_ge(rest_ready.sem, rest_ready.next())
                    z = stick_z[:, (i - 1) % 3, :]
                    act.activation(z, z, ACT.Exp).then_inc(share_ready.sem, 1)

        Q = L
        NIN = A["w_in_2"].shape[2]
        MIN = -(-NIN // P)
        proj = view(0, MIN, L)
        A_T, B_T, C_T = 0, 9, 21
        CH = 16
        NCH = L // CH


        def gain_norm_vector(dve, g, l, n=KD):
            norm_vector(dve, D, L)
            for k in range(KD):
                dve.scalar_tensor_tensor(out=H[:, k, :], in0=X[:, k, :], scalar=V(g, l * KD + k), in1=rstd[:, :],
                                         op0=ALU.mult, op1=ALU.mult)
            dve.drain().then_inc(operand_ready.sem, 1)

        def second_in_plan(l):
            project_plan(A["w_in_2"][l], NIN, KD)

        def second_in_tensor(pe):
            norm_tensor(pe, KD, L)
            pe.wait_ge(operand_ready.sem, operand_ready.next())
            project_tensor(pe, NIN, KD, lambda k: H[:, k, :], L)

        def second_in_vector(dve, l):
            gain_norm_vector(dve, "norm1_g_2", l)
            project_vector(dve, NIN, lambda m, rows, b: dve.tensor_copy(proj[0:rows, m, :], b[0:rows, 0:L]))

        DB = MIN * Q
        diff_v = view(DB, 3, 512)
        diff_e = view(DB + 1536, 3, 2, L)
        diff_t = view(DB + 1536 + 6 * L, 2, 3 * P)
        diff_r = view(DB + 1536 + 6 * L + 6 * P, 2, L)
        UNITS = [(h, t) for h in range(4) for t in range(3)]

        def diff_tensor(pe):
            for m in range(8):
                b = fill_bank(pe, "v")
                pe.matmul(b[:, 0:L], C("rot_diff"), proj[:, B_T + m, :], start=True, stop=True).then_inc(FV, 1)
            for t, (t0, n) in enumerate(TILES):
                b = fill_bank(pe, "a")
                for m in range(4):
                    mm = pe.transpose(b[0:n, m * P:(m + 1) * P], proj[:, B_T + 8 + m, t0:t0 + n], C("ident"))
                mm.then_inc(FA, 1)
            pe.wait_ge(operand_ready.sem, operand_ready.next())
            b = fill_bank(pe, "v")
            pe.matmul(b[:, 0:2], C("ones")[0:HD, :], small[0:HD, 32:34], start=True, stop=True).then_inc(FV, 1)
            for i in range(len(UNITS) + 3):
                if i < len(UNITS):
                    h, t = UNITS[i]
                    t0, n = TILES[t]
                    for c in range(2):
                        r = slice(64 * c, 64 * c + 64)
                        b = fill_bank(pe, "v")
                        pe.matmul(b[0:n, 0:L], proj[r, B_T + h, t0:t0 + n], proj[r, B_T + 4 + h, :], start=True, stop=True)\
                            .then_inc(FV, 1)
                if 2 <= i < len(UNITS) + 2:
                    h, t = UNITS[i - 2]
                    n = TILES[t][1]
                    pe.wait_ge(operand_ready.sem, operand_ready.next())
                    b = fill_bank(pe, "a")
                    for kt, (k0, kn) in enumerate(TILES):
                        mm = pe.transpose(b[0:kn, kt * P:kt * P + n], diff_e[0:n, (i - 2) % 3, 0, k0:k0 + kn],
                                          C("ident")[0:n, 0:n])
                    mm.then_inc(FA, 1)
                if i >= 3:
                    h, t = UNITS[i - 3]
                    n = TILES[t][1]
                    pe.wait_ge(aoperand_ready.sem, aoperand_ready.next())
                    b = fill_bank(pe, "v")
                    for kt, (k0, kn) in enumerate(TILES):
                        mm = pe.matmul(b[:, 0:n], diff_v[0:kn, kt, h * P:(h + 1) * P],
                                       diff_t[0:kn, (i - 3) % 2, kt * P:kt * P + n], start=(kt == 0), stop=(kt == 2))
                    mm.then_inc(FV, 1)
            for h in range(4):
                norm_tensor(pe, 1, L)

        def diff_vector(dve, l):
            lam_init = 0.8 - 0.6 * math.exp(-0.3 * l)
            for m in range(8):
                b = take_bank(dve, "v")
                dve.tensor_tensor(diff_r[:, m % 2, :], b[:, 0:L], C("sin_diff"), ALU.mult).then_inc(EV, 1)
                dve.tensor_tensor(proj[:, B_T + m, :], proj[:, B_T + m, :], C("cos_diff"), ALU.mult)
                dve.drain()
                dve.tensor_tensor(proj[:, B_T + m, :], proj[:, B_T + m, :], diff_r[:, m % 2, :], ALU.add)
            for j in range(2):
                dve.tensor_tensor(small[0:HD, 32 + j:33 + j], V("df_lam_2", 4 * l + 2 * j, 1, HD),
                                  V("df_lam_2", 4 * l + 2 * j + 1, 1, HD), ALU.mult)
            dve.drain().then_inc(operand_ready.sem, 1)
            b = take_bank(dve, "v")
            dve.tensor_copy(small[:, 34:36], b[:, 0:2]).then_inc(EV, 1)
            dve.drain().then_inc(for_scalar.sem, 1)
            dve.wait_ge(from_scalar.sem, from_scalar.next())
            dve.tensor_tensor(small[:, 36:37], small[:, 35:36], small[:, 34:35], ALU.subtract)
            dve.drain()
            dve.tensor_scalar(small[:, 36:37], small[:, 36:37], -lam_init, None, ALU.add)
            dve.drain()
            for i in range(len(UNITS) + 3):
                if i < len(UNITS):
                    h, t = UNITS[i]
                    n = TILES[t][1]
                    o = 8 * (i % 3)
                    for c in range(2):
                        b = take_bank(dve, "v")
                        dve.tensor_copy(diff_e[0:n, i % 3, c, :], b[0:n, 0:L]).then_inc(EV, 1)
                    dve.drain()
                    dve.tensor_reduce(small[0:n, o:o + 2], diff_e[0:n, i % 3, :, :], AX.X, ALU.max)
                    dve.drain()
                    dve.tensor_scalar(small[0:n, o:o + 2], small[0:n, o:o + 2], -HD ** -0.5, None, ALU.mult)\
                        .then_inc(logits_ready.sem, 1)
                if 1 <= i <= len(UNITS):
                    h, t = UNITS[i - 1]
                    n = TILES[t][1]
                    o = 8 * ((i - 1) % 3)
                    e = diff_e[0:n, (i - 1) % 3, :, :]
                    dve.wait_ge(exp_ready.sem, exp_ready.next())
                    dve.reciprocal(small[0:n, o + 4:o + 6], small[0:n, o + 2:o + 4])
                    dve.drain()
                    dve.tensor_scalar(small[0:n, o + 6:o + 7], small[0:n, o + 5:o + 6], small[0:n, 36:37], None, ALU.mult)
                    dve.tensor_scalar(e[:, 0, :], e[:, 0, :], small[0:n, o + 4:o + 5], None, ALU.mult)
                    dve.drain()
                    dve.scalar_tensor_tensor(out=e[:, 0, :], in0=e[:, 1, :], scalar=small[0:n, o + 6:o + 7], in1=e[:, 0, :],
                                             op0=ALU.mult, op1=ALU.add).then_inc(operand_ready.sem, 1)
                if i >= 3:
                    h, t = UNITS[i - 3]
                    t0, n = TILES[t]
                    b = take_bank(dve, "v")
                    dve.tensor_copy(H[:, 2 + h, t0:t0 + n], b[:, 0:n]).then_inc(EV, 1)
            for h in range(4):
                dve.drain().then_inc(latent_ready.sem, 1)
                norm_vector(dve, P, L)
                dve.tensor_tensor(H[:, 2 + h, :], H[:, 2 + h, :], rstd[:, :], ALU.mult)
                dve.drain()
                dve.tensor_scalar(H[:, 2 + h, :], H[:, 2 + h, :], V("df_subln_g_2", l), 1.0 - lam_init, ALU.mult, ALU.mult)

        def diff_scalar(act):
            for t, (t0, n) in enumerate(TILES):
                b = take_bank(act, "a")
                act.activation(diff_v[0:n, t, :], b[0:n, :], ACT.Copy).then_inc(EA, 1)
            act.wait_ge(for_scalar.sem, for_scalar.next())
            act.activation(small[:, 34:36], small[:, 34:36], ACT.Exp).then_inc(from_scalar.sem, 1)
            for i in range(len(UNITS) + 2):
                if i < len(UNITS):
                    n = TILES[UNITS[i][1]][1]
                    o = 8 * (i % 3)
                    act.wait_ge(logits_ready.sem, logits_ready.next())
                    for c in range(2):
                        e = diff_e[0:n, i % 3, c, :]
                        ins = act.activation(e, e, ACT.Exp, bias=small[0:n, o + c:o + c + 1], scale=HD ** -0.5,
                                             accum_out=small[0:n, o + 2 + c:o + 3 + c])
                    ins.then_inc(exp_ready.sem, 1)
                if i >= 2:
                    n = TILES[UNITS[i - 2][1]][1]
                    b = take_bank(act, "a")
                    for kt, (k0, kn) in enumerate(TILES):
                        ins = act.activation(diff_t[0:kn, i % 2, kt * P:kt * P + n], b[0:kn, kt * P:kt * P + n], ACT.Copy)
                    ins.then_inc(EA, 1)
                    act.drain().then_inc(aoperand_ready.sem, 1)
            for h in range(4):
                act.wait_ge(latent_ready.sem, latent_ready.next())
                norm_scalar(act, H[:, 2 + h:3 + h, :], 1, L)

        G0 = MIN * Q
        gl = [view(G0 + 5 * Q * d, 5, L) for d in range(2)]
        gl_dc = view(G0 + 10 * Q, 2, NCH)
        gl_kt = view(G0 + 10 * Q + 40, 2, 3 * P)
        gl_v = view(G0 + 10 * Q + 40 + 6 * P, 3, 256)
        gl_ve = view(G0 + 10 * Q + 40 + 12 * P, 4, 8, HD)
        gl_st = view(G0 + 10 * Q + 40 + 12 * P + 2048, 2, NCH, HD)
        gl_at = view(G0 + 10 * Q + 40 + 12 * P + 2048 + 2 * NCH * HD, 4, 2, P)

        def ends_of(x, d):
            c = x.rearrange("p (c t) -> p c t", t=CH)
            return c[:, :, CH - 1:CH] if d == 0 else c[:, :, 0:1]

        def cumsum(dve, out, x, d):
            if d == 0:
                return dve.tensor_tensor_scan(out, C("go_f"), x, 0.0, ALU.mult, ALU.add)
            return dve.tensor_tensor_scan(out[:, ::-1], C("go_b")[:, ::-1], x[:, ::-1], 0.0, ALU.mult, ALU.add)

        def gla_tensor(pe, l):
            for d in range(2):
                b = fill_bank(pe, "v")
                pe.matmul(b[:, 0:L], V("gl_gate_up_2", (2 * l + d) * P, P, 32), proj[0:32, C_T + 6, :], start=True, stop=True)\
                    .then_inc(FV, 1)
            for t, (t0, n) in enumerate(TILES):
                b = fill_bank(pe, "v")
                for m in range(2):
                    mm = pe.transpose(b[0:n, m * P:(m + 1) * P], proj[:, C_T + 2 + m, t0:t0 + n], C("ident"))
                mm.then_inc(FV, 1)
            for d in range(2):
                pe.wait_ge(operand_ready.sem, operand_ready.next())
                b = fill_bank(pe, "v")
                for t, (t0, n) in enumerate(TILES):
                    mm = pe.transpose(b[0:n, t * P:(t + 1) * P], gl[d][:, 3, t0:t0 + n], C("ident"))
                mm.then_inc(FV, 1)
            for t, (t0, n) in enumerate(TILES):
                nc_ = n // CH
                pe.wait_ge(operand_ready.sem, operand_ready.next())
                for d in range(2):
                    b = fill_bank(pe, "v")
                    for h in range(4):
                        mm = pe.matmul(b[32 * h:32 * h + 32, 0:nc_ * HD], gl_kt[0:n, d, t * P + 32 * h:t * P + 32 * h + 32],
                                       gl_ve[0:n, h, 0:nc_, :], start=True, stop=True, tile_position=(0, 32 * h))
                    mm.then_inc(FV, 1)
            pe.wait_ge(operand_ready.sem, operand_ready.next())
            for t, (t0, n) in enumerate(TILES):
                for h in range(4):
                    r = slice(32 * h, 32 * h + 32)
                    b = fill_bank(pe, "v")
                    for d in range(2):
                        mm = pe.matmul(b[0:n, d * P:d * P + n], gl[d][r, 2, t0:t0 + n], gl[d][r, 1, t0:t0 + n],
                                       start=True, stop=True, tile_position=(32 * h, 0))
                    mm.then_inc(FV, 1)
                pe.wait_ge(operand_ready.sem, operand_ready.next())
                for j in range(2):
                    b = fill_bank(pe, "v")
                    for h in (2 * j, 2 * j + 1):
                        rr = 64 * (h % 2)
                        parts = []
                        for d in range(2):
                            parts.append((0, n, gl_v[0:n, t, h * HD:(h + 1) * HD], gl_at[0:n, h, d, 0:n], (0, rr)))
                        for d in range(2):
                            for c in range(t0 // CH, (t0 + n) // CH):
                                prev = c - 1 if d == 0 else c + 1
                                if 0 <= prev < NCH:
                                    parts.append((c * CH - t0, CH, gl_st[32 * h:32 * h + 32, d, prev, :],
                                                  gl[d][32 * h:32 * h + 32, 1, c * CH:(c + 1) * CH], (32 * h, rr)))
                        for i, (a, w, lhs, rhs, tp) in enumerate(parts):
                            if i == 2 and n <= 32:
                                pe.drain()
                            mm = pe.matmul(b[rr:rr + 64, a:a + w], lhs, rhs, start=(i == 0), stop=(i == len(parts) - 1),
                                           skip_group_check=True, tile_position=tp)
                    mm.then_inc(FV, 1)
            for m in range(2):
                norm_tensor(pe, 1, L, C("ones64"))

        def gla_vector(dve, l):
            for d in range(2):
                b = take_bank(dve, "v")
                dve.tensor_scalar(gl[d][:, 0, :], b[:, 0:L], V("gl_gate_b_2", 2 * l + d), None, ALU.add).then_inc(EV, 1)
                dve.drain().then_inc(for_scalar.sem, 1)
            for t, (t0, n) in enumerate(TILES):
                b = take_bank(dve, "v")
                dve.tensor_copy(gl_v[0:n, t, :], b[0:n, 0:256]).then_inc(EV, 1)
            for d in range(2):
                z, tmp = gl[d][:, 0, :], gl[d][:, 4, :]
                dve.wait_ge(from_scalar.sem, from_scalar.next())
                dve.scalar_tensor_tensor(out=tmp, in0=z, scalar=0.0, in1=tmp, op0=ALU.min, op1=ALU.subtract)
                dve.drain()
                dve.tensor_scalar(tmp, tmp, 1.0 / 16.0, None, ALU.mult)
                dve.drain()
                cumsum(dve, z, tmp, d)
                dve.drain()
                dve.tensor_tensor(gl[d][:, 3, :].rearrange("p (c t) -> p c t", t=CH),
                                  ends_of(z, d).to_broadcast([P, NCH, CH]), z.rearrange("p (c t) -> p c t", t=CH),
                                  ALU.subtract)
                dve.drain().then_inc(for_scalar.sem, 1)
            for d in range(2):
                g = gl[d]
                dve.wait_ge(from_scalar.sem, from_scalar.next())
                dve.tensor_copy(gl_dc[:, d, :], ends_of(g[:, 1, :], d).rearrange("p c o -> p (c o)"))
                dve.drain()
                dve.scalar_tensor_tensor(out=g[:, 1, :], in0=g[:, 1, :], scalar=32 ** -0.5, in1=proj[:, C_T, :],
                                         op0=ALU.mult, op1=ALU.mult)
                dve.tensor_tensor(g[:, 2, :], g[:, 2, :], proj[:, C_T + 1, :], ALU.mult)
                dve.tensor_tensor(g[:, 3, :], g[:, 3, :], proj[:, C_T + 1, :], ALU.mult)
                dve.drain().then_inc(operand_ready.sem, 1)
                b = take_bank(dve, "v")
                dve.tensor_copy(gl_kt[:, d, 0:2 * P], b[:, 0:2 * P])
                dve.tensor_copy(gl_kt[0:16, d, 2 * P:3 * P], b[0:16, 2 * P:3 * P]).then_inc(EV, 1)
            for t, (t0, n) in enumerate(TILES):
                nc_ = n // CH
                dve.drain()
                for h in range(4):
                    dve.tensor_tensor(gl_ve[0:n, h, 0:nc_, :],
                                      gl_v[0:n, t, h * HD:(h + 1) * HD].unsqueeze(1).to_broadcast([n, nc_, HD]),
                                      C("chunk_of")[0:n, 0:nc_].unsqueeze(2).to_broadcast([n, nc_, HD]), ALU.mult)
                dve.drain().then_inc(operand_ready.sem, 1)
                for d in range(2):
                    b = take_bank(dve, "v")
                    dve.tensor_copy(gl_st[:, d, t0 // CH:t0 // CH + nc_, :],
                                    b[:, 0:nc_ * HD].rearrange("p (c v) -> p c v", v=HD)).then_inc(EV, 1)
            dve.drain()
            for i in range(1, NCH):
                for d in range(2):
                    c, prev = (i, i - 1) if d == 0 else (NCH - 1 - i, NCH - i)
                    dve.scalar_tensor_tensor(out=gl_st[:, d, c, :], in0=gl_st[:, d, prev, :], scalar=gl_dc[:, d, c:c + 1],
                                             in1=gl_st[:, d, c, :], op0=ALU.mult, op1=ALU.add)
                dve.drain()
            dve.drain().then_inc(operand_ready.sem, 1)
            for t, (t0, n) in enumerate(TILES):
                for h in range(4):
                    b = take_bank(dve, "v")
                    dve.tensor_tensor(gl_at[0:n, h, :, 0:n], b[0:n, 0:2 * P].rearrange("p (d t) -> p d t", d=2)[:, :, 0:n],
                                      C("le_fb")[0:n, :].rearrange("p (d t) -> p d t", d=2)[:, :, 0:n],
                                      ALU.mult).then_inc(EV, 1)
                dve.drain().then_inc(operand_ready.sem, 1)
                for j in range(2):
                    b = take_bank(dve, "v")
                    dve.tensor_copy(H[:, 6 + j, t0:t0 + n], b[:, 0:n]).then_inc(EV, 1)
            for m in range(2):
                dve.drain().then_inc(latent_ready.sem, 1)
                norm_vector(dve, HD, L)
                dve.tensor_tensor(H[:, 6 + m, :], H[:, 6 + m, :], rstd[:, :], ALU.mult)
                dve.drain()
                dve.scalar_tensor_tensor(out=H[:, 6 + m, :], in0=H[:, 6 + m, :], scalar=V("gl_norm_g_2", l),
                                         in1=proj[:, C_T + 4 + m, :], op0=ALU.mult, op1=ALU.mult)

        def gla_scalar(act):
            for d in range(2):
                t = gl[d][:, 4, :]
                act.wait_ge(for_scalar.sem, for_scalar.next())
                act.activation(t, gl[d][:, 0, :], ACT.Abs)
                act.drain()
                act.activation(t, t, ACT.Exp, scale=-1.0)
                act.drain()
                act.activation(t, t, ACT.Ln, bias=1.0).then_inc(from_scalar.sem, 1)
            for d in range(2):
                g = gl[d]
                act.wait_ge(for_scalar.sem, for_scalar.next())
                act.activation(g[:, 1, :], g[:, 0, :], ACT.Exp)
                act.activation(g[:, 2, :], g[:, 0, :], ACT.Exp, scale=-1.0)
                act.activation(g[:, 3, :], g[:, 3, :], ACT.Exp)
                act.drain().then_inc(from_scalar.sem, 1)
            act.activation(proj[:, C_T + 4:C_T + 6, :], proj[:, C_T + 4:C_T + 6, :], ACT.Silu)
            act.drain()
            for m in range(2):
                act.wait_ge(latent_ready.sem, latent_ready.next())
                norm_scalar(act, H[:, 6 + m:7 + m, :], 1, L)

        raw = view(0, 9, L)
        sh = view(9 * Q, 9, L)
        kk, rw_o, ksum, rtmp = view(0, 2, L), view(2 * Q, 2, L), view(4 * Q, 2, L), view(6 * Q, 2, L)
        kdir, ka, lwa, bR, Kb, Bb = [view((18 + 2 * i) * Q, 2, L) for i in range(6)]
        R0 = 30 * Q
        rv = view(R0, 3, 256)
        kht, bht = view(R0 + 768, 256), view(R0 + 1024, 256)
        rve, rbe, rpe = [view(R0 + 1280 + 512 * i, 4, 2, HD) for i in range(3)]
        rF = view(R0 + 2816, 2, NCH, HD)
        rS = view(R0 + 2816 + 2 * NCH * HD, 2, NCH, HD)
        M0 = R0 + 2816 + 4 * NCH * HD
        s_flat = S[:, :, :].rearrange("p a b -> p (a b)")
        mT, mM, mM2, mM2T = [s_flat[:, 512 * i:512 * (i + 1)].rearrange("p (h t) -> p h t", h=4) for i in range(4)]
        nT, LkT, LbT, Z = [view(M0 + 512 * i, 4, P) for i in range(4)]
        rdc = view(M0 + 2048, 2, NCH)

        def rwkv_plan(l):
            for w in ("rw_w_up_2", "rw_a_up_2"):
                plan.append((A[w][l].rearrange("d r c -> (d r) c").unsqueeze(1), 1, 256))
            plan.append((A["rw_g_up_2"][l].unsqueeze(1), 1, 256))

        def rwkv_tensor(pe, l):
            pe.wait_ge(operand_ready.sem, operand_ready.next())
            for j in range(2):
                b = fill_bank(pe, "v")
                pe.matmul(b[:, 0:L], C("ones64"), S[:, j, :], start=True, stop=True).then_inc(FV, 1)
            for t, (t0, n) in enumerate(TILES):
                b = fill_bank(pe, "v")
                for j in range(2):
                    mm = pe.transpose(b[0:n, j * P:(j + 1) * P], sh[:, 4 + j, t0:t0 + n], C("ident"))
                mm.then_inc(FV, 1)
            W = [next_slot(pe, 1, 256) for _ in range(3)]
            pe.wait_ge(aoperand_ready.sem, aoperand_ready.next())
            for d in range(2):
                dr = slice(64 * d, 64 * d + 64)
                for part in range(2):
                    for j in range(2):
                        b = fill_bank(pe, "v")
                        pe.matmul(b[:, 0:L], W[part][dr, 0, j * P:(j + 1) * P], sh[dr, 6 + part, :], start=True, stop=True)\
                            .then_inc(FV, 1)
                pe.wait_ge(operand_ready.sem, operand_ready.next())
                for t in range(3):
                    rwkv_tile_tensor(pe, d, t)
                pe.wait_ge(aoperand_ready.sem, aoperand_ready.next())
                for i in range(1, NCH):
                    c, prev = (i, i - 1) if d == 0 else (NCH - 1 - i, NCH - i)
                    pe.wait_ge(operand_ready.sem, operand_ready.next())
                    b = fill_bank(pe, "v")
                    for h in range(4):
                        r, j = slice(64 * (h % 2), 64 * (h % 2) + 64), h // 2
                        mm = pe.matmul(b[r, j * HD:(j + 1) * HD], rF[r, j, c, :], rS[r, j, prev, :], start=True, stop=True)
                    mm.then_inc(FV, 1)
                pe.wait_ge(operand_ready.sem, operand_ready.next())
                for t, (t0, n) in enumerate(TILES):
                    pairs = inter_chunks(d, t0, n)
                    if not pairs:
                        continue
                    b = fill_bank(pe, "v")
                    for c, prev in pairs:
                        for h in range(4):
                            r, j = slice(64 * (h % 2), 64 * (h % 2) + 64), h // 2
                            a = j * P + c * CH - t0
                            mm = pe.matmul(b[r, a:a + CH], rS[r, j, prev, :], bR[r, j, c * CH:(c + 1) * CH], start=True, stop=True)
                    mm.then_inc(FV, 1)
            for j in range(2):
                b = fill_bank(pe, "v")
                pe.matmul(b[:, 0:L], W[2][:, 0, j * P:(j + 1) * P], sh[:, 8, :], start=True, stop=True).then_inc(FV, 1)
            for _ in range(3):
                read_with_bank()
            pe.wait_ge(operand_ready.sem, operand_ready.next())
            for src in (rw_o, rtmp):
                for j in range(2):
                    b = fill_bank(pe, "v")
                    pe.matmul(b[:, 0:L], C("ones64"), src[:, j, :], start=True, stop=True).then_inc(FV, 1)
            for j in range(2):
                norm_tensor(pe, 1, L, C("ones64"))

        def inter_chunks(d, t0, n):
            out = [(c, c - 1 if d == 0 else c + 1) for c in range(t0 // CH, (t0 + n) // CH)]
            return [(c, p) for c, p in out if 0 <= p < NCH]

        def rwkv_tile_tensor(pe, d, t):
            t0, n = TILES[t]
            tok = slice(t0, t0 + n)
            nc_ = n // CH
            b = fill_bank(pe, "v")
            for i, src in enumerate((lwa, kdir)):
                for j in range(2):
                    mm = pe.transpose(b[0:n, i * 256 + j * P:i * 256 + (j + 1) * P], src[:, j, tok], C("ident"))
            mm.then_inc(FV, 1)
            b = fill_bank(pe, "v")
            for j in range(2):
                mm = pe.transpose(b[0:n, j * P:(j + 1) * P], ka[:, j, tok], C("ident"))
            mm.then_inc(FV, 1)
            for pp in range(2):
                r = slice(64 * pp, 64 * pp + 64)
                for pairs in (((Bb, lwa), (lwa, Bb)), ((Kb, lwa), (Kb, bR)), ((Bb, bR),)):
                    b = fill_bank(pe, "v")
                    for i, (x, y) in enumerate(pairs):
                        for j in range(2):
                            a = (2 * i + j) * P
                            mm = pe.matmul(b[0:n, a:a + n], x[r, j, tok], y[r, j, tok], start=True, stop=True)
                    mm.then_inc(FV, 1)
            pe.wait_ge(operand_ready.sem, operand_ready.next())

            def per_head(lhs, rhs, w):
                b = fill_bank(pe, "v")
                for h in range(4):
                    mm = pe.matmul(b[0:n, h * w:h * w + (n if rhs is not Z and w == P else w)], lhs(h), rhs_of(rhs, h, w), start=True, stop=True)
                mm.then_inc(FV, 1)

            def rhs_of(rhs, h, w):
                if rhs is Z:
                    return Z[0:n, h, :]
                if rhs is rv:
                    return rv[0:n, t, h * HD:(h + 1) * HD]
                return rhs[0:n, h, 0:n]
            m = lambda x: (lambda h: x[0:n, h, 0:n])

            def squares(which, lhs, rhs):
                b = fill_bank(pe, which)
                for h in range(4):
                    mm = pe.matmul(b[0:n, h * P:h * P + n], lhs[0:n, h, 0:n], rhs[0:n, h, 0:n], start=True, stop=True)
                mm.then_inc(FV if which == "v" else FA, 1)
            per_head(m(nT), rv, HD)
            squares("v", mT, mM)
            squares("a", mM, mT)
            pe.wait_ge(operand_ready.sem, operand_ready.next())
            per_head(m(mT), Z, P)
            pe.wait_ge(operand_ready.sem, operand_ready.next())
            pe.wait_ge(aoperand_ready.sem, aoperand_ready.next())
            per_head(m(mM2T), Z, P)
            squares("v", mM2T, mM2)
            squares("a", mM2, mM2T)
            pe.wait_ge(operand_ready.sem, operand_ready.next())
            pe.wait_ge(aoperand_ready.sem, aoperand_ready.next())
            per_head(m(nT), Z, P)
            squares("a", mM, nT)
            pe.wait_ge(operand_ready.sem, operand_ready.next())
            pe.wait_ge(aoperand_ready.sem, aoperand_ready.next())
            per_head(m(mM2), Z, P)
            pe.wait_ge(operand_ready.sem, operand_ready.next())
            b = fill_bank(pe, "v")
            for h in range(4):
                rr, j = 64 * (h % 2), h // 2
                mm = pe.matmul(b[rr:rr + 64, j * P:j * P + n], Z[0:n, h, 0:HD], LbT[0:n, h, 0:n], start=True, stop=True)
            mm.then_inc(FV, 1)
            b = fill_bank(pe, "v")
            for h in range(4):
                rr, j = 64 * (h % 2), h // 2
                o = b[rr:rr + 64, j * P:j * P + n]
                pe.matmul(o, rv[0:n, t, h * HD:(h + 1) * HD], LkT[0:n, h, 0:n], start=True, stop=False)
                mm = pe.matmul(o, Z[0:n, h, HD:P], LbT[0:n, h, 0:n], start=False, stop=True)
            mm.then_inc(FV, 1)
            pe.wait_ge(operand_ready.sem, operand_ready.next())
            for g in range(0, n, 32):
                r = slice(g, min(g + 32, n))
                w = (r.stop - r.start) // CH * HD
                b, b2 = fill_bank(pe, "a"), fill_bank(pe, "v")
                for h in range(4):
                    rr, j = 64 * (h % 2), h // 2
                    o = slice(j * P, j * P + w)
                    tp = (g, rr)
                    mm2 = pe.matmul(b[rr:rr + 64, o], Z[r, h, 0:HD], rbe[r, h, 0:w // HD, :], start=True, stop=True, tile_position=tp)
                    pe.matmul(b2[rr:rr + 64, o], kht[r, h * HD:(h + 1) * HD], rve[r, h, 0:w // HD, :], start=True, stop=False,
                              tile_position=tp)
                    mm = pe.matmul(b2[rr:rr + 64, o], bht[r, h * HD:(h + 1) * HD], rpe[r, h, 0:w // HD, :], start=False,
                                   stop=True, tile_position=tp)
                mm2.then_inc(FA, 1)
                mm.then_inc(FV, 1)

        def rwkv_tile_vector(dve, d, t):
            t0, n = TILES[t]
            tok = slice(t0, t0 + n)
            nc_ = n // CH
            lt, lt_t, le = ("lt_f", "lt_b", "le_f") if d == 0 else ("lt_b", "lt_f", "le_b")
            b = take_bank(dve, "v")
            dve.tensor_copy(Z[0:n, :, 0:HD], b[0:n, 0:256].rearrange("p (h k) -> p h k", h=4))
            dve.tensor_copy(kht[0:n, :], b[0:n, 256:512]).then_inc(EV, 1)
            b = take_bank(dve, "v")
            dve.tensor_copy(bht[0:n, :], b[0:n, 0:256]).then_inc(EV, 1)

            def masked(b, at, out, pp, mask, sign=1.0):
                return dve.scalar_tensor_tensor(out=out[0:n, pp::2, 0:n],
                                                in0=b[0:n, at:at + 256].rearrange("p (j t) -> p j t", j=2)[:, :, 0:n],
                                                scalar=sign, in1=C(mask)[0:n, 0:n].unsqueeze(1).to_broadcast([n, 2, n]),
                                                op0=ALU.mult, op1=ALU.mult)
            for pp in range(2):
                b = take_bank(dve, "v")
                masked(b, 0, mT, pp, lt)
                masked(b, 256, mM, pp, lt_t).then_inc(EV, 1)
                b = take_bank(dve, "v")
                masked(b, 0, nT, pp, lt)
                masked(b, 256, LkT, pp, le).then_inc(EV, 1)
                b = take_bank(dve, "v")
                masked(b, 0, LbT, pp, le, -1.0).then_inc(EV, 1)
            dve.drain().then_inc(operand_ready.sem, 1)

            def by_chunk(out, x):
                two = C("half_of")[0:n, :]
                for half in range(2):
                    dve.tensor_tensor(out[0:n, :, half, :], x, two[:, half:half + 1].unsqueeze(1).to_broadcast([n, 4, HD]), ALU.mult)

            def copy4(out, w=P):
                b = take_bank(dve, "v")
                dve.tensor_copy(out[0:n, :, 0:n], b[0:n, :].rearrange("p (h t) -> p h t", h=4)[:, :, 0:n]).then_inc(EV, 1)
            b = take_bank(dve, "v")
            dve.tensor_copy(Z[0:n, :, HD:P], b[0:n, 0:256].rearrange("p (h v) -> p h v", h=4)).then_inc(EV, 1)
            dve.drain().then_inc(operand_ready.sem, 1)

            def apply(sign):
                b = take_bank(dve, "v")
                dve.tensor_tensor(Z[0:n, :, :], Z[0:n, :, :], b[0:n, :].rearrange("p (h t) -> p h t", h=4), sign)\
                    .then_inc(EV, 1)
            copy4(mM2)
            apply(ALU.subtract)
            dve.drain().then_inc(operand_ready.sem, 1)
            apply(ALU.add)
            copy4(mM)
            dve.drain().then_inc(operand_ready.sem, 1)
            by_chunk(rve, rv[0:n, t, :].rearrange("p (h v) -> p h v", h=4))
            apply(ALU.add)
            dve.drain().then_inc(operand_ready.sem, 1)
            by_chunk(rbe, bht[0:n, :].rearrange("p (h k) -> p h k", h=4))
            apply(ALU.add)
            dve.drain().then_inc(operand_ready.sem, 1)
            by_chunk(rpe, Z[0:n, :, HD:P])
            dve.drain().then_inc(operand_ready.sem, 1)
            b = take_bank(dve, "v")
            two = lambda b: b[:, 0:256].rearrange("p (j t) -> p j t", j=2)[:, :, 0:n]
            dve.tensor_tensor(bR[:, :, tok], bR[:, :, tok], two(b), ALU.add).then_inc(EV, 1)
            b = take_bank(dve, "v")
            if d == 0:
                dve.tensor_copy(rw_o[:, :, tok], two(b)).then_inc(EV, 1)
            else:
                dve.tensor_tensor(rw_o[:, :, tok], rw_o[:, :, tok], two(b), ALU.add).then_inc(EV, 1)
            for g in range(0, n, 32):
                nn = min(32, n - g) // CH
                c = (t0 + g) // CH
                b = take_bank(dve, "v")
                dve.tensor_copy(rS[:, :, c:c + nn, :],
                                b[:, 0:2 * P].rearrange("p (j c v) -> p j c v", j=2, c=2)[:, :, 0:nn, :]).then_inc(EV, 1)

        def rwkv_tile_scalar(act, t):
            t0, n = TILES[t]
            for out in (mM2T, nT, mM2):
                b = take_bank(act, "a")
                act.activation(out[0:n, :, 0:n], b[0:n, :].rearrange("p (h t) -> p h t", h=4)[:, :, 0:n], ACT.Copy)\
                    .then_inc(EA, 1)
                act.drain().then_inc(aoperand_ready.sem, 1)
            for g in range(0, n, 32):
                nn = min(32, n - g) // CH
                c = (t0 + g) // CH
                b = take_bank(act, "a")
                act.activation(rF[:, :, c:c + nn, :], b[:, 0:2 * P].rearrange("p (j c v) -> p j c v", j=2, c=2)[:, :, 0:nn, :],
                               ACT.Copy).then_inc(EA, 1)

        def rwkv_vector(dve, l):
            mu = lambda s: V("rw_shift_2", (2 * l + s) * 9, 9)
            c0 = small[:, 40:49]
            oka = small[:, 49:51]
            dve.tensor_tensor(c0, mu(0), mu(1), ALU.add)
            dve.tensor_scalar(oka, V("rw_k_a_2", 2 * l, 2), -1.0, 1.0, ALU.mult, ALU.add)
            dve.drain()
            dve.tensor_scalar(c0, c0, -1.0, 1.0, ALU.mult, ALU.add)
            dve.drain()
            for m in range(9):
                dve.tensor_scalar(sh[:, m, :], raw[:, m, :], c0[:, m:m + 1], None, ALU.mult)
            dve.drain()
            for m in range(9):
                dve.scalar_tensor_tensor(out=sh[:, m, 1:], in0=raw[:, m, 0:L - 1], scalar=mu(0)[:, m:m + 1], in1=sh[:, m, 1:],
                                         op0=ALU.mult, op1=ALU.add)
            dve.drain()
            for m in range(9):
                dve.scalar_tensor_tensor(out=sh[:, m, 0:L - 1], in0=raw[:, m, 1:], scalar=mu(1)[:, m:m + 1],
                                         in1=sh[:, m, 0:L - 1], op0=ALU.mult, op1=ALU.add)
            dve.drain().then_inc(for_scalar.sem, 1)
            for j in range(2):
                dve.tensor_scalar(kk[:, j, :], sh[:, 2 + j, :], V("rw_k_k_2", 2 * l + j), None, ALU.mult)
            dve.drain()
            dve.tensor_tensor(S[:, 0:2, :], kk, kk, ALU.mult)
            dve.drain().then_inc(operand_ready.sem, 1)
            for j in range(2):
                b = take_bank(dve, "v")
                dve.tensor_scalar(rtmp[:, j, :], b[:, 0:L], 1e-24, None, ALU.max).then_inc(EV, 1)
            dve.drain().then_inc(for_scalar.sem, 1)
            for t, (t0, n) in enumerate(TILES):
                b = take_bank(dve, "v")
                dve.tensor_copy(rv[0:n, t, :], b[0:n, 0:256]).then_inc(EV, 1)
            dve.wait_ge(from_scalar.sem, from_scalar.next())
            dve.reciprocal(rtmp, rtmp)
            dve.drain()
            dve.tensor_tensor(kk, kk, rtmp, ALU.mult)
            dve.drain()
            for d in range(2):
                for out, g in ((lwa, "rw_w0_2"), (ka, "rw_a0_2")):
                    for j in range(2):
                        b = take_bank(dve, "v")
                        dve.tensor_scalar(out[:, j, :], b[:, 0:L], V(g, (2 * l + d) * 2 + j), None, ALU.add).then_inc(EV, 1)
                dve.drain().then_inc(for_scalar.sem, 1)
                dve.wait_ge(from_scalar.sem, from_scalar.next())
                for j in range(2):
                    dve.tensor_scalar(kdir[:, j, :], ka[:, j, :], V("rw_k_a_2", 2 * l + j), oka[:, j:j + 1], ALU.mult, ALU.add)
                dve.tensor_scalar(lwa, lwa, -0.6065306597126334, None, ALU.mult)
                dve.drain()
                dve.tensor_tensor(kdir, kdir, sh[:, 2:4, :], ALU.mult)
                dve.tensor_tensor(ka, ka, kk, ALU.mult)
                for j in range(2):
                    cumsum(dve, bR[:, j, :], lwa[:, j, :], d)
                dve.drain()
                if d == 0:
                    dve.tensor_copy(ksum, kdir)
                else:
                    dve.tensor_tensor(ksum, ksum, kdir, ALU.add)
                dve.tensor_tensor(lwa, bR, lwa, ALU.subtract)
                for j in range(2):
                    dve.tensor_tensor(rtmp[:, j, :].rearrange("p (c t) -> p c t", t=CH),
                                      ends_of(bR[:, j, :], d).to_broadcast([P, NCH, CH]),
                                      bR[:, j, :].rearrange("p (c t) -> p c t", t=CH), ALU.subtract)
                dve.drain().then_inc(for_scalar.sem, 1)
                dve.wait_ge(from_scalar.sem, from_scalar.next())
                for j in range(2):
                    dve.tensor_copy(rdc[:, j, :], ends_of(bR[:, j, :], d).rearrange("p c o -> p (c o)"))
                dve.tensor_tensor(lwa, lwa, kk, ALU.mult)
                dve.tensor_tensor(Bb, Kb, ka, ALU.mult)
                dve.drain()
                dve.tensor_tensor(Kb, Kb, kdir, ALU.mult)
                dve.tensor_tensor(bR, bR, sh[:, 0:2, :], ALU.mult)
                dve.drain()
                dve.tensor_tensor(kdir, kdir, rtmp, ALU.mult)
                for j in range(2):
                    dve.scalar_tensor_tensor(out=ka[:, j, :], in0=ka[:, j, :], scalar=-1.0, in1=rtmp[:, j, :], op0=ALU.mult,
                                             op1=ALU.mult)
                dve.drain().then_inc(operand_ready.sem, 1)
                for t in range(3):
                    rwkv_tile_vector(dve, d, t)
                for i in range(1, NCH):
                    c, prev = (i, i - 1) if d == 0 else (NCH - 1 - i, NCH - i)
                    dve.drain().then_inc(operand_ready.sem, 1)
                    for j in range(2):
                        dve.scalar_tensor_tensor(out=rS[:, j, c, :], in0=rS[:, j, prev, :], scalar=rdc[:, j, c:c + 1],
                                                 in1=rS[:, j, c, :], op0=ALU.mult, op1=ALU.add)
                    dve.drain()
                    b = take_bank(dve, "v")
                    dve.tensor_tensor(rS[:, :, c, :], rS[:, :, c, :], b[:, 0:2 * HD].rearrange("p (j v) -> p j v", j=2), ALU.add)\
                        .then_inc(EV, 1)
                dve.drain().then_inc(operand_ready.sem, 1)
                for t, (t0, n) in enumerate(TILES):
                    pairs = inter_chunks(d, t0, n)
                    if not pairs:
                        continue
                    lo, hi = min(c for c, _ in pairs) * CH, max(c for c, _ in pairs) * CH + CH
                    b = take_bank(dve, "v")
                    dve.tensor_tensor(rw_o[:, :, lo:hi], rw_o[:, :, lo:hi],
                                      b[:, 0:256].rearrange("p (j t) -> p j t", j=2)[:, :, lo - t0:hi - t0], ALU.add)\
                        .then_inc(EV, 1)
                    dve.drain()
            for j in range(2):
                b = take_bank(dve, "v")
                dve.tensor_copy(kdir[:, j, :], b[:, 0:L]).then_inc(EV, 1)
            for j in range(2):
                dve.scalar_tensor_tensor(out=rtmp[:, j, :], in0=sh[:, j, :], scalar=V("rw_r_k_2", 2 * l + j), in1=ksum[:, j, :],
                                         op0=ALU.mult, op1=ALU.mult)
            dve.drain().then_inc(operand_ready.sem, 1)
            for j in range(2):
                b = take_bank(dve, "v")
                dve.scalar_tensor_tensor(out=rw_o[:, j, :], in0=b[:, 0:L], scalar=-1.0 / HD, in1=rw_o[:, j, :],
                                         op0=ALU.mult, op1=ALU.add).then_inc(EV, 1)
            for j in range(2):
                b = take_bank(dve, "v")
                dve.tensor_tensor(ka[:, j, :], b[:, 0:L], sh[:, 4 + j, :], ALU.mult).then_inc(EV, 1)
            for j in range(2):
                dve.drain().then_inc(latent_ready.sem, 1)
                norm_vector(dve, HD, L, 64e-5)
                dve.tensor_tensor(rw_o[:, j, :], rw_o[:, j, :], rstd[:, :], ALU.mult)
                dve.drain()
                dve.tensor_scalar(rw_o[:, j, :], rw_o[:, j, :], V("rw_gn_g_2", 2 * l + j), V("rw_gn_b_2", 2 * l + j),
                                  ALU.mult, ALU.add)
                dve.drain()
                dve.tensor_tensor(rw_o[:, j, :], rw_o[:, j, :], ka[:, j, :], ALU.add)
                dve.drain()
                dve.tensor_tensor(H[:, j, :], rw_o[:, j, :], kdir[:, j, :], ALU.mult)

        def rwkv_scalar(act):
            act.wait_ge(for_scalar.sem, for_scalar.next())
            act.activation(sh[:, 6, :], sh[:, 6, :], ACT.Tanh)
            act.activation(sh[:, 8, :], sh[:, 8, :], ACT.Sigmoid)
            act.drain().then_inc(aoperand_ready.sem, 1)
            act.wait_ge(for_scalar.sem, for_scalar.next())
            act.activation(rtmp, rtmp, ACT.Sqrt).then_inc(from_scalar.sem, 1)
            for d in range(2):
                act.wait_ge(for_scalar.sem, for_scalar.next())
                act.activation(lwa, lwa, ACT.Sigmoid)
                act.activation(ka, ka, ACT.Sigmoid)
                act.drain().then_inc(from_scalar.sem, 1)
                act.wait_ge(for_scalar.sem, for_scalar.next())
                act.activation(Kb, bR, ACT.Exp, scale=-1.0)
                act.activation(lwa, lwa, ACT.Exp)
                act.activation(rtmp, rtmp, ACT.Exp)
                act.drain()
                act.activation(bR, bR, ACT.Exp)
                act.drain().then_inc(from_scalar.sem, 1)
                for t in range(3):
                    rwkv_tile_scalar(act, t)
                act.drain().then_inc(aoperand_ready.sem, 1)
            for j in range(2):
                act.wait_ge(latent_ready.sem, latent_ready.next())
                norm_scalar(act, rw_o[:, j:j + 1, :], 1, L)

        def mix_out_tensor(pe):
            project_tensor(pe, D, KD, lambda k: H[:, k, :], L)

        def mix_out_vector(dve):
            project_vector(dve, D, lambda m, rows, b: dve.tensor_tensor(X[:, m, :], X[:, m, :], b[:, 0:L], ALU.add))

        NE, CAP, FE = 16, 34, A["e_w1_2"].shape[3]
        KE = FE // P
        PAIRS = NE // 2
        xs = view(0, KD, NE * 64)
        gT = view(8192, PAIRS, L)
        T0 = 8192 + PAIRS * L
        utok = view(T0, 3, D)
        hot = view(T0 + 3072, 3, NE, 64)
        E0 = T0 + 6144
        aff, cum, mask = [view(E0 + 48 * i, 3, NE) for i in range(3)]
        affT, work = view(E0 + 144, L), view(E0 + 144 + L, L)
        top8 = view(E0 + 144 + 2 * L, 8)
        ghot = view(E0 + 152 + 2 * L, NE, 64)
        hs, hid2 = view(T0, FE), view(T0 + FE, FE)
        hidT = view(T0 + 2 * FE, KE, P)
        ys = view(T0 + 3 * FE, 4, D)
        CHUNKS = ((0, 512), (512, 512), (1024, 384))
        KSPLIT = ((0, 4), (4, 4), (8, 3))
        silu_ready = signal("silu_ready")

        def moe_plan(l):
            load_plan(A["router_2"][l], 0, NE, 0, KD)
            for p in range(PAIRS):
                for w in ("e_w1_2", "e_w3_2"):
                    for k in range(0, KD, 2):
                        for e in (2 * p, 2 * p + 1):
                            load_plan(A[w][l, e], 0, FE, k, 2)
                for k0, nk in KSPLIT:
                    for e in (2 * p, 2 * p + 1):
                        load_plan(A["e_w2_2"][l, e], 0, D, k0, nk)

        def moe_tensor(pe):
            norm_tensor(pe, KD, L)
            pe.wait_ge(operand_ready.sem, operand_ready.next())
            W = next_slot(pe, KD, NE)
            b = fill_bank(pe, "v")
            for t, (t0, n) in enumerate(TILES):
                for k in range(KD):
                    mm = pe.matmul(b[0:n, t * NE:(t + 1) * NE], H[:, k, t0:t0 + n], W[:, k, :], start=(k == 0), stop=(k == KD - 1))
            mm.then_inc(FV, 1)
            read_with_bank()
            for t, (t0, n) in enumerate(TILES):
                for half in range(2):
                    b = fill_bank(pe, "a")
                    for m in range(4):
                        mm = pe.transpose(b[0:n, m * P:(m + 1) * P], H[:, 4 * half + m, t0:t0 + n], C("ident"))
                    mm.then_inc(FA, 1)
            pe.wait_ge(operand_ready.sem, operand_ready.next())
            b = fill_bank(pe, "v")
            for t, (t0, n) in enumerate(TILES):
                mm = pe.transpose(b[0:NE, t0:t0 + n], aff[0:n, t, :], C("ident")[0:n, 0:n])
            mm.then_inc(FV, 1)
            pe.wait_ge(operand_ready.sem, operand_ready.next())
            b = fill_bank(pe, "v")
            for t, (t0, n) in enumerate(TILES):
                mm = pe.transpose(b[0:n, t * NE:(t + 1) * NE], work[0:NE, t0:t0 + n], C("ident")[0:NE, 0:NE])
            mm.then_inc(FV, 1)
            pe.wait_ge(operand_ready.sem, operand_ready.next())
            b = fill_bank(pe, "v")
            for t, (t0, n) in enumerate(TILES):
                o = b[0:n, t * NE:(t + 1) * NE]
                for s_ in range(t):
                    pe.matmul(o, C("ones")[:, 0:n], mask[:, s_, :], start=(s_ == 0), stop=False)
                mm = pe.matmul(o, C("before")[0:n, 0:n], mask[0:n, t, :], start=(t == 0), stop=True)
            mm.then_inc(FV, 1)
            for t, (t0, n) in enumerate(TILES):
                pe.wait_ge(operand_ready.sem, operand_ready.next())
                for half in range(2):
                    b = fill_bank(pe, "v")
                    for q in range(4):
                        p = 4 * half + q
                        mm = pe.transpose(b[:, q * P:q * P + n], ghot[0:n, 2 * p:2 * p + 2, :].rearrange("p e s -> p (e s)"),
                                          C("ident")[0:n, 0:n])
                    mm.then_inc(FV, 1)
            pe.wait_ge(aoperand_ready.sem, aoperand_ready.next())
            for k in range(KD):
                for half in range(2):
                    b = fill_bank(pe, "v")
                    o = b[:, :].rearrange("p (e s) -> p e s", s=64)[:, :, 0:CAP]
                    for t, (t0, n) in enumerate(TILES):
                        mm = pe.matmul(o, utok[0:n, t, k * P:(k + 1) * P], hot[0:n, t, 8 * half:8 * half + 8, 0:CAP],
                                       start=(t == 0), stop=(t == 2))
                    mm.then_inc(FV, 1)
            pe.wait_ge(operand_ready.sem, operand_ready.next())
            for p in range(PAIRS):
                for which in ("a", "v"):
                    b = [fill_bank(pe, which) for _ in CHUNKS]
                    for k0 in range(0, KD, 2):
                        W = [next_slot(pe, 2, FE) for _ in range(2)]
                        for k in range(2):
                            for ci, (c0, cw) in enumerate(CHUNKS):
                                for e in range(2):
                                    x = xs[:, k0 + k, (2 * p + e) * 64:(2 * p + e + 1) * 64]
                                    mm = pe.matmul(b[ci][64 * e:64 * e + 64, 0:cw], x, W[e][:, k, c0:c0 + cw],
                                                   start=(k0 + k == 0), stop=(k0 + k == KD - 1))
                                    last = k == 1 and ci == len(CHUNKS) - 1
                                    if last and e == 0:
                                        read_alone(mm)
                                if k0 + k == KD - 1:
                                    mm.then_inc(FA if which == "a" else FV, 1)
                        if k0 + 2 < KD:
                            read_alone(mm)
                        else:
                            read_with_bank(which)
                pe.wait_ge(operand_ready.sem, operand_ready.next())
                for f0, nf in KSPLIT:
                    b = fill_bank(pe, "a")
                    for f in range(nf):
                        mm = pe.transpose(b[:, f * P:(f + 1) * P], hid2[:, (f0 + f) * P:(f0 + f + 1) * P], C("ident"))
                    mm.then_inc(FA, 1)
                pe.wait_ge(aoperand_ready.sem, aoperand_ready.next())
                b = [fill_bank(pe, "v") for _ in range(2)]
                for f0, nf in KSPLIT:
                    W = [next_slot(pe, nf, D) for _ in range(2)]
                    for f in range(nf):
                        for c in range(2):
                            for e in range(2):
                                mm = pe.matmul(b[c][64 * e:64 * e + 64, :], hidT[:, f0 + f, 64 * e:64 * e + 64],
                                               W[e][:, f, c * 512:(c + 1) * 512], start=(f0 + f == 0), stop=(f0 + f == KE - 1))
                                if f == nf - 1 and c == 1 and e == 0:
                                    read_alone(mm)
                            if f0 + f == KE - 1:
                                mm.then_inc(FV, 1)
                    if f0 + nf < KE:
                        read_alone(mm)
                    else:
                        read_with_bank("v")
                if p % 4 == 3:
                    pe.wait_ge(operand_ready.sem, operand_ready.next())
                    for m in range(KD):
                        b = fill_bank(pe, "v")
                        for q in range(4):
                            mm = pe.matmul(b[:, 0:L], ys[:, q, m * P:(m + 1) * P], gT[:, p - 3 + q, :], start=(q == 0), stop=(q == 3))
                        mm.then_inc(FV, 1)

        def moe_vector(dve, l):
            gain_norm_vector(dve, "norm2_g_2", l)
            dve.memset(hot.rearrange("p t e s -> p (t e s)"), 0.0)
            dve.memset(ghot.rearrange("p e s -> p (e s)"), 0.0)
            dve.memset(xs.rearrange("p k s -> p (k s)"), 0.0)
            dve.memset(aff.rearrange("p t e -> p (t e)"), 0.0)
            dve.drain()
            b = take_bank(dve, "v")
            for t, (t0, n) in enumerate(TILES):
                ins = dve.tensor_copy(aff[0:n, t, :], b[0:n, t * NE:(t + 1) * NE])
            ins.then_inc(EV, 1)
            dve.drain()
            mx, sm = small[:, 52:55], small[:, 56:59]
            bc = lambda x: x.unsqueeze(2).to_broadcast([P, 3, NE])
            dve.tensor_reduce(mx, aff, AX.X, ALU.max)
            dve.drain()
            dve.tensor_tensor(aff, aff, bc(mx), ALU.subtract)
            dve.drain().then_inc(for_scalar.sem, 1)
            dve.wait_ge(from_scalar.sem, from_scalar.next())
            dve.tensor_reduce(sm, aff, AX.X, ALU.add)
            dve.drain()
            dve.reciprocal(sm, sm)
            dve.drain()
            dve.tensor_tensor(aff, aff, bc(sm), ALU.mult)
            dve.drain().then_inc(operand_ready.sem, 1)
            b = take_bank(dve, "v")
            w = work[0:NE, :]
            dve.tensor_copy(w, b[0:NE, 0:L]).then_inc(EV, 1)
            dve.drain()
            for i in range(0, CAP, 8):
                dve.max(out=top8[0:NE, :], in_=w)
                dve.drain()
                if CAP - i < 8:
                    dve.memset(top8[0:NE, CAP - i:8], -1.0)
                    dve.drain()
                dve.match_replace(out=w, in_to_replace=top8[0:NE, :], in_values=w, imm_value=-1.0)
                dve.drain()
            dve.tensor_scalar(w, w, 0.0, None, ALU.is_lt)
            dve.drain().then_inc(operand_ready.sem, 1)
            b = take_bank(dve, "v")
            for t, (t0, n) in enumerate(TILES):
                ins = dve.tensor_copy(mask[0:n, t, :], b[0:n, t * NE:(t + 1) * NE])
            ins.then_inc(EV, 1)
            dve.drain().then_inc(operand_ready.sem, 1)
            b = take_bank(dve, "v")
            for t, (t0, n) in enumerate(TILES):
                ins = dve.scalar_tensor_tensor(out=cum[0:n, t, :], in0=mask[0:n, t, :], scalar=-1000.0,
                                               in1=b[0:n, t * NE:(t + 1) * NE], op0=ALU.mult, op1=ALU.add)
            ins.then_inc(EV, 1)
            dve.drain()
            for t, (t0, n) in enumerate(TILES):
                dve.tensor_scalar(cum[0:n, t, :], cum[0:n, t, :], 1000.0, None, ALU.add)
            dve.drain()
            for t, (t0, n) in enumerate(TILES):
                if t:
                    pass
                ht = hot[0:n, t, :, 0:CAP]
                dve.tensor_tensor(ht, C("slot_no")[0:n, :].unsqueeze(1).to_broadcast([n, NE, CAP]),
                                  cum[0:n, t, :].unsqueeze(2).to_broadcast([n, NE, CAP]), ALU.is_equal)
                dve.drain()
                dve.tensor_tensor(ghot[0:n, :, 0:CAP], ht, aff[0:n, t, :].unsqueeze(2).to_broadcast([n, NE, CAP]), ALU.mult)
                dve.drain().then_inc(operand_ready.sem, 1)
                for half in range(2):
                    b = take_bank(dve, "v")
                    dve.tensor_copy(gT[:, 4 * half:4 * half + 4, t0:t0 + n],
                                    b[:, :].rearrange("p (q t) -> p q t", q=4)[:, :, 0:n]).then_inc(EV, 1)
            for k in range(KD):
                for half in range(2):
                    b = take_bank(dve, "v")
                    dve.tensor_copy(xs[:, k, 512 * half:512 * half + 512].rearrange("p (e s) -> p e s", s=64)[:, :, 0:CAP],
                                    b[:, :].rearrange("p (e s) -> p e s", s=64)[:, :, 0:CAP]).then_inc(EV, 1)
            dve.drain().then_inc(operand_ready.sem, 1)
            for p in range(PAIRS):
                for c0, cw in CHUNKS:
                    dve.wait_ge(silu_ready.sem, silu_ready.next())
                    b = take_bank(dve, "v")
                    dve.tensor_tensor(hid2[:, c0:c0 + cw], hs[:, c0:c0 + cw], b[:, 0:cw], ALU.mult).then_inc(EV, 1)
                dve.drain().then_inc(operand_ready.sem, 1)
                for c in range(2):
                    b = take_bank(dve, "v")
                    dve.tensor_copy(ys[:, p % 4, c * 512:(c + 1) * 512], b[:, :]).then_inc(EV, 1)
                if p % 4 == 3:
                    dve.drain().then_inc(operand_ready.sem, 1)
                    for m in range(KD):
                        b = take_bank(dve, "v")
                        dve.tensor_tensor(X[:, m, :], X[:, m, :], b[:, 0:L], ALU.add).then_inc(EV, 1)
                        dve.drain()

        def moe_scalar(act):
            norm_scalar(act, X[:, :, :], KD, L)
            for t, (t0, n) in enumerate(TILES):
                for half in range(2):
                    b = take_bank(act, "a")
                    act.activation(utok[0:n, t, 512 * half:512 * half + 512], b[0:n, :], ACT.Copy).then_inc(EA, 1)
            act.drain().then_inc(aoperand_ready.sem, 1)
            act.wait_ge(for_scalar.sem, for_scalar.next())
            act.activation(aff, aff, ACT.Exp).then_inc(from_scalar.sem, 1)
            for p in range(PAIRS):
                for c0, cw in CHUNKS:
                    b = take_bank(act, "a")
                    act.activation(hs[:, c0:c0 + cw], b[:, 0:cw], ACT.Silu).then_inc(EA, 1)
                    act.drain().then_inc(silu_ready.sem, 1)
                for f0, nf in KSPLIT:
                    b = take_bank(act, "a")
                    act.activation(hidT[:, f0:f0 + nf, :], b[:, 0:nf * P].rearrange("p (f s) -> p f s", s=P), ACT.Copy)\
                        .then_inc(EA, 1)
                act.drain().then_inc(aoperand_ready.sem, 1)

        def make_plan():
            for i in range(4):
                ada_plan(i)
            project_plan(A["ab_w_in"][0], 3072, KD)
            for i in range(4, AG):
                ada_plan(i)
            project_plan(A["ab_w_out"][0], D, KD)
            ffn_plan(0)
            odd_plan()
            ffn_plan(1)
            for l in range(DEPTH):
                second_in_plan(l)
                rwkv_plan(l)
                project_plan(A["w_out_2"][l], D, KD)
                moe_plan(l)
        make_plan()

        block = ctx.enter_context(nc.Block())

        def guarded(f):
            try:
                f()
            except Stop:
                pass

        @block.tensor
        def _(pe):
            def prog():
                start_tensor(pe)
                end_phase(pe, "pe")
                norm_tensor(pe, KD, SEQ)
                pe.wait_ge(operand_ready.sem, operand_ready.next())
                project_tensor(pe, 3072, KD, hrhs(SEQ), SEQ)
                turn_values_tensor(pe, 8)
                pe.wait_ge(aoperand_ready.sem, aoperand_ready.next())
                attend_tensor(pe, 16, head_rows(att_q), head_rows(att_k),
                              lambda h, t: att_v[:, t, h * HD:(h + 1) * HD], even_ada(ada_tensor, pe))
                pe.wait_ge(operand_ready.sem, operand_ready.next())
                project_tensor(pe, D, KD, lambda k: att_q[:, k, :], SEQ)
                norm_tensor(pe, KD, SEQ)
                end_phase(pe, "pe")
                norm_tensor(pe, KD, SEQ)
                ffn_tensor(pe, 0)
                norm_tensor(pe, KD, SEQ)
                end_phase(pe, "pe")
                norm_tensor(pe, KD, SEQ)
                odd_tensor(pe)
                norm_tensor(pe, KD, SEQ)
                end_phase(pe, "pe")
                norm_tensor(pe, KD, SEQ)
                ffn_tensor(pe, 1)
                norm_tensor(pe, KD, SEQ)
                end_phase(pe, "pe")
                for l in range(DEPTH):
                    second_in_tensor(pe)
                    end_phase(pe, "pe")
                    diff_tensor(pe)
                    end_phase(pe, "pe")
                    gla_tensor(pe, l)
                    end_phase(pe, "pe")
                    rwkv_tensor(pe, l)
                    end_phase(pe, "pe")
                    mix_out_tensor(pe)
                    end_phase(pe, "pe")
                    moe_tensor(pe)
                    end_phase(pe, "pe")
                norm_tensor(pe, KD, L)
                end_phase(pe, "pe")
            guarded(prog)

        @block.vector
        def _(dve):
            def prog():
                start_vector(dve)
                end_phase(dve, "dve")
                pre_norm_vector(dve, 0, "mix_pre_g", 0, 1)
                project_vector(dve, 3072, even_put(dve))
                dve.drain().then_inc(operand_ready.sem, 1)
                attend_vector(dve, 16, 0.125, lambda h: att_b[:, h, :], head_rows(att_q), even_ada(ada_vector, dve))
                dve.drain().then_inc(operand_ready.sem, 1)
                project_vector(dve, D, lambda m, rows, b: dve.tensor_copy(H[:, m, 0:SEQ], b[:, 0:SEQ]))
                dve.drain().then_inc(dve_done_y.sem, 1)
                post_norm_vector(dve, 0, "mix_post_g", 2)
                end_phase(dve, "dve")
                pre_norm_vector(dve, 0, "ffn_pre_g", 3, 4)
                ffn_first[0] = ntake["v"]
                ffn_vector(dve, 0)
                post_norm_vector(dve, 0, "ffn_post_g", 5)
                end_phase(dve, "dve")
                pre_norm_vector(dve, 1, "mix_pre_g", 0, 1)
                odd_vector(dve)
                post_norm_vector(dve, 1, "mix_post_g", 2)
                end_phase(dve, "dve")
                pre_norm_vector(dve, 1, "ffn_pre_g", 3, 4)
                ffn_first[1] = ntake["v"]
                ffn_vector(dve, 1)
                post_norm_vector(dve, 1, "ffn_post_g", 5)
                end_phase(dve, "dve")
                for l in range(DEPTH):
                    second_in_vector(dve, l)
                    end_phase(dve, "dve")
                    diff_vector(dve, l)
                    end_phase(dve, "dve")
                    gla_vector(dve, l)
                    end_phase(dve, "dve")
                    rwkv_vector(dve, l)
                    end_phase(dve, "dve")
                    mix_out_vector(dve)
                    end_phase(dve, "dve")
                    moe_vector(dve, l)
                    end_phase(dve, "dve")
                gain_norm_vector(dve, "final_g_2", 0)
                end_phase(dve, "dve")
            guarded(prog)

        @block.scalar
        def _(act):
            def prog():
                start_scalar(act)
                end_phase(act, "act")
                norm_scalar(act, XB, KD, SEQ)
                turn_values_scalar(act, 8)
                attend_scalar(act, 16)
                act.wait_ge(dve_done_y.sem, dve_done_y.next())
                norm_scalar(act, H[:, :, 0:SEQ], KD, SEQ)
                end_phase(act, "act")
                norm_scalar(act, XB, KD, SEQ)
                ffn_scalar(act, 0)
                act.wait_ge(dve_done_y.sem, dve_done_y.next())
                norm_scalar(act, H[:, :, 0:SEQ], KD, SEQ)
                end_phase(act, "act")
                norm_scalar(act, XB, KD, SEQ)
                odd_scalar(act)
                act.wait_ge(dve_done_y.sem, dve_done_y.next())
                norm_scalar(act, H[:, :, 0:SEQ], KD, SEQ)
                end_phase(act, "act")
                norm_scalar(act, XB, KD, SEQ)
                ffn_scalar(act, 1)
                act.wait_ge(dve_done_y.sem, dve_done_y.next())
                norm_scalar(act, H[:, :, 0:SEQ], KD, SEQ)
                end_phase(act, "act")
                for l in range(DEPTH):
                    norm_scalar(act, X[:, :, :], KD, L)
                    end_phase(act, "act")
                    diff_scalar(act)
                    end_phase(act, "act")
                    gla_scalar(act)
                    end_phase(act, "act")
                    rwkv_scalar(act)
                    end_phase(act, "act")
                    pass
                    end_phase(act, "act")
                    moe_scalar(act)
                    end_phase(act, "act")
                norm_scalar(act, X[:, :, :], KD, L)
                end_phase(act, "act")
            guarded(prog)

        @block.gpsimd
        def _(pool):
            def prog():
                pool.wait_ge(loaded.sem, 16 * 4)
                bias_pool(pool)
                for _ in range(5 + 6 * DEPTH + 1):
                    end_phase(pool, "pool")
            guarded(prog)

        @block.sync
        def _(sp):
            sp.dma_start(cst[:, :], A["consts"]).then_inc(loaded.sem, 16)
            sp.dma_start(vec[:, :], A["vectors"]).then_inc(loaded.sem, 16)
            sp.dma_start(X[:, :, META:L], A["xt"]).then_inc(loaded.sem, 16)
            sp.dma_start(X[:, :, 0:META], A["metat"]).then_inc(loaded.sem, 16)
            for i, (src, nk, w) in enumerate(plan[:nslot[0]]):
                if i >= NSLOT:
                    sp.wait_ge(*slot_read[i - NSLOT])
                sp.dma_start(ring[:, i % NSLOT, 0:nk * w].rearrange("p (k n) -> p k n", k=nk), src)\
                    .then_inc(slot_filled[i % NSLOT].sem, 16)
            sp.wait_ge(phase_end, 4 * ends["dve"])
            src = H if stop is None else X
            if dump == "H":
                src = H
            if dump and dump.startswith("arena"):
                a0, nn, tt = [int(v) for v in dump[5:].split(",")]
                sp.dma_start(out[:, 0:nn, 0:tt], view(a0, nn, tt)).then_inc(stored.sem, 16)
                sp.wait_ge(stored.sem, 16)
                return
            sp.dma_start(out, src[:, :, :]).then_inc(stored.sem, 16)
            sp.wait_ge(stored.sem, 16)


SHARED = ["ada_w", "ab_w_in", "ab_w_out", "cd_w_in", "mla_w_uq", "mla_w_ukv", "cd_w_out", "ffn_w_up", "ffn_w_down",
          "w_in_2", "rw_w_up_2", "rw_a_up_2", "rw_g_up_2", "w_out_2", "router_2", "e_w1_2", "e_w3_2", "e_w2_2"]


def kernel(_stop=None, _dump=None, **inputs):
    import concourse.bacc as _bacc
    from concourse.bass_utils import run_bass_kernel_spmd as _run

    nc = _bacc.Bacc("TRN2", target_bir_lowering=False, num_devices=1)
    consts, cat = pack(shape_constants())
    vectors, vat = pack(vector_parts(inputs))
    arrays = {"consts": consts, "vectors": vectors}
    x = np.asarray(inputs["x"])[0]
    arrays["xt"] = np.ascontiguousarray(x.T.reshape(KD, P, SEQ).transpose(1, 0, 2))
    meta = np.asarray(inputs["meta_2"])
    arrays["metat"] = np.ascontiguousarray(meta.T.reshape(KD, P, META).transpose(1, 0, 2))
    for n in SHARED:
        arrays[n] = np.ascontiguousarray(inputs[n])
    A = {n: nc.dram_tensor(f"in_{n}", a.shape, FP32, kind="ExternalInput").ap() for n, a in arrays.items()}
    out = nc.dram_tensor("out_0", (P, KD, L), FP32, kind="ExternalOutput").ap()
    build(nc, A, cat, vat, out, _stop, _dump)
    r = _run(nc, [{f"in_{n}": a for n, a in arrays.items()}], core_ids=[0])
    got = r.results[0]["out_0"]
    return np.ascontiguousarray(got[:, :, META:L].transpose(2, 1, 0).reshape(1, SEQ, D))
```

```python
import concourse.bass as bass
from concourse import mybir
from contextlib import ExitStack
import math
import numpy as np

FP32 = mybir.dt.float32
ALU = mybir.AluOpType
ACT = mybir.ActivationFunctionType
AX = mybir.AxisListType

P = 128
D = 1024
KD = D // P
SEQ = 256
META = 16
L = SEQ + META
TILES = ((0, 128), (128, 128), (256, 16))
EPS = 1e-6
NEG = -1e30
DEPTH = 2
F1 = 2816
KF = F1 // P
HD = 64
BUCKETS = 32
SLOT = 4096
NSLOT = 5
RANK = 256
SPAN = 2 * SEQ - 1


class Count:

    def __init__(self, sem):
        self.sem, self.read = sem, {}

    def next(self, who="", n=1):
        self.read[who] = self.read.get(who, 0) + n
        return self.read[who]



def t5_bucket(dist):
    exact = BUCKETS // 2
    d = np.maximum(dist, 0)
    f = np.maximum(d, exact).astype(np.float32)
    large = exact + (np.log(f / np.float32(exact)) / np.float32(math.log(2048 / exact))
                     * np.float32(BUCKETS - exact)).astype(np.int32)
    return np.where(d < exact, d, np.minimum(large, BUCKETS - 1))


def shape_constants():
    c = {}
    i = np.arange(P)
    c["ident"] = np.eye(P)
    c["ones"] = np.ones((P, P))
    c["ones64"] = (i[:, None] // 64 == i[None, :] // 64).astype(float)
    pos = np.arange(SEQ, dtype=np.float32)
    inv = (1.0 / (np.float32(10000.0) ** (np.arange(0, 32, 2, dtype=np.float32) / np.float32(32)))).astype(np.float32)
    ang = pos[None, :] * inv[:, None]
    c["cos_mla"] = np.concatenate([np.ones((64, SEQ)), np.cos(ang), np.cos(ang)])
    c["sin_mla"] = np.concatenate([np.zeros((64, SEQ)), np.sin(ang), np.sin(ang)])
    rot = np.zeros((96, 96))
    for r in range(16):
        rot[80 + r, 64 + r] = -1.0
        rot[64 + r, 80 + r] = 1.0
    c["rot_mla"] = rot
    inv = (np.float32(10000.0) ** (-np.arange(32, dtype=np.float32) / np.float32(32))).astype(np.float32)
    ang = np.arange(L, dtype=np.float32)[None, :] * inv[:, None]
    c["cos_diff"] = np.tile(np.cos(ang), (4, 1))
    c["sin_diff"] = np.tile(np.sin(ang), (4, 1))
    rot = np.zeros((P, P))
    for g in (0, 64):
        for r in range(32):
            rot[g + 32 + r, g + r] = -1.0
            rot[g + r, g + 32 + r] = 1.0
    c["rot_diff"] = rot
    q, k = i[:, None], np.arange(SEQ)[None, :]
    c["causal"] = np.concatenate([np.where(k <= q + 128, 0.0, NEG), np.where(k <= q, 0.0, NEG)], axis=1)
    dist = SEQ - 1 - np.arange(SPAN)
    hot = (t5_bucket(dist)[None, :] == np.arange(BUCKETS)[:, None]) & (dist >= 0)
    times = np.zeros(SPAN)
    for window, dil in ((128, 1), (512, 4), (2048, 16)):
        times += (dist >= 0) & (dist <= window) & (dist % dil == 0)
    c["hot_moba"] = np.concatenate([hot, np.where(dist >= 0, 0.0, NEG)[None, :]])
    c["hot_dil"] = np.concatenate([hot, np.where(times > 0, np.log(np.maximum(times, 1)), NEG)[None, :]])
    q = np.arange(SEQ)[None, :]
    c["strict"] = np.concatenate([i[:, None] < q, i[:, None] + 128 < q], axis=1).astype(float)
    c["later"] = (i[:, None] >= i[None, :]).astype(float)
    c["before"] = (i[:, None] < i[None, :]).astype(float)
    c["slot_no"] = np.tile(np.arange(34)[None, :], (P, 1))
    same = i[:, None] // 16 == i[None, :] // 16
    s, t = i[:, None], i[None, :]
    c["lt_f"], c["lt_b"] = (same & (s < t)).astype(float), (same & (s > t)).astype(float)
    c["le_fb"] = np.concatenate([same & (s <= t), same & (s >= t)], axis=1).astype(float)
    c["half_of"] = (i[:, None] // 16 % 2 == np.arange(2)[None, :]).astype(float)
    c["chunk_of"] = (i[:, None] // 16 == np.arange(8)[None, :]).astype(float)
    t = np.arange(L)
    c["go_f"] = np.tile((t % 16 != 0).astype(float)[None, :], (P, 1))
    c["go_b"] = np.tile((t % 16 != 15).astype(float)[None, :], (P, 1))
    return {k: np.asarray(v, np.float32) for k, v in c.items()}


def pack(parts):
    at, n = {}, 0
    for name, a in parts.items():
        at[name] = (n, a.shape[1], a.shape[0])
        n += a.shape[1]
    out = np.zeros((P, n), np.float32)
    for name, a in parts.items():
        out[:a.shape[0], at[name][0]:at[name][0] + a.shape[1]] = a
    return out, at


def vector_parts(w):
    def cols(a):
        a = np.asarray(a)
        a = a.reshape(-1, a.shape[-1])
        return a.reshape(a.shape[0] * (a.shape[1] // P), P).T
    parts = {"c": cols(w["c"]), "ada_b": cols(w["ada_b"])}
    for n in ("mix_pre_g", "mix_post_g", "ffn_pre_g", "ffn_post_g", "mla_q_norm_g", "mla_kv_norm_g",
              "ffn_conv_w", "ffn_conv_b", "norm1_g_2", "rw_shift_2", "rw_w0_2", "rw_a0_2", "rw_k_k_2",
              "rw_k_a_2", "rw_r_k_2", "rw_gn_g_2", "rw_gn_b_2", "df_subln_g_2", "gl_gate_b_2", "norm2_g_2",
              "final_g_2"):
        parts[n] = cols(w[n])
    g = np.asarray(w["gl_norm_g_2"])
    parts["gl_norm_g_2"] = np.concatenate([g, g], axis=1).T
    lam = np.asarray(w["df_lam_2"]).reshape(DEPTH * 4, HD).T
    parts["df_lam_2"] = lam
    table = np.asarray(w["rel_bias"]).T
    parts["rel_bias"] = table
    up = np.asarray(w["gl_gate_up_2"])
    gate = np.zeros((32, DEPTH * 2 * P), np.float32)
    for l in range(DEPTH):
        for d in range(2):
            gate[16 * d:16 * d + 16, (2 * l + d) * P:(2 * l + d + 1) * P] = up[l, d]
    parts["gl_gate_up_2"] = gate
    return parts


def build(nc, A, cat, vat, out):
    ctx = ExitStack()
    with ctx:
        def sb(name, shape):
            return ctx.enter_context(nc.sbuf_tensor(name, shape, FP32))

        def sem(name):
            return ctx.enter_context(nc.semaphore(name))

        def signal(name):
            return Count(sem(name))

        X = sb("residual", [P, KD, L])
        H = sb("normed", [P, KD, L])
        S = sb("scratch", [P, KD, L])
        ring = sb("weight_ring", [P, NSLOT, SLOT])
        ncst = A["consts"].shape[1]
        nvec = A["vectors"].shape[1]
        cst = sb("constants", [P, ncst])
        vec = sb("vectors", [P, nvec])
        mod = sb("modulation", [P, DEPTH, 6 * KD])
        gain = sb("gain", [P, 2, KD])
        rstd = sb("rstd", [P, L])
        cond = sb("cond", [P, KD, 32])
        small = sb("small", [P, 64])
        AN = (nc.sbuf_bytes_remaining if not callable(nc.sbuf_bytes_remaining) else nc.sbuf_bytes_remaining()) // 4 - 64

        arena = sb("arena", [P, AN])
        banks = [ctx.enter_context(nc.psum_tensor(f"bank{i}", [P, 512], FP32)) for i in range(8)]
        scratch = nc.dram_tensor("bias_rows", (16, P, 512), FP32, kind="Internal").ap()

        cat["le_f"] = (cat["le_fb"][0], P, P)
        cat["le_b"] = (cat["le_fb"][0] + P, P, P)

        def C(name, rows=None):
            a, n, r = cat[name]
            return cst[0:(rows or r), a:a + n]

        def V(name, j=0, n=1, rows=P):
            a = vat[name][0]
            return vec[0:rows, a + j:a + j + n]

        def view(at, *shape):
            n = int(np.prod(shape))
            assert at + n <= AN, (at, n, AN)
            v = arena[:, at:at + n]
            if len(shape) == 2:
                v = v.rearrange("p (a b) -> p a b", a=shape[0])
            if len(shape) == 3:
                v = v.rearrange("p (a b c) -> p a b c", a=shape[0], b=shape[1])
            return v

        loaded = signal("loaded")
        phase_end = sem("phase_end")
        slot_filled = [signal(f"slot{i}_filled") for i in range(NSLOT)]
        slot_used = signal("slot_used")
        vbank_filled, vbank_emptied = signal("vbank_filled"), signal("vbank_emptied")
        abank_filled, abank_emptied = signal("abank_filled"), signal("abank_emptied")
        squares_ready = signal("squares_ready")
        tile_ready = signal("tile_ready")
        root_ready = signal("root_ready")
        h_ready = signal("h_ready")
        operand_ready = signal("operand_ready")
        aoperand_ready = signal("aoperand_ready")
        logits_ready = signal("logits_ready")
        exp_ready = signal("exp_ready")
        act_ready = signal("act_ready")
        dve_ready = signal("dve_ready")
        rows_ready = signal("rows_ready")
        rows_stored = [signal(f"rows_stored{g}") for g in range(2)]
        bias_loaded = signal("bias_loaded")
        stored = signal("stored")

        for_scalar = signal("for_scalar")
        from_scalar = signal("from_scalar")

        ends = {}

        def end_phase(eng, name):
            ends[name] = ends.get(name, 0) + 1
            eng.drain().then_inc(phase_end, 1)
            eng.wait_ge(phase_end, 4 * ends[name])

        plan = []

        def load_plan(W, c0, w, k0, nk):
            plan.append((W[k0 * P:(k0 + nk) * P, c0:c0 + w].rearrange("(k p) n -> p k n", p=P), nk, w))

        def slot_loads(i):
            return sum(16 * (len(plan[j][0]) if type(plan[j][0]) is list else 1) for j in range(i % NSLOT, i + 1, NSLOT))

        nslot = [0]
        slot_read = {}
        open_slots = []

        def read_with_bank(which="v", at=0):
            slot_read[open_slots.pop(at)] = ((vbank_filled if which == "v" else abank_filled).sem, nfill[which])

        def read_alone(mm):
            mm.then_inc(slot_used.sem, 1)
            slot_read[open_slots.pop(0)] = (slot_used.sem, slot_used.next("pe"))

        def next_slot(pe, nk, w):
            i = nslot[0]
            nslot[0] += 1
            open_slots.append(i)
            assert plan[i][1:] == (nk, w), (i, plan[i][1:], nk, w)
            pe.wait_ge(slot_filled[i % NSLOT].sem, slot_loads(i))
            return ring[:, i % NSLOT, 0:nk * w].rearrange("p (k n) -> p k n", k=nk)

        nfill = {"v": 0, "a": 0}

        def fill_bank(pe, which):
            i = nfill[which]
            nfill[which] += 1
            if i >= 4:
                pe.wait_ge((vbank_emptied if which == "v" else abank_emptied).sem, i - 3)
            return banks[(i % 4) + (4 if which == "a" else 0)]

        ntake = {"v": 0, "a": 0}

        def take_bank(eng, which):
            i = ntake[which]
            ntake[which] += 1
            eng.wait_ge((vbank_filled if which == "v" else abank_filled).sem, i + 1)
            return banks[(i % 4) + (4 if which == "a" else 0)]

        FV, EV = vbank_filled.sem, vbank_emptied.sem
        FA, EA = abank_filled.sem, abank_emptied.sem

        eps, eps_rwkv = small[:, 60:61], small[:, 61:62]

        def norm_scalar(act, src, nk, T, width, tiles=False):
            for k in range(nk):
                if tiles:
                    act.wait_ge(tile_ready.sem, tile_ready.next())
                act.activation(S[:, k, 0:T], src[:, k, :], ACT.Square).then_inc(squares_ready.sem, 1)
            b = take_bank(act, "a")
            act.activation(rstd[:, 0:T], b[:, 0:T], ACT.Sqrt, bias=eps, scale=1.0 / width).then_inc(EA, 1)
            act.drain().then_inc(root_ready.sem, 1)

        def norm_tensor(pe, nk, T):
            b = fill_bank(pe, "a")
            for k in range(nk):
                pe.wait_ge(squares_ready.sem, squares_ready.next())
                mm = pe.matmul(b[:, 0:T], C("ones"), S[:, k, 0:T], start=(k == 0), stop=(k == nk - 1))
            mm.then_inc(FA, 1)

        def norm_vector(dve, T):
            dve.wait_ge(root_ready.sem, root_ready.next())
            dve.reciprocal(rstd[:, 0:T], rstd[:, 0:T])
            dve.drain()

        def head_norm_scalar(act, src, n, width, eps=eps):
            act.wait_ge(latent_ready.sem, latent_ready.next())
            act.activation(S[:, 0:n, :], src, ACT.Square).then_inc(squares_ready.sem, 1)
            for i in range(n):
                b = take_bank(act, "a")
                act.activation(S[:, 4 + i, :], b[:, 0:L], ACT.Sqrt, bias=eps, scale=1.0 / width).then_inc(EA, 1)
                act.drain().then_inc(root_ready.sem, 1)

        def head_norm_tensor(pe, n, ones):
            pe.wait_ge(squares_ready.sem, squares_ready.next())
            for i in range(n):
                b = fill_bank(pe, "a")
                pe.matmul(b[:, 0:L], ones, S[:, i, :], start=True, stop=True).then_inc(FA, 1)

        def head_norm_vector(dve, n):
            dve.drain().then_inc(latent_ready.sem, 1)
            r = S[:, 4:4 + n, :]
            for i in range(n):
                dve.wait_ge(root_ready.sem, root_ready.next())
                dve.reciprocal(r[:, i, :], r[:, i, :])
            dve.drain()
            return r

        def groups(width):
            return [(g, min(512, width - g)) for g in range(0, width, 512)]

        def project_plan(W, width, nk, first=0):
            for g, w in groups(width):
                for k0 in range(0, nk, KD):
                    load_plan(W, first + g, w, k0, min(KD, nk - k0))

        def project_tensor(pe, width, nk, rhs, T, fresh=False):
            for g, w in groups(width):
                tiles = [(m, min(P, w - m)) for m in range(0, w, P)]
                b = [None] * len(tiles)
                for k0 in range(0, nk, KD):
                    n = min(KD, nk - k0)
                    W = next_slot(pe, n, w)
                    for i, (m, mw) in enumerate(tiles):
                        if k0 == 0:
                            b[i] = fill_bank(pe, "v")
                        for k in range(k0, k0 + n):
                            if fresh and g == 0 and i == 0:
                                pe.wait_ge(h_ready.sem, h_ready.next())
                            mm = pe.matmul(b[i][0:mw, 0:T], W[:, k - k0, m:m + mw], rhs(k),
                                           start=(k == 0), stop=(k == nk - 1))
                        if k0 + n == nk:
                            mm.then_inc(FV, 1)
                    if k0 + n == nk:
                        read_with_bank()
                    else:
                        read_alone(mm)

        def project_vector(dve, width, put):
            for m in range(-(-width // P)):
                b = take_bank(dve, "v")
                put(m, min(P, width - m * P), b).then_inc(EV, 1)

        XB = X[:, :, META:L]

        flat = H[:, :, :].rearrange("p a b -> p (a b)")
        arow = [flat[:, 512 * i:512 * (i + 1)] for i in range(2)]
        AG = 6 * D // 512
        astep = {"pe": 0, "dve": 0}

        def ada_plan(i):
            load_plan(A["ada_w"][i // AG], (i % AG) * 512, 512, 0, KD)

        def ada_tensor(pe, more=True, first=False):
            i = astep["pe"]
            if more:
                astep["pe"] += 1
                W = next_slot(pe, KD, 512)
                b = fill_bank(pe, "v")
                for k in range(KD):
                    g = k % 4
                    mm = pe.matmul(b[32 * g:32 * g + 32, :], cond[:, k, :], W[:, k, :], start=(k < 4), stop=(k >= 4),
                                   tile_position=(0, 32 * g))
                mm.then_inc(FV, 1)
                read_with_bank("v", -1)
            if not first:
                pe.wait_ge(row_ready.sem, row_ready.next())
                b = fill_bank(pe, "v")
                for j in range(4):
                    mm = pe.matmul(b[:, j:j + 1], arow[(i - 1) % 2][:, j * P:(j + 1) * P], C("ones")[:, 0:1], start=True, stop=True)
                mm.then_inc(FV, 1)

        def ada_vector(dve, more=True, first=False):
            i = astep["dve"]
            if more:
                astep["dve"] += 1
                b = take_bank(dve, "v")
                dve.tensor_copy(arow[i % 2], b[:, :]).then_inc(EV, 1)
                dve.drain().then_inc(row_ready.sem, 1)
            if not first:
                b = take_bank(dve, "v")
                l, g = divmod(i - 1, AG)
                dve.tensor_tensor(mod[:, l, 4 * g:4 * g + 4], b[:, 0:4], V("ada_b", l * 6 * KD + 4 * g, 4), ALU.add)\
                    .then_inc(EV, 1)

        row_ready = signal("row_ready")

        scaled_ready = signal("scaled_ready")
        ada_slots = []
        LATER = (6, 7, 7)
        assert sum(LATER) == DEPTH * AG - 4

        def later_ada_tensor(pe):
            ada_slots.append(nslot[0])
            astep["pe"] += 1
            W = next_slot(pe, KD, 512)
            pe.wait_ge(scaled_ready.sem, scaled_ready.next())
            b = fill_bank(pe, "v")
            for j in range(4):
                mm = pe.matmul(b[:, j:j + 1], W[:, 0, j * P:(j + 1) * P], C("ones")[:, 0:1], start=True, stop=True)
            mm.then_inc(FV, 1)
            read_with_bank("v", -1)

        def later_ada_vector(dve):
            l, g = divmod(astep["dve"], AG)
            astep["dve"] += 1
            b = take_bank(dve, "v")
            dve.tensor_tensor(mod[:, l, 4 * g:4 * g + 4], b[:, 0:4], V("ada_b", l * 6 * KD + 4 * g, 4), ALU.add)\
                .then_inc(EV, 1)

        def later_ada_pool(pool, n):
            for _ in range(n):
                i = ada_slots.pop(0)
                W = ring[:, i % NSLOT, :].rearrange("p (k n) -> p k n", k=KD)
                pool.wait_ge(slot_filled[i % NSLOT].sem, slot_loads(i))
                pool.tensor_tensor(W, W, cond[:, :, 0:1].to_broadcast([P, KD, 512]), ALU.mult)
                for half in (4, 2, 1):
                    pool.drain()
                    pool.tensor_tensor(W[:, 0:half, :], W[:, 0:half, :], W[:, half:2 * half, :], ALU.add)
                pool.drain().then_inc(scaled_ready.sem, 1)

        def start_tensor(pe):
            bias_tensor(pe)
            norm_tensor(pe, KD, SEQ)
            pe.wait_ge(aoperand_ready.sem, aoperand_ready.next())
            for i in range(4):
                ada_tensor(pe, first=(i == 0))
            ada_tensor(pe, more=False)

        def start_vector(dve):
            dve.wait_ge(loaded.sem, 16 * 4)
            dve.memset(cond[:, :, :], 0.0)
            dve.memset(eps, EPS)
            dve.memset(eps_rwkv, 64e-5)
            dve.drain().then_inc(for_scalar.sem, 1)
            bias_vector(dve)
            for i in range(4):
                ada_vector(dve, first=(i == 0))
            ada_vector(dve, more=False)

        def start_scalar(act):
            act.wait_ge(for_scalar.sem, for_scalar.next())
            act.activation(cond[:, :, 0], V("c", 0, KD), ACT.Silu).then_inc(aoperand_ready.sem, 1)

        def modulation(l, what):
            return mod[:, l, what * KD:(what + 1) * KD]

        def pre_norm_vector(dve, l, g, shift, scale):
            dve.scalar_tensor_tensor(out=gain[:, 0, :], in0=modulation(l, scale), scalar=1.0,
                                     in1=V(g, l * KD, KD), op0=ALU.add, op1=ALU.mult)
            norm_vector(dve, SEQ)
            dve.tensor_tensor(S[:, :, 0:SEQ], XB, rstd[:, 0:SEQ].unsqueeze(1).to_broadcast([P, KD, SEQ]), ALU.mult)
            dve.drain()
            for k in range(KD):
                dve.tensor_scalar(H[:, k, 0:SEQ], S[:, k, 0:SEQ], gain[:, 0, k:k + 1], modulation(l, shift)[:, k:k + 1],
                                  ALU.mult, ALU.add).then_inc(h_ready.sem, 1)

        def project_y_vector(dve):
            for m in range(KD):
                b = take_bank(dve, "v")
                dve.tensor_copy(H[:, m, 0:SEQ], b[:, 0:SEQ]).then_inc(EV, 1)
                dve.drain().then_inc(tile_ready.sem, 1)

        def post_norm_vector(dve, l, g, gate):
            dve.tensor_tensor(gain[:, 0, :], modulation(l, gate), V(g, l * KD, KD), ALU.mult)
            norm_vector(dve, SEQ)
            dve.tensor_tensor(H[:, :, 0:SEQ], H[:, :, 0:SEQ], rstd[:, 0:SEQ].unsqueeze(1).to_broadcast([P, KD, SEQ]), ALU.mult)
            dve.drain()
            for k in range(KD):
                dve.scalar_tensor_tensor(out=XB[:, k, :], in0=H[:, k, 0:SEQ], scalar=gain[:, 0, k:k + 1],
                                         in1=XB[:, k, :], op0=ALU.mult, op1=ALU.add).then_inc(tile_ready.sem, 1)

        hrhs = lambda T: (lambda k: H[:, k, 0:T])

        HALVES = (slice(0, SEQ), slice(SEQ, SEQ + P))

        def attend_tensor(pe, n, q, k, vtok, beside=None):
            for i in range(n + 3):
                if i < n:
                    b = fill_bank(pe, "v")
                    pe.matmul(b[:, HALVES[0]], q(i)[:, P:2 * P], k(i), start=True, stop=True)
                    pe.matmul(b[:, HALVES[1]], q(i)[:, 0:P], k(i)[:, 0:P], start=True, stop=True).then_inc(FV, 1)
                if 2 <= i < n + 2:
                    x = att_l[:, (i - 2) % 3, :]
                    pe.wait_ge(operand_ready.sem, operand_ready.next())
                    b = fill_bank(pe, "a")
                    for j, a in enumerate((SEQ, 0, P)):
                        mm = pe.transpose(b[:, j * P:(j + 1) * P], x[:, a:a + P], C("ident"))
                    mm.then_inc(FA, 1)
                if i >= 3:
                    h = i - 3
                    x = att_pt[:, h % 2, :]
                    pe.wait_ge(aoperand_ready.sem, aoperand_ready.next())
                    b = fill_bank(pe, "v")
                    r = slice(64 * (h % 2), 64 * (h % 2) + 64)
                    pe.matmul(b[r, 0:SEQ], vtok(h, 0), x[:, 0:SEQ], start=True, stop=False)
                    pe.matmul(b[r, P:SEQ], vtok(h, 1), x[:, SEQ:SEQ + P], start=False, stop=True).then_inc(FV, 1)
                if beside:
                    beside(i)

        def attend_vector(dve, n, scale, bias, put, beside=None):
            for i in range(n + 3):
                if i < n:
                    o = 8 * (i % 3)
                    x = att_l[:, i % 3, :]
                    b = take_bank(dve, "v")
                    dve.scalar_tensor_tensor(out=x, in0=b[:, 0:SEQ + P], scalar=scale, in1=bias(i)[:, 0:SEQ + P],
                                             op0=ALU.mult, op1=ALU.add).then_inc(EV, 1)
                    dve.drain()
                    for j, c in enumerate(HALVES):
                        dve.tensor_reduce(small[:, o + j:o + j + 1], x[:, c], AX.X, ALU.max)
                    dve.drain()
                    dve.tensor_scalar(small[:, o:o + 2], small[:, o:o + 2], -1.0, None, ALU.mult).then_inc(logits_ready.sem, 1)
                if 1 <= i <= n:
                    o = 8 * ((i - 1) % 3)
                    x = att_l[:, (i - 1) % 3, :]
                    dve.wait_ge(exp_ready.sem, exp_ready.next())
                    dve.reciprocal(small[:, o + 4:o + 6], small[:, o + 2:o + 4])
                    dve.drain()
                    for j, c in enumerate(HALVES):
                        ins = dve.tensor_scalar(x[:, c], x[:, c], small[:, o + 4 + j:o + 5 + j], None, ALU.mult)
                    ins.then_inc(operand_ready.sem, 1)
                if i >= 3:
                    h = i - 3
                    b = take_bank(dve, "v")
                    dve.tensor_copy(put(h), b[64 * (h % 2):64 * (h % 2) + 64, 0:SEQ]).then_inc(EV, 1)
                if beside:
                    beside(i)

        def attend_scalar(act, n):
            for i in range(n + 2):
                if i < n:
                    o = 8 * (i % 3)
                    act.wait_ge(logits_ready.sem, logits_ready.next())
                    for j, c in enumerate(HALVES):
                        x = att_l[:, i % 3, c]
                        ins = act.activation(x, x, ACT.Exp, bias=small[:, o + j:o + j + 1],
                                             accum_out=small[:, o + 2 + j:o + 3 + j])
                    ins.then_inc(exp_ready.sem, 1)
                if i >= 2:
                    b = take_bank(act, "a")
                    act.activation(att_pt[:, i % 2, :], b[:, 0:SEQ + P], ACT.Copy).then_inc(EA, 1)
                    act.drain().then_inc(aoperand_ready.sem, 1)

        def turn_values_tensor(pe, n):
            pe.wait_ge(operand_ready.sem, operand_ready.next())
            for m in range(n):
                b = fill_bank(pe, "a")
                for t in range(2):
                    mm = pe.transpose(b[:, t * P:(t + 1) * P], S[:, m, t * P:(t + 1) * P], C("ident"))
                mm.then_inc(FA, 1)

        def turn_values_scalar(act, n):
            for m in range(n):
                b = take_bank(act, "a")
                act.activation(att_v[:, :, m * P:(m + 1) * P], b[:, 0:2 * P].rearrange("p (t f) -> p t f", t=2),
                               ACT.Copy).then_inc(EA, 1)
            act.drain().then_inc(aoperand_ready.sem, 1)

        att_q = view(0, 8, SEQ)
        att_k = view(8 * SEQ, 8, SEQ)
        att_v = view(16 * SEQ, 2, D)
        att_l = view(24 * SEQ, 3, SEQ + P)
        att_pt = view(29 * SEQ, 2, SEQ + P)
        att_b = view(32 * SEQ, 16, 2 * SEQ)
        table = sb("bias_table", [BUCKETS + 1, 16])

        def bias_vector(dve):
            dve.memset(table[:, :], 1.0)
            dve.drain()
            dve.tensor_copy(table[0:BUCKETS, :], V("rel_bias", 0, 16, rows=BUCKETS)).then_inc(operand_ready.sem, 1)
            for g in range(2):
                b = take_bank(dve, "v")
                dve.tensor_copy(att_b[0:8, 8 * g, 0:SPAN], b[0:8, 0:SPAN]).then_inc(EV, 1)
                dve.drain().then_inc(rows_ready.sem, 1)

        def bias_tensor(pe):
            pe.wait_ge(operand_ready.sem, operand_ready.next())
            for g, hot in enumerate(("hot_moba", "hot_dil")):
                b = fill_bank(pe, "v")
                pe.matmul(b[0:8, 0:SPAN], table[:, 8 * g:8 * g + 8], C(hot), start=True, stop=True).then_inc(FV, 1)

        def bias_pool(pool):
            for g in range(2):
                pool.wait_ge(rows_ready.sem, rows_ready.next())
                pool.dma_start(scratch[8 * g:8 * g + 8, :, 0:SPAN],
                               att_b[0:8, 8 * g, 0:SPAN].unsqueeze(1).to_broadcast([8, P, SPAN])).then_inc(rows_stored[g].sem, 16)
            for g in range(2):
                pool.wait_ge(rows_stored[g].sem, 16)
                for h in range(8 * g, 8 * g + 8):
                    skew = bass.AP(tensor=scratch.tensor, offset=scratch.offset + h * P * 512 + P - 1,
                                   ap=[[511, P], [P, 2], [1, SEQ]])
                    pool.dma_start(att_b[:, h, :].rearrange("p (j k) -> p j k", j=2), skew).then_inc(bias_loaded.sem, 16)

        def even_put(dve):
            def put(m, rows, b):
                part, i = m // 4, m % 4
                half, kind = part // 3, part % 3
                if kind == 2:
                    return dve.tensor_copy(S[:, half * 4 + i, 0:SEQ], b[:, 0:SEQ])
                return dve.tensor_copy((att_q, att_k)[kind][:, half * 4 + i, :], b[:, 0:SEQ])
            return put

        def ada_beside_heads(step, eng):
            return lambda i: step(eng) if i % 3 == 2 else None

        def head_rows(buf):
            return lambda h: buf[64 * (h % 2):64 * (h % 2) + 64, h // 2, :]

        hid = view(0, KF, SEQ)
        conv = view(KF * SEQ, 4, SEQ)

        def ffn_plan(l):
            W = A["ffn_w_up"][l].rearrange("(k p) n -> p k n", p=P)
            for g in range(0, F1, 2 * P):
                plan.append(([W[:, :, c:c + 2 * P] for c in (g, F1 + g)], 2 * KD, 2 * P))
                for i in (g // P, g // P + 1):
                    if l == 0 and ada_beside(i):
                        ada_plan(4 + LATER[0] + i // 3)
            project_plan(A["ffn_w_down"][l], D, KF)

        def ada_beside(i):
            return i % 3 == 2

        def ffn_tensor(pe, l):
            for g in range(0, F1, 2 * P):
                W = next_slot(pe, 2 * KD, 2 * P)
                for m in (0, P):
                    for part in range(2):
                        b = fill_bank(pe, "v")
                        for k in range(KD):
                            if g + m + part == 0:
                                pe.wait_ge(h_ready.sem, h_ready.next())
                            mm = pe.matmul(b[:, 0:SEQ], W[:, part * KD + k, m:m + P], H[:, k, 0:SEQ],
                                           start=(k == 0), stop=(k == KD - 1))
                        mm.then_inc(FV, 1)
                    if m:
                        read_with_bank()
                    if l == 0 and ada_beside((g + m) // P):
                        later_ada_tensor(pe)
            pe.wait_ge(operand_ready.sem, operand_ready.next())
            project_tensor(pe, D, KF, lambda k: hid[:, k, :], SEQ)

        def ffn_scalar(act, l):
            for i in range(KF):
                for part in range(2):
                    m = part * KF + i
                    n = ffn_taken[0]
                    ffn_taken[0] += 1
                    act.wait_ge(vbank_filled.sem, ntake_ffn(n))
                    if i >= 2:
                        act.wait_ge(dve_ready.sem, dve_ready_at(i, l))
                    act.activation(conv[:, 2 * (i % 2) + part, :], banks[(ntake_ffn(n) - 1) % 4][:, 0:SEQ], ACT.Identity,
                                   bias=V("ffn_conv_b", l * 44 + m),
                                   scale=V("ffn_conv_w", (l * 3 + 2) * 44 + m)).then_inc(act_ready.sem, 1)
                if i >= 1:
                    gelu_scalar(act, i - 1, l)
            gelu_scalar(act, KF - 1, l)

        def gelu_scalar(act, i, l):
            act.wait_ge(logits_ready.sem, logits_ready.next())
            act.activation(conv[:, 2 * (i % 2), :], conv[:, 2 * (i % 2), :], ACT.Gelu_apprx_tanh)\
                .then_inc(exp_ready.sem, 1)

        ffn_taken = [0]
        ffn_first = {}

        def ntake_ffn(n):
            l, j = divmod(n, 2 * KF)
            before = 0
            if l == 0:
                before = sum(ada_beside(i) for i in range(j // 2))
            return ffn_first[l] + j + before + 1

        def dve_ready_at(i, l):
            return l * KF + i - 1

        def ffn_vector(dve, l):
            def product(i):
                dve.wait_ge(exp_ready.sem, exp_ready.next())
                dve.tensor_tensor(hid[:, i, :], conv[:, 2 * (i % 2), :], conv[:, 2 * (i % 2) + 1, :], ALU.mult)\
                    .then_inc(dve_ready.sem, 1)
            for i in range(KF):
                for part in range(2):
                    m = part * KF + i
                    b = take_bank(dve, "v")
                    c = conv[:, 2 * (i % 2) + part, :]
                    dve.wait_ge(act_ready.sem, act_ready.next())
                    dve.scalar_tensor_tensor(out=c[:, 1:SEQ], in0=b[:, 0:SEQ - 1], scalar=V("ffn_conv_w", (l * 3 + 1) * 44 + m),
                                             in1=c[:, 1:SEQ], op0=ALU.mult, op1=ALU.add)
                    dve.drain()
                    dve.scalar_tensor_tensor(out=c[:, 2:SEQ], in0=b[:, 0:SEQ - 2], scalar=V("ffn_conv_w", l * 3 * 44 + m),
                                             in1=c[:, 2:SEQ], op0=ALU.mult, op1=ALU.add).then_inc(EV, 1)
                dve.drain().then_inc(logits_ready.sem, 1)
                if i >= 1:
                    product(i - 1)
                if l == 0 and ada_beside(i):
                    later_ada_vector(dve)
            product(KF - 1)
            dve.drain().then_inc(operand_ready.sem, 1)
            project_y_vector(dve)

        NR = 96
        cq = view(0, 4, SEQ)
        krope = view(4 * SEQ, SEQ)
        qfull = view(5 * SEQ, 8, SEQ)
        kfull = view(13 * SEQ, 8, SEQ)
        stick_q = view(64 * SEQ, 4, SEQ)
        odd_v = view(32 * SEQ, 2, D)
        stick_k = view(40 * SEQ, 4, SEQ)
        odd_o = view(44 * SEQ, 8, SEQ)
        stick_z = view(52 * SEQ, 3, 2 * SEQ)
        stick_t = view(58 * SEQ, 2, 2 * SEQ)
        rope_t = view(62 * SEQ, 2, SEQ)

        def odd_plan():
            W = A["cd_w_in"][0]
            load_plan(W, 0, 512, 0, KD)
            load_plan(W, 512, 32, 0, KD)
            for g in range(2):
                load_plan(A["mla_w_uq"][0], g * 4 * NR, 4 * NR, 0, 2)
            for g in range(2):
                load_plan(A["mla_w_ukv"][0], g * 512, 512, 0, 2)
            project_plan(W, 1536, KD, 544)
            for i in range(DEPTH * AG - LATER[2], DEPTH * AG):
                ada_plan(i)
            project_plan(A["cd_w_out"][0], D, KD)

        def odd_tensor(pe):
            project_tensor(pe, 512, KD, hrhs(SEQ), SEQ, fresh=True)
            W = next_slot(pe, KD, 32)
            b = fill_bank(pe, "v")
            for k in range(KD):
                mm = pe.matmul(b[64:96, 0:SEQ], W[:, k, :], H[:, k, 0:SEQ], start=(k == 0), stop=(k == KD - 1))
            mm.then_inc(FV, 1)
            read_with_bank()
            pe.wait_ge(operand_ready.sem, operand_ready.next())
            b = fill_bank(pe, "v")
            pe.matmul(b[64:96, 0:SEQ], C("rot_mla")[64:96, 64:96], krope[64:96, :], start=True, stop=True).then_inc(FV, 1)
            norm_tensor(pe, 2, SEQ)
            norm_tensor(pe, 2, SEQ)
            pe.wait_ge(operand_ready.sem, operand_ready.next())
            for g in range(2):
                W = next_slot(pe, 2, 4 * NR)
                for h in range(4):
                    b = fill_bank(pe, "v")
                    for k in range(2):
                        mm = pe.matmul(b[0:NR, 0:SEQ], W[:, k, h * NR:(h + 1) * NR], cq[:, k, :], start=(k == 0), stop=(k == 1))
                    mm.then_inc(FV, 1)
                read_with_bank()
            pe.wait_ge(operand_ready.sem, operand_ready.next())
            for h in range(8):
                b = fill_bank(pe, "v")
                pe.matmul(b[0:NR, 0:SEQ], C("rot_mla"), qfull[0:NR, h, :], start=True, stop=True).then_inc(FV, 1)
            for g in range(2):
                W = next_slot(pe, 2, 512)
                W4 = W.rearrange("p k (h f) -> p k h f", h=4)
                for h in range(4):
                    b = fill_bank(pe, "v")
                    for k in range(2):
                        mm = pe.matmul(b[0:HD, 0:SEQ], W[:, k, h * P:h * P + HD], cq[:, 2 + k, :], start=(k == 0), stop=(k == 1))
                    mm.then_inc(FV, 1)
                for t in range(2):
                    b = fill_bank(pe, "v")
                    for k in range(2):
                        mm = pe.matmul(b[:, 0:SEQ].rearrange("p (h f) -> p h f", h=4), cq[:, 2 + k, t * P:(t + 1) * P],
                                       W4[:, k, :, HD:P], start=(k == 0), stop=(k == 1))
                    mm.then_inc(FV, 1)
                read_with_bank()
            project_tensor(pe, 1536, KD, hrhs(SEQ), SEQ)
            turn_values_tensor(pe, 4)
            pe.wait_ge(aoperand_ready.sem, aoperand_ready.next())
            later_ada_tensor(pe)
            attend_tensor(pe, 8, lambda h: qfull[0:NR, h, :], lambda h: kfull[0:NR, h, :],
                          lambda h, t: odd_v[:, t, h * HD:(h + 1) * HD], ada_beside_heads(later_ada_tensor, pe))
            stick_tensor(pe, ada_beside_heads(later_ada_tensor, pe))
            pe.wait_ge(operand_ready.sem, operand_ready.next())
            project_tensor(pe, D, KD, lambda k: odd_o[:, k, :], SEQ)

        def odd_vector(dve):
            project_vector(dve, 512, lambda m, rows, b: dve.tensor_copy(cq[:, m, :], b[:, 0:SEQ]))
            b = take_bank(dve, "v")
            r = slice(64, 96)
            dve.tensor_copy(krope[r, :], b[r, 0:SEQ]).then_inc(EV, 1)
            dve.drain().then_inc(operand_ready.sem, 1)
            b = take_bank(dve, "v")
            dve.tensor_tensor(rope_t[r, 0, :], b[r, 0:SEQ], C("sin_mla")[r, :], ALU.mult).then_inc(EV, 1)
            dve.tensor_tensor(krope[r, :], krope[r, :], C("cos_mla")[r, :], ALU.mult)
            dve.drain()
            for h in range(8):
                dve.tensor_tensor(kfull[r, h, :], krope[r, :], rope_t[r, 0, :], ALU.add)
            for part, g in ((0, "mla_q_norm_g"), (1, "mla_kv_norm_g")):
                dve.drain().then_inc(latent_ready.sem, 1)
                norm_vector(dve, SEQ)
                for k in range(2):
                    dve.scalar_tensor_tensor(out=cq[:, 2 * part + k, :], in0=cq[:, 2 * part + k, :], scalar=V(g, k),
                                             in1=rstd[:, 0:SEQ], op0=ALU.mult, op1=ALU.mult)
            dve.drain().then_inc(operand_ready.sem, 1)
            for h in range(8):
                b = take_bank(dve, "v")
                dve.tensor_copy(qfull[0:NR, h, :], b[0:NR, 0:SEQ]).then_inc(EV, 1)
            dve.drain().then_inc(operand_ready.sem, 1)
            for h in range(8):
                b = take_bank(dve, "v")
                t = rope_t[0:NR, h % 2, :]
                dve.tensor_tensor(t, b[0:NR, 0:SEQ], C("sin_mla"), ALU.mult).then_inc(EV, 1)
                dve.tensor_tensor(qfull[0:NR, h, :], qfull[0:NR, h, :], C("cos_mla"), ALU.mult)
                dve.drain()
                dve.tensor_tensor(qfull[0:NR, h, :], qfull[0:NR, h, :], t, ALU.add)
            for g in range(2):
                for h in range(4 * g, 4 * g + 4):
                    b = take_bank(dve, "v")
                    dve.tensor_copy(kfull[0:HD, h, :], b[0:HD, 0:SEQ]).then_inc(EV, 1)
                for t in range(2):
                    b = take_bank(dve, "v")
                    dve.tensor_copy(odd_v[:, t, g * SEQ:(g + 1) * SEQ], b[:, 0:SEQ]).then_inc(EV, 1)

            def put(m, rows, b):
                if m < 4:
                    return dve.tensor_scalar(stick_q[:, m, :], b[:, 0:SEQ], HD ** -0.5, None, ALU.mult)
                if m < 8:
                    return dve.tensor_copy(stick_k[:, m - 4, :], b[:, 0:SEQ])
                return dve.tensor_copy(S[:, m - 8, 0:SEQ], b[:, 0:SEQ])
            project_vector(dve, 1536, put)
            dve.drain().then_inc(operand_ready.sem, 1)
            later_ada_vector(dve)
            attend_vector(dve, 8, NR ** -0.5, lambda h: C("causal"), head_rows(odd_o), ada_beside_heads(later_ada_vector, dve))
            stick_vector(dve, ada_beside_heads(later_ada_vector, dve))
            dve.drain().then_inc(operand_ready.sem, 1)
            project_y_vector(dve)

        def odd_scalar(act):
            for part in range(2):
                act.wait_ge(latent_ready.sem, latent_ready.next())
                norm_scalar(act, cq[:, 2 * part:2 * part + 2, :], 2, SEQ, RANK)
            for m in range(4):
                b = take_bank(act, "a")
                act.activation(odd_v[:, :, 512 + m * P:512 + (m + 1) * P], b[:, 0:2 * P].rearrange("p (t f) -> p t f", t=2),
                               ACT.Copy).then_inc(EA, 1)
            act.drain().then_inc(aoperand_ready.sem, 1)
            attend_scalar(act, 8)
            stick_scalar(act)

        latent_ready = signal("latent_ready")
        score_ready = signal("score_ready")
        log_ready = signal("log_ready")
        rest_ready = signal("rest_ready")
        share_ready = signal("share_ready")

        def stick_tensor(pe, beside):
            qh, kh = head_rows(stick_q), head_rows(stick_k)
            for i in range(8 + 2):
                if i < 8:
                    b = fill_bank(pe, "v")
                    for kt in range(2):
                        mm = pe.matmul(b[:, kt * SEQ:(kt + 1) * SEQ], kh(i)[:, kt * P:(kt + 1) * P], qh(i), start=True, stop=True)
                    mm.then_inc(FV, 1)
                if 1 <= i <= 8:
                    t = stick_t[:, (i - 1) % 2, :]
                    pe.wait_ge(operand_ready.sem, operand_ready.next())
                    b = fill_bank(pe, "v")
                    pe.matmul(b[:, 0:SEQ], C("later"), t[:, 0:SEQ], start=True, stop=False)
                    pe.matmul(b[:, 0:SEQ], C("ones"), t[:, SEQ:], start=False, stop=True)
                    pe.matmul(b[:, SEQ:], C("later"), t[:, SEQ:], start=True, stop=True).then_inc(FV, 1)
                if i >= 2:
                    h = i - 2
                    pe.wait_ge(operand_ready.sem, operand_ready.next())
                    b = fill_bank(pe, "v")
                    for kt in range(2):
                        mm = pe.matmul(b[64 * (h % 2):64 * (h % 2) + 64, 0:SEQ], odd_v[:, kt, 512 + h * HD:512 + (h + 1) * HD],
                                       stick_z[:, h % 3, kt * SEQ:(kt + 1) * SEQ], start=(kt == 0), stop=(kt == 1))
                    mm.then_inc(FV, 1)
                beside(i)

        def stick_vector(dve, beside):
            for i in range(8 + 2):
                if i < 8:
                    b = take_bank(dve, "v")
                    dve.tensor_tensor(stick_z[:, i % 3, :], b[:, :], C("strict"), ALU.mult).then_inc(EV, 1)
                    dve.drain().then_inc(score_ready.sem, 1)
                if 1 <= i <= 8:
                    t, z = stick_t[:, (i - 1) % 2, :], stick_z[:, (i - 1) % 3, :]
                    dve.wait_ge(log_ready.sem, log_ready.next())
                    dve.scalar_tensor_tensor(out=t, in0=z, scalar=0.0, in1=t, op0=ALU.max, op1=ALU.add)
                    dve.drain()
                    dve.tensor_tensor(t, t, C("strict"), ALU.mult).then_inc(operand_ready.sem, 1)
                if i >= 2:
                    z = stick_z[:, (i - 2) % 3, :]
                    dve.wait_ge(share_ready.sem, share_ready.next())
                    dve.tensor_tensor(z, z, C("strict"), ALU.mult).then_inc(operand_ready.sem, 1)
                if 1 <= i <= 8:
                    z = stick_z[:, (i - 1) % 3, :]
                    b = take_bank(dve, "v")
                    dve.tensor_tensor(z, z, b[:, :], ALU.subtract).then_inc(EV, 1)
                    dve.drain().then_inc(rest_ready.sem, 1)
                if i >= 2:
                    h = i - 2
                    b = take_bank(dve, "v")
                    dve.tensor_copy(odd_o[64 * (h % 2):64 * (h % 2) + 64, 4 + h // 2, :],
                                    b[64 * (h % 2):64 * (h % 2) + 64, 0:SEQ]).then_inc(EV, 1)
                beside(i)

        def stick_scalar(act):
            for i in range(8 + 1):
                if i < 8:
                    t = stick_t[:, i % 2, :]
                    act.wait_ge(score_ready.sem, score_ready.next())
                    act.activation(t, stick_z[:, i % 3, :], ACT.Abs)
                    act.drain()
                    act.activation(t, t, ACT.Exp, scale=-1.0)
                    act.drain()
                    act.activation(t, t, ACT.Ln, bias=1.0).then_inc(log_ready.sem, 1)
                if i >= 1:
                    act.wait_ge(rest_ready.sem, rest_ready.next())
                    z = stick_z[:, (i - 1) % 3, :]
                    act.activation(z, z, ACT.Exp).then_inc(share_ready.sem, 1)

        Q = L
        NIN = A["w_in_2"].shape[2]
        MIN = -(-NIN // P)
        proj = view(0, MIN, L)
        A_T, B_T, C_T = 0, 9, 21
        CH = 16
        NCH = L // CH


        def gain_norm_vector(dve, g, l, n=KD):
            norm_vector(dve, L)
            for k in range(KD):
                dve.scalar_tensor_tensor(out=H[:, k, :], in0=X[:, k, :], scalar=V(g, l * KD + k), in1=rstd[:, :],
                                         op0=ALU.mult, op1=ALU.mult).then_inc(h_ready.sem, 1)

        def second_in_plan(l):
            project_plan(A["w_in_2"][l], NIN, KD)

        def second_in_tensor(pe):
            project_tensor(pe, NIN, KD, lambda k: H[:, k, :], L, fresh=True)

        def second_in_vector(dve, l):
            gain_norm_vector(dve, "norm1_g_2", l)
            mu = lambda s: V("rw_shift_2", (2 * l + s) * 9, 9)
            c0 = small[:, 40:49]
            dve.tensor_tensor(c0, mu(0), mu(1), ALU.add)
            dve.drain()
            dve.tensor_scalar(c0, c0, -1.0, 1.0, ALU.mult, ALU.add)
            dve.drain()

            def put(m, rows, b):
                y = proj[0:rows, m, :]
                if m >= B_T:
                    return dve.tensor_copy(y, b[0:rows, 0:L])
                dve.tensor_scalar(y, b[:, 0:L], c0[:, m:m + 1], None, ALU.mult)
                dve.drain()
                dve.scalar_tensor_tensor(out=y[:, 1:], in0=b[:, 0:L - 1], scalar=mu(0)[:, m:m + 1], in1=y[:, 1:],
                                         op0=ALU.mult, op1=ALU.add)
                dve.drain()
                return dve.scalar_tensor_tensor(out=y[:, 0:L - 1], in0=b[:, 1:L], scalar=mu(1)[:, m:m + 1],
                                                in1=y[:, 0:L - 1], op0=ALU.mult, op1=ALU.add)
            project_vector(dve, NIN, put)

        DB = MIN * Q
        diff_v = view(DB, 3, 512)
        diff_e = view(DB + 1536, 3, 2, L)
        diff_t = view(DB + 1536 + 6 * L, 2, 3 * P)
        diff_r = view(DB + 1536 + 6 * L + 6 * P, 2, L)
        UNITS = [(h, t) for h in range(4) for t in range(3)]

        def diff_tensor(pe):
            for m in range(8):
                b = fill_bank(pe, "v")
                pe.matmul(b[:, 0:L], C("rot_diff"), proj[:, B_T + m, :], start=True, stop=True).then_inc(FV, 1)
            for t, (t0, n) in enumerate(TILES):
                b = fill_bank(pe, "a")
                for m in range(4):
                    mm = pe.transpose(b[0:n, m * P:(m + 1) * P], proj[:, B_T + 8 + m, t0:t0 + n], C("ident"))
                mm.then_inc(FA, 1)
            pe.wait_ge(operand_ready.sem, operand_ready.next())
            b = fill_bank(pe, "v")
            pe.matmul(b[:, 0:2], C("ones")[0:HD, :], small[0:HD, 32:34], start=True, stop=True).then_inc(FV, 1)
            for i in range(len(UNITS) + 3):
                if i < len(UNITS):
                    h, t = UNITS[i]
                    t0, n = TILES[t]
                    for c in range(2):
                        r = slice(64 * c, 64 * c + 64)
                        b = fill_bank(pe, "v")
                        pe.matmul(b[0:n, 0:L], proj[r, B_T + h, t0:t0 + n], proj[r, B_T + 4 + h, :], start=True, stop=True)\
                            .then_inc(FV, 1)
                if 2 <= i < len(UNITS) + 2:
                    h, t = UNITS[i - 2]
                    n = TILES[t][1]
                    pe.wait_ge(operand_ready.sem, operand_ready.next())
                    b = fill_bank(pe, "a")
                    for kt, (k0, kn) in enumerate(TILES):
                        mm = pe.transpose(b[0:kn, kt * P:kt * P + n], diff_e[0:n, (i - 2) % 3, 0, k0:k0 + kn],
                                          C("ident")[0:n, 0:n])
                    mm.then_inc(FA, 1)
                if i >= 3:
                    h, t = UNITS[i - 3]
                    n = TILES[t][1]
                    pe.wait_ge(aoperand_ready.sem, aoperand_ready.next())
                    b = fill_bank(pe, "v")
                    for kt, (k0, kn) in enumerate(TILES):
                        mm = pe.matmul(b[:, 0:n], diff_v[0:kn, kt, h * P:(h + 1) * P],
                                       diff_t[0:kn, (i - 3) % 2, kt * P:kt * P + n], start=(kt == 0), stop=(kt == 2))
                    mm.then_inc(FV, 1)
            head_norm_tensor(pe, 4, C("ones"))

        def diff_vector(dve, l):
            lam_init = 0.8 - 0.6 * math.exp(-0.3 * l)
            for m in range(8):
                b = take_bank(dve, "v")
                dve.tensor_tensor(diff_r[:, m % 2, :], b[:, 0:L], C("sin_diff"), ALU.mult).then_inc(EV, 1)
                dve.tensor_tensor(proj[:, B_T + m, :], proj[:, B_T + m, :], C("cos_diff"), ALU.mult)
                dve.drain()
                dve.tensor_tensor(proj[:, B_T + m, :], proj[:, B_T + m, :], diff_r[:, m % 2, :], ALU.add)
            for j in range(2):
                dve.tensor_tensor(small[0:HD, 32 + j:33 + j], V("df_lam_2", 4 * l + 2 * j, 1, HD),
                                  V("df_lam_2", 4 * l + 2 * j + 1, 1, HD), ALU.mult)
            dve.drain().then_inc(operand_ready.sem, 1)
            b = take_bank(dve, "v")
            dve.tensor_copy(small[:, 34:36], b[:, 0:2]).then_inc(EV, 1)
            dve.drain().then_inc(for_scalar.sem, 1)
            dve.wait_ge(from_scalar.sem, from_scalar.next())
            dve.tensor_tensor(small[:, 36:37], small[:, 35:36], small[:, 34:35], ALU.subtract)
            dve.drain()
            dve.tensor_scalar(small[:, 36:37], small[:, 36:37], -lam_init, None, ALU.add)
            dve.drain()
            for i in range(len(UNITS) + 3):
                if i < len(UNITS):
                    h, t = UNITS[i]
                    n = TILES[t][1]
                    o = 8 * (i % 3)
                    for c in range(2):
                        b = take_bank(dve, "v")
                        dve.tensor_copy(diff_e[0:n, i % 3, c, :], b[0:n, 0:L]).then_inc(EV, 1)
                    dve.drain()
                    dve.tensor_reduce(small[0:n, o:o + 2], diff_e[0:n, i % 3, :, :], AX.X, ALU.max)
                    dve.drain()
                    dve.tensor_scalar(small[0:n, o:o + 2], small[0:n, o:o + 2], -HD ** -0.5, None, ALU.mult)\
                        .then_inc(logits_ready.sem, 1)
                if 1 <= i <= len(UNITS):
                    h, t = UNITS[i - 1]
                    n = TILES[t][1]
                    o = 8 * ((i - 1) % 3)
                    e = diff_e[0:n, (i - 1) % 3, :, :]
                    dve.wait_ge(exp_ready.sem, exp_ready.next())
                    dve.reciprocal(small[0:n, o + 4:o + 6], small[0:n, o + 2:o + 4])
                    dve.drain()
                    dve.tensor_scalar(small[0:n, o + 6:o + 7], small[0:n, o + 5:o + 6], small[0:n, 36:37], None, ALU.mult)
                    dve.tensor_scalar(e[:, 0, :], e[:, 0, :], small[0:n, o + 4:o + 5], None, ALU.mult)
                    dve.drain()
                    dve.scalar_tensor_tensor(out=e[:, 0, :], in0=e[:, 1, :], scalar=small[0:n, o + 6:o + 7], in1=e[:, 0, :],
                                             op0=ALU.mult, op1=ALU.add).then_inc(operand_ready.sem, 1)
                if i >= 3:
                    h, t = UNITS[i - 3]
                    t0, n = TILES[t]
                    b = take_bank(dve, "v")
                    dve.tensor_copy(H[:, 2 + h, t0:t0 + n], b[:, 0:n]).then_inc(EV, 1)
            r = head_norm_vector(dve, 4)
            dve.tensor_tensor(H[:, 2:6, :], H[:, 2:6, :], r, ALU.mult)
            dve.drain()
            dve.tensor_scalar(H[:, 2:6, :], H[:, 2:6, :], V("df_subln_g_2", l), 1.0 - lam_init, ALU.mult, ALU.mult)

        def diff_scalar(act):
            for t, (t0, n) in enumerate(TILES):
                b = take_bank(act, "a")
                act.activation(diff_v[0:n, t, :], b[0:n, :], ACT.Copy).then_inc(EA, 1)
            act.wait_ge(for_scalar.sem, for_scalar.next())
            act.activation(small[:, 34:36], small[:, 34:36], ACT.Exp).then_inc(from_scalar.sem, 1)
            for i in range(len(UNITS) + 2):
                if i < len(UNITS):
                    n = TILES[UNITS[i][1]][1]
                    o = 8 * (i % 3)
                    act.wait_ge(logits_ready.sem, logits_ready.next())
                    for c in range(2):
                        e = diff_e[0:n, i % 3, c, :]
                        ins = act.activation(e, e, ACT.Exp, bias=small[0:n, o + c:o + c + 1], scale=HD ** -0.5,
                                             accum_out=small[0:n, o + 2 + c:o + 3 + c])
                    ins.then_inc(exp_ready.sem, 1)
                if i >= 2:
                    n = TILES[UNITS[i - 2][1]][1]
                    b = take_bank(act, "a")
                    for kt, (k0, kn) in enumerate(TILES):
                        ins = act.activation(diff_t[0:kn, i % 2, kt * P:kt * P + n], b[0:kn, kt * P:kt * P + n], ACT.Copy)
                    ins.then_inc(EA, 1)
                    act.drain().then_inc(aoperand_ready.sem, 1)
            head_norm_scalar(act, H[:, 2:6, :], 4, P)

        G0 = MIN * Q
        gl = [view(G0 + 5 * Q * d, 5, L) for d in range(2)]
        gl_dc = view(G0 + 10 * Q, 2, NCH)
        gl_kt = view(G0 + 10 * Q + 40, 2, 3 * P)
        gl_v = view(G0 + 10 * Q + 40 + 6 * P, 3, 256)
        gl_ve = view(G0 + 10 * Q + 40 + 12 * P, 4, 8, HD)
        gl_st = view(G0 + 10 * Q + 40 + 12 * P + 2048, 2, NCH, HD)
        s_at = S[:, :, :].rearrange("p a b -> p (a b)")
        gl_at = [view(G0 + 10 * Q + 40 + 12 * P + 2048 + 2 * NCH * HD, 4, 2, P)]
        gl_at += [s_at[:, 1024 * i:1024 * (i + 1)].rearrange("p (h d t) -> p h d t", h=4, d=2) for i in range(2)]

        def ends_of(x, d):
            c = x.rearrange("p (c t) -> p c t", t=CH)
            return c[:, :, CH - 1:CH] if d == 0 else c[:, :, 0:1]

        def cumsum(dve, out, x, d):
            if d == 0:
                return dve.tensor_tensor_scan(out, C("go_f"), x, 0.0, ALU.mult, ALU.add)
            return dve.tensor_tensor_scan(out[:, ::-1], C("go_b")[:, ::-1], x[:, ::-1], 0.0, ALU.mult, ALU.add)

        def gla_tensor(pe, l):
            for d in range(2):
                b = fill_bank(pe, "v")
                pe.matmul(b[:, 0:L], V("gl_gate_up_2", (2 * l + d) * P, P, 32), proj[0:32, C_T + 6, :], start=True, stop=True)\
                    .then_inc(FV, 1)
            for t, (t0, n) in enumerate(TILES):
                b = fill_bank(pe, "v")
                for m in range(2):
                    mm = pe.transpose(b[0:n, m * P:(m + 1) * P], proj[:, C_T + 2 + m, t0:t0 + n], C("ident"))
                mm.then_inc(FV, 1)
            for d in range(2):
                pe.wait_ge(operand_ready.sem, operand_ready.next())
                b = fill_bank(pe, "v")
                for t, (t0, n) in enumerate(TILES):
                    mm = pe.transpose(b[0:n, t * P:(t + 1) * P], gl[d][:, 3, t0:t0 + n], C("ident"))
                mm.then_inc(FV, 1)
            for t, (t0, n) in enumerate(TILES):
                nc_ = n // CH
                pe.wait_ge(operand_ready.sem, operand_ready.next())
                for d in range(2):
                    b = fill_bank(pe, "v")
                    for h in range(4):
                        mm = pe.matmul(b[32 * h:32 * h + 32, 0:nc_ * HD], gl_kt[0:n, d, t * P + 32 * h:t * P + 32 * h + 32],
                                       gl_ve[0:n, h, 0:nc_, :], start=True, stop=True, tile_position=(0, 32 * h))
                    mm.then_inc(FV, 1)
            for t, (t0, n) in enumerate(TILES):
                for h in range(4):
                    r = slice(32 * h, 32 * h + 32)
                    b = fill_bank(pe, "v")
                    for d in range(2):
                        mm = pe.matmul(b[0:n, d * P:d * P + n], gl[d][r, 2, t0:t0 + n], gl[d][r, 1, t0:t0 + n],
                                       start=True, stop=True, tile_position=(32 * h, 0))
                    mm.then_inc(FV, 1)
            pe.wait_ge(operand_ready.sem, operand_ready.next())
            out_of = {(t, j): fill_bank(pe, "a" if t == 2 else "v") for t in (1, 0, 2) for j in range(2)}
            for t, (t0, n) in enumerate(TILES):
                for h in range(4):
                    rr = 64 * (h % 2)
                    for d in range(2):
                        pe.matmul(out_of[t, h // 2][rr:rr + 64, 0:n], gl_v[0:n, t, h * HD:(h + 1) * HD], gl_at[t][0:n, h, d, 0:n],
                                  start=(d == 0), stop=False, skip_group_check=True, tile_position=(0, rr))
            pe.drain()
            for i in range(1, NCH):
                pe.wait_ge(operand_ready.sem, operand_ready.next())
                for d in range(2):
                    c, prev = (i, i - 1) if d == 0 else (NCH - 1 - i, NCH - i)
                    t = c * CH // P
                    a = c * CH - t * P
                    last = c == (NCH - 1 if d == 0 else 0)
                    for h in range(4):
                        rr = 64 * (h % 2)
                        mm = pe.matmul(out_of[t, h // 2][rr:rr + 64, a:a + CH], gl_st[32 * h:32 * h + 32, d, prev, :],
                                       gl[d][32 * h:32 * h + 32, 1, c * CH:(c + 1) * CH], start=False,
                                       stop=(last or (d == 0 and c * CH + CH == 2 * P)), skip_group_check=True,
                                       tile_position=(32 * h, rr))
                        if d == 1 and i == NCH - 1 and h % 2:
                            mm.then_inc(FV, 1)
                        if d == 0 and i == NCH - 2 and h % 2:
                            mm.then_inc(FV, 1)
                        if d == 0 and i == NCH - 1 and h % 2:
                            mm.then_inc(FA, 1)
            head_norm_tensor(pe, 2, C("ones64"))

        def gla_vector(dve, l):
            for d in range(2):
                b = take_bank(dve, "v")
                dve.tensor_scalar(gl[d][:, 0, :], b[:, 0:L], V("gl_gate_b_2", 2 * l + d), None, ALU.add).then_inc(EV, 1)
                dve.drain().then_inc(for_scalar.sem, 1)
            for t, (t0, n) in enumerate(TILES):
                b = take_bank(dve, "v")
                dve.tensor_copy(gl_v[0:n, t, :], b[0:n, 0:256]).then_inc(EV, 1)
            for d in range(2):
                z, tmp = gl[d][:, 0, :], gl[d][:, 4, :]
                dve.wait_ge(from_scalar.sem, from_scalar.next())
                dve.scalar_tensor_tensor(out=tmp, in0=z, scalar=0.0, in1=tmp, op0=ALU.min, op1=ALU.subtract)
                dve.drain()
                dve.tensor_scalar(tmp, tmp, 1.0 / 16.0, None, ALU.mult)
                dve.drain()
                cumsum(dve, z, tmp, d)
                dve.drain()
                dve.tensor_tensor(gl[d][:, 3, :].rearrange("p (c t) -> p c t", t=CH),
                                  ends_of(z, d).to_broadcast([P, NCH, CH]), z.rearrange("p (c t) -> p c t", t=CH),
                                  ALU.subtract)
                dve.drain().then_inc(for_scalar.sem, 1)
            for d in range(2):
                g = gl[d]
                dve.wait_ge(from_scalar.sem, from_scalar.next())
                dve.tensor_copy(gl_dc[:, d, :], ends_of(g[:, 1, :], d).rearrange("p c o -> p (c o)"))
                dve.drain()
                dve.scalar_tensor_tensor(out=g[:, 1, :], in0=g[:, 1, :], scalar=32 ** -0.5, in1=proj[:, C_T, :],
                                         op0=ALU.mult, op1=ALU.mult)
                dve.tensor_tensor(g[:, 2, :], g[:, 2, :], proj[:, C_T + 1, :], ALU.mult)
                dve.tensor_tensor(g[:, 3, :], g[:, 3, :], proj[:, C_T + 1, :], ALU.mult)
                dve.drain().then_inc(operand_ready.sem, 1)
                b = take_bank(dve, "v")
                dve.tensor_copy(gl_kt[:, d, 0:2 * P], b[:, 0:2 * P])
                dve.tensor_copy(gl_kt[0:16, d, 2 * P:3 * P], b[0:16, 2 * P:3 * P]).then_inc(EV, 1)
            for t, (t0, n) in enumerate(TILES):
                nc_ = n // CH
                dve.drain()
                for h in range(4):
                    dve.tensor_tensor(gl_ve[0:n, h, 0:nc_, :],
                                      gl_v[0:n, t, h * HD:(h + 1) * HD].unsqueeze(1).to_broadcast([n, nc_, HD]),
                                      C("chunk_of")[0:n, 0:nc_].unsqueeze(2).to_broadcast([n, nc_, HD]), ALU.mult)
                dve.drain().then_inc(operand_ready.sem, 1)
                for d in range(2):
                    b = take_bank(dve, "v")
                    dve.tensor_copy(gl_st[:, d, t0 // CH:t0 // CH + nc_, :],
                                    b[:, 0:nc_ * HD].rearrange("p (c v) -> p c v", v=HD)).then_inc(EV, 1)
            for t, (t0, n) in enumerate(TILES):
                for h in range(4):
                    b = take_bank(dve, "v")
                    dve.tensor_tensor(gl_at[t][0:n, h, :, 0:n], b[0:n, 0:2 * P].rearrange("p (d t) -> p d t", d=2)[:, :, 0:n],
                                      C("le_fb")[0:n, :].rearrange("p (d t) -> p d t", d=2)[:, :, 0:n],
                                      ALU.mult).then_inc(EV, 1)
            dve.drain().then_inc(operand_ready.sem, 1)
            dve.drain().then_inc(operand_ready.sem, 1)
            for i in range(1, NCH):
                for d in range(2):
                    c, prev = (i, i - 1) if d == 0 else (NCH - 1 - i, NCH - i)
                    dve.scalar_tensor_tensor(out=gl_st[:, d, c, :], in0=gl_st[:, d, prev, :], scalar=gl_dc[:, d, c:c + 1],
                                             in1=gl_st[:, d, c, :], op0=ALU.mult, op1=ALU.add)
                if i < NCH - 1:
                    dve.drain().then_inc(operand_ready.sem, 1)
            for t in (1, 0):
                for j in range(2):
                    b = take_bank(dve, "v")
                    dve.tensor_copy(H[:, 6 + j, t * P:(t + 1) * P], b[:, 0:P]).then_inc(EV, 1)
            r = head_norm_vector(dve, 2)
            dve.tensor_tensor(H[:, 6:8, :], H[:, 6:8, :], r, ALU.mult)
            dve.drain()
            dve.scalar_tensor_tensor(out=H[:, 6:8, :], in0=H[:, 6:8, :], scalar=V("gl_norm_g_2", l),
                                     in1=proj[:, C_T + 4:C_T + 6, :], op0=ALU.mult, op1=ALU.mult)

        def gla_scalar(act):
            for d in range(2):
                t = gl[d][:, 4, :]
                act.wait_ge(for_scalar.sem, for_scalar.next())
                act.activation(t, gl[d][:, 0, :], ACT.Abs)
                act.drain()
                act.activation(t, t, ACT.Exp, scale=-1.0)
                act.drain()
                act.activation(t, t, ACT.Ln, bias=1.0).then_inc(from_scalar.sem, 1)
            for d in range(2):
                g = gl[d]
                act.wait_ge(for_scalar.sem, for_scalar.next())
                act.activation(g[:, 1, :], g[:, 0, :], ACT.Exp)
                act.activation(g[:, 2, :], g[:, 0, :], ACT.Exp, scale=-1.0)
                act.activation(g[:, 3, :], g[:, 3, :], ACT.Exp)
                act.drain().then_inc(from_scalar.sem, 1)
            act.activation(proj[:, C_T + 4:C_T + 6, :], proj[:, C_T + 4:C_T + 6, :], ACT.Silu)
            for j in range(2):
                b = take_bank(act, "a")
                act.activation(H[:, 6 + j, 2 * P:], b[:, 0:L - 2 * P], ACT.Copy).then_inc(EA, 1)
            act.drain()
            head_norm_scalar(act, H[:, 6:8, :], 2, HD)

        sh = view(0, 9, L)
        kk, rw_o, ksum, rtmp = [view((9 + 2 * i) * Q, 2, L) for i in range(4)]
        kdir, ka, lwa, bR, Kb, Bb = [view((18 + 2 * i) * Q, 2, L) for i in range(6)]
        R0 = 30 * Q
        rv = view(R0, 3, 256)
        kht, bht = view(R0 + 768, 256), view(R0 + 1024, 256)
        rve, rbe, rpe = [view(R0 + 1280 + 512 * i, 4, 2, HD) for i in range(3)]
        rF = view(R0 + 2816, 2, NCH, HD)
        rS = view(R0 + 2816 + 2 * NCH * HD, 2, NCH, HD)
        M0 = R0 + 2816 + 4 * NCH * HD
        s_flat = S[:, :, :].rearrange("p a b -> p (a b)")
        mT, mM, mM2, mM2T = [s_flat[:, 512 * i:512 * (i + 1)].rearrange("p (h t) -> p h t", h=4) for i in range(4)]
        s_inter = S[:, 0:2, :]
        nT, LkT, LbT, Z = [view(M0 + 512 * i, 4, P) for i in range(4)]
        rdc = view(M0 + 2048, 2, NCH)

        def rwkv_plan(l):
            for w in ("rw_w_up_2", "rw_a_up_2"):
                plan.append((A[w][l].rearrange("d r c -> (d r) c").unsqueeze(1), 1, 256))
            plan.append((A["rw_g_up_2"][l].unsqueeze(1), 1, 256))

        def rwkv_tensor(pe, l):
            pe.wait_ge(operand_ready.sem, operand_ready.next())
            for j in range(2):
                b = fill_bank(pe, "v")
                pe.matmul(b[:, 0:L], C("ones64"), S[:, j, :], start=True, stop=True).then_inc(FV, 1)
            for t, (t0, n) in enumerate(TILES):
                b = fill_bank(pe, "v")
                for j in range(2):
                    mm = pe.transpose(b[0:n, j * P:(j + 1) * P], sh[:, 4 + j, t0:t0 + n], C("ident"))
                mm.then_inc(FV, 1)
            W = [next_slot(pe, 1, 256) for _ in range(3)]
            pe.wait_ge(aoperand_ready.sem, aoperand_ready.next())
            for d in range(2):
                dr = slice(64 * d, 64 * d + 64)
                for part in range(2):
                    for j in range(2):
                        b = fill_bank(pe, "v")
                        pe.matmul(b[:, 0:L], W[part][dr, 0, j * P:(j + 1) * P], sh[dr, 6 + part, :], start=True, stop=True)\
                            .then_inc(FV, 1)
                pe.wait_ge(operand_ready.sem, operand_ready.next())
                for t in range(3):
                    rwkv_tile_tensor(pe, d, t)
                pe.wait_ge(aoperand_ready.sem, aoperand_ready.next())
                inter = None
                for i in range(1, NCH):
                    c, prev = (i, i - 1) if d == 0 else (NCH - 1 - i, NCH - i)
                    pe.wait_ge(operand_ready.sem, operand_ready.next())
                    b = fill_bank(pe, "v")
                    for h in range(4):
                        r, j = slice(64 * (h % 2), 64 * (h % 2) + 64), h // 2
                        mm = pe.matmul(b[r, j * HD:(j + 1) * HD], rF[r, j, c, :], rS[r, j, prev, :], start=True, stop=True)
                    mm.then_inc(FV, 1)
                    t = c * CH // P
                    if inter is None:
                        inter = fill_bank(pe, "a")
                    for h in range(4):
                        r, j = slice(64 * (h % 2), 64 * (h % 2) + 64), h // 2
                        o = j * P + c * CH - t * P
                        mm = pe.matmul(inter[r, o:o + CH], rS[r, j, prev, :], bR[r, j, c * CH:(c + 1) * CH], start=True, stop=True)
                    if c == inter_chunks(d, t)[-1]:
                        mm.then_inc(FA, 1)
                        inter = None
            for j in range(2):
                b = fill_bank(pe, "v")
                pe.matmul(b[:, 0:L], W[2][:, 0, j * P:(j + 1) * P], sh[:, 8, :], start=True, stop=True).then_inc(FV, 1)
            for _ in range(3):
                read_with_bank()
            pe.wait_ge(operand_ready.sem, operand_ready.next())
            for src in (rw_o, rtmp):
                for j in range(2):
                    b = fill_bank(pe, "v")
                    pe.matmul(b[:, 0:L], C("ones64"), src[:, j, :], start=True, stop=True).then_inc(FV, 1)
            head_norm_tensor(pe, 2, C("ones64"))

        def inter_chunks(d, t):
            t0, n = TILES[t]
            order = range(1, NCH) if d == 0 else range(NCH - 2, -1, -1)
            return [c for c in order if t0 <= c * CH < t0 + n]

        def rwkv_tile_tensor(pe, d, t):
            t0, n = TILES[t]
            tok = slice(t0, t0 + n)
            nc_ = n // CH
            b = fill_bank(pe, "v")
            for i, src in enumerate((lwa, kdir)):
                for j in range(2):
                    mm = pe.transpose(b[0:n, i * 256 + j * P:i * 256 + (j + 1) * P], src[:, j, tok], C("ident"))
            mm.then_inc(FV, 1)
            b = fill_bank(pe, "v")
            for j in range(2):
                mm = pe.transpose(b[0:n, j * P:(j + 1) * P], ka[:, j, tok], C("ident"))
            mm.then_inc(FV, 1)
            for pp in range(2):
                r = slice(64 * pp, 64 * pp + 64)
                for pairs in (((Bb, lwa), (lwa, Bb)), ((Kb, lwa), (Kb, bR)), ((Bb, bR),)):
                    b = fill_bank(pe, "v")
                    for i, (x, y) in enumerate(pairs):
                        for j in range(2):
                            a = (2 * i + j) * P
                            mm = pe.matmul(b[0:n, a:a + n], x[r, j, tok], y[r, j, tok], start=True, stop=True)
                    mm.then_inc(FV, 1)
            pe.wait_ge(operand_ready.sem, operand_ready.next())

            def per_head(lhs, rhs, w):
                b = fill_bank(pe, "v")
                for h in range(4):
                    mm = pe.matmul(b[0:n, h * w:h * w + (n if rhs is not Z and w == P else w)], lhs(h), rhs_of(rhs, h, w), start=True, stop=True)
                mm.then_inc(FV, 1)

            def rhs_of(rhs, h, w):
                if rhs is Z:
                    return Z[0:n, h, :]
                if rhs is rv:
                    return rv[0:n, t, h * HD:(h + 1) * HD]
                return rhs[0:n, h, 0:n]
            m = lambda x: (lambda h: x[0:n, h, 0:n])

            def squares(which, lhs, rhs):
                b = fill_bank(pe, which)
                for h in range(4):
                    mm = pe.matmul(b[0:n, h * P:h * P + n], lhs[0:n, h, 0:n], rhs[0:n, h, 0:n], start=True, stop=True)
                mm.then_inc(FV if which == "v" else FA, 1)
            per_head(m(nT), rv, HD)
            squares("v", mT, mM)
            squares("a", mM, mT)
            pe.wait_ge(operand_ready.sem, operand_ready.next())
            per_head(m(mT), Z, P)
            pe.wait_ge(operand_ready.sem, operand_ready.next())
            pe.wait_ge(aoperand_ready.sem, aoperand_ready.next())
            per_head(m(mM2T), Z, P)
            squares("v", mM2T, mM2)
            squares("a", mM2, mM2T)
            pe.wait_ge(operand_ready.sem, operand_ready.next())
            pe.wait_ge(aoperand_ready.sem, aoperand_ready.next())
            per_head(m(nT), Z, P)
            squares("a", mM, nT)
            pe.wait_ge(operand_ready.sem, operand_ready.next())
            pe.wait_ge(aoperand_ready.sem, aoperand_ready.next())
            per_head(m(mM2), Z, P)
            pe.wait_ge(operand_ready.sem, operand_ready.next())
            b = fill_bank(pe, "v")
            for h in range(4):
                rr, j = 64 * (h % 2), h // 2
                mm = pe.matmul(b[rr:rr + 64, j * P:j * P + n], Z[0:n, h, 0:HD], LbT[0:n, h, 0:n], start=True, stop=True)
            mm.then_inc(FV, 1)
            b = fill_bank(pe, "v")
            for h in range(4):
                rr, j = 64 * (h % 2), h // 2
                o = b[rr:rr + 64, j * P:j * P + n]
                pe.matmul(o, rv[0:n, t, h * HD:(h + 1) * HD], LkT[0:n, h, 0:n], start=True, stop=False)
                mm = pe.matmul(o, Z[0:n, h, HD:P], LbT[0:n, h, 0:n], start=False, stop=True)
            mm.then_inc(FV, 1)
            pe.wait_ge(operand_ready.sem, operand_ready.next())
            for g in range(0, n, 32):
                r = slice(g, min(g + 32, n))
                w = (r.stop - r.start) // CH * HD
                b, b2 = fill_bank(pe, "a"), fill_bank(pe, "v")
                for h in range(4):
                    rr, j = 64 * (h % 2), h // 2
                    o = slice(j * P, j * P + w)
                    tp = (g, rr)
                    mm2 = pe.matmul(b[rr:rr + 64, o], Z[r, h, 0:HD], rbe[r, h, 0:w // HD, :], start=True, stop=True, tile_position=tp)
                    pe.matmul(b2[rr:rr + 64, o], kht[r, h * HD:(h + 1) * HD], rve[r, h, 0:w // HD, :], start=True, stop=False,
                              tile_position=tp)
                    mm = pe.matmul(b2[rr:rr + 64, o], bht[r, h * HD:(h + 1) * HD], rpe[r, h, 0:w // HD, :], start=False,
                                   stop=True, tile_position=tp)
                mm2.then_inc(FA, 1)
                mm.then_inc(FV, 1)

        def rwkv_tile_vector(dve, d, t):
            t0, n = TILES[t]
            tok = slice(t0, t0 + n)
            nc_ = n // CH
            lt, lt_t, le = ("lt_f", "lt_b", "le_f") if d == 0 else ("lt_b", "lt_f", "le_b")
            b = take_bank(dve, "v")
            dve.tensor_copy(Z[0:n, :, 0:HD], b[0:n, 0:256].rearrange("p (h k) -> p h k", h=4))
            dve.tensor_copy(kht[0:n, :], b[0:n, 256:512]).then_inc(EV, 1)
            b = take_bank(dve, "v")
            dve.tensor_copy(bht[0:n, :], b[0:n, 0:256]).then_inc(EV, 1)

            def masked(b, at, out, pp, mask, sign=1.0):
                return dve.scalar_tensor_tensor(out=out[0:n, pp::2, 0:n],
                                                in0=b[0:n, at:at + 256].rearrange("p (j t) -> p j t", j=2)[:, :, 0:n],
                                                scalar=sign, in1=C(mask)[0:n, 0:n].unsqueeze(1).to_broadcast([n, 2, n]),
                                                op0=ALU.mult, op1=ALU.mult)
            for pp in range(2):
                b = take_bank(dve, "v")
                masked(b, 0, mT, pp, lt)
                masked(b, 256, mM, pp, lt_t).then_inc(EV, 1)
                b = take_bank(dve, "v")
                masked(b, 0, nT, pp, lt)
                masked(b, 256, LkT, pp, le).then_inc(EV, 1)
                b = take_bank(dve, "v")
                masked(b, 0, LbT, pp, le, -1.0).then_inc(EV, 1)
            dve.drain().then_inc(operand_ready.sem, 1)

            def by_chunk(out, x):
                two = C("half_of")[0:n, :]
                for half in range(2):
                    dve.tensor_tensor(out[0:n, :, half, :], x, two[:, half:half + 1].unsqueeze(1).to_broadcast([n, 4, HD]), ALU.mult)

            def copy4(out, w=P):
                b = take_bank(dve, "v")
                dve.tensor_copy(out[0:n, :, 0:n], b[0:n, :].rearrange("p (h t) -> p h t", h=4)[:, :, 0:n]).then_inc(EV, 1)
            b = take_bank(dve, "v")
            dve.tensor_copy(Z[0:n, :, HD:P], b[0:n, 0:256].rearrange("p (h v) -> p h v", h=4)).then_inc(EV, 1)
            dve.drain().then_inc(operand_ready.sem, 1)

            def apply(sign):
                b = take_bank(dve, "v")
                dve.tensor_tensor(Z[0:n, :, :], Z[0:n, :, :], b[0:n, :].rearrange("p (h t) -> p h t", h=4), sign)\
                    .then_inc(EV, 1)
            copy4(mM2)
            apply(ALU.subtract)
            dve.drain().then_inc(operand_ready.sem, 1)
            apply(ALU.add)
            copy4(mM)
            dve.drain().then_inc(operand_ready.sem, 1)
            by_chunk(rve, rv[0:n, t, :].rearrange("p (h v) -> p h v", h=4))
            apply(ALU.add)
            dve.drain().then_inc(operand_ready.sem, 1)
            by_chunk(rbe, bht[0:n, :].rearrange("p (h k) -> p h k", h=4))
            apply(ALU.add)
            dve.drain().then_inc(operand_ready.sem, 1)
            by_chunk(rpe, Z[0:n, :, HD:P])
            dve.drain().then_inc(operand_ready.sem, 1)
            b = take_bank(dve, "v")
            two = lambda b: b[:, 0:256].rearrange("p (j t) -> p j t", j=2)[:, :, 0:n]
            dve.tensor_tensor(bR[:, :, tok], bR[:, :, tok], two(b), ALU.add).then_inc(EV, 1)
            b = take_bank(dve, "v")
            if d == 0:
                dve.tensor_copy(rw_o[:, :, tok], two(b)).then_inc(EV, 1)
            else:
                dve.tensor_tensor(rw_o[:, :, tok], rw_o[:, :, tok], two(b), ALU.add).then_inc(EV, 1)
            for g in range(0, n, 32):
                nn = min(32, n - g) // CH
                c = (t0 + g) // CH
                b = take_bank(dve, "v")
                dve.tensor_copy(rS[:, :, c:c + nn, :],
                                b[:, 0:2 * P].rearrange("p (j c v) -> p j c v", j=2, c=2)[:, :, 0:nn, :]).then_inc(EV, 1)

        def rwkv_tile_scalar(act, t):
            t0, n = TILES[t]
            for out in (mM2T, nT, mM2):
                b = take_bank(act, "a")
                act.activation(out[0:n, :, 0:n], b[0:n, :].rearrange("p (h t) -> p h t", h=4)[:, :, 0:n], ACT.Copy)\
                    .then_inc(EA, 1)
                act.drain().then_inc(aoperand_ready.sem, 1)
            for g in range(0, n, 32):
                nn = min(32, n - g) // CH
                c = (t0 + g) // CH
                b = take_bank(act, "a")
                act.activation(rF[:, :, c:c + nn, :], b[:, 0:2 * P].rearrange("p (j c v) -> p j c v", j=2, c=2)[:, :, 0:nn, :],
                               ACT.Copy).then_inc(EA, 1)

        def rwkv_vector(dve, l):
            oka = small[:, 49:51]
            dve.tensor_scalar(oka, V("rw_k_a_2", 2 * l, 2), -1.0, 1.0, ALU.mult, ALU.add)
            for j in range(2):
                dve.tensor_scalar(kk[:, j, :], sh[:, 2 + j, :], V("rw_k_k_2", 2 * l + j), None, ALU.mult)
            dve.drain()
            dve.tensor_tensor(S[:, 0:2, :], kk, kk, ALU.mult)
            dve.drain().then_inc(operand_ready.sem, 1)
            for j in range(2):
                b = take_bank(dve, "v")
                dve.tensor_scalar(rtmp[:, j, :], b[:, 0:L], 1e-24, None, ALU.max).then_inc(EV, 1)
            dve.drain().then_inc(for_scalar.sem, 1)
            for t, (t0, n) in enumerate(TILES):
                b = take_bank(dve, "v")
                dve.tensor_copy(rv[0:n, t, :], b[0:n, 0:256]).then_inc(EV, 1)
            dve.wait_ge(from_scalar.sem, from_scalar.next())
            dve.reciprocal(rtmp, rtmp)
            dve.drain()
            dve.tensor_tensor(kk, kk, rtmp, ALU.mult)
            dve.drain()
            for d in range(2):
                for out, g in ((lwa, "rw_w0_2"), (ka, "rw_a0_2")):
                    for j in range(2):
                        b = take_bank(dve, "v")
                        dve.tensor_scalar(out[:, j, :], b[:, 0:L], V(g, (2 * l + d) * 2 + j), None, ALU.add).then_inc(EV, 1)
                dve.drain().then_inc(for_scalar.sem, 1)
                dve.wait_ge(from_scalar.sem, from_scalar.next())
                for j in range(2):
                    dve.tensor_scalar(kdir[:, j, :], ka[:, j, :], V("rw_k_a_2", 2 * l + j), oka[:, j:j + 1], ALU.mult, ALU.add)
                dve.tensor_scalar(lwa, lwa, -0.6065306597126334, None, ALU.mult)
                dve.drain()
                dve.tensor_tensor(kdir, kdir, sh[:, 2:4, :], ALU.mult)
                dve.tensor_tensor(ka, ka, kk, ALU.mult)
                for j in range(2):
                    cumsum(dve, bR[:, j, :], lwa[:, j, :], d)
                dve.drain()
                if d == 0:
                    dve.tensor_copy(ksum, kdir)
                else:
                    dve.tensor_tensor(ksum, ksum, kdir, ALU.add)
                dve.tensor_tensor(lwa, bR, lwa, ALU.subtract)
                for j in range(2):
                    dve.tensor_tensor(rtmp[:, j, :].rearrange("p (c t) -> p c t", t=CH),
                                      ends_of(bR[:, j, :], d).to_broadcast([P, NCH, CH]),
                                      bR[:, j, :].rearrange("p (c t) -> p c t", t=CH), ALU.subtract)
                dve.drain().then_inc(for_scalar.sem, 1)
                dve.wait_ge(from_scalar.sem, from_scalar.next())
                for j in range(2):
                    dve.tensor_copy(rdc[:, j, :], ends_of(bR[:, j, :], d).rearrange("p c o -> p (c o)"))
                dve.tensor_tensor(lwa, lwa, kk, ALU.mult)
                dve.tensor_tensor(Bb, Kb, ka, ALU.mult)
                dve.drain()
                dve.tensor_tensor(Kb, Kb, kdir, ALU.mult)
                dve.tensor_tensor(bR, bR, sh[:, 0:2, :], ALU.mult)
                dve.drain()
                dve.tensor_tensor(kdir, kdir, rtmp, ALU.mult)
                for j in range(2):
                    dve.scalar_tensor_tensor(out=ka[:, j, :], in0=ka[:, j, :], scalar=-1.0, in1=rtmp[:, j, :], op0=ALU.mult,
                                             op1=ALU.mult)
                dve.drain().then_inc(operand_ready.sem, 1)
                for t in range(3):
                    rwkv_tile_vector(dve, d, t)
                for i in range(1, NCH):
                    c, prev = (i, i - 1) if d == 0 else (NCH - 1 - i, NCH - i)
                    dve.drain().then_inc(operand_ready.sem, 1)
                    for j in range(2):
                        dve.scalar_tensor_tensor(out=rS[:, j, c, :], in0=rS[:, j, prev, :], scalar=rdc[:, j, c:c + 1],
                                                 in1=rS[:, j, c, :], op0=ALU.mult, op1=ALU.add)
                    dve.drain()
                    b = take_bank(dve, "v")
                    dve.tensor_tensor(rS[:, :, c, :], rS[:, :, c, :], b[:, 0:2 * HD].rearrange("p (j v) -> p j v", j=2), ALU.add)\
                        .then_inc(EV, 1)
                dve.wait_ge(from_scalar.sem, from_scalar.next())
                lo = CH if d == 0 else 0
                dve.tensor_tensor(rw_o[:, :, lo:lo + L - CH], rw_o[:, :, lo:lo + L - CH], s_inter[:, :, lo:lo + L - CH], ALU.add)
                dve.drain()
            for j in range(2):
                b = take_bank(dve, "v")
                dve.tensor_copy(kdir[:, j, :], b[:, 0:L]).then_inc(EV, 1)
            for j in range(2):
                dve.scalar_tensor_tensor(out=rtmp[:, j, :], in0=sh[:, j, :], scalar=V("rw_r_k_2", 2 * l + j), in1=ksum[:, j, :],
                                         op0=ALU.mult, op1=ALU.mult)
            dve.drain().then_inc(operand_ready.sem, 1)
            for j in range(2):
                b = take_bank(dve, "v")
                dve.scalar_tensor_tensor(out=rw_o[:, j, :], in0=b[:, 0:L], scalar=-1.0 / HD, in1=rw_o[:, j, :],
                                         op0=ALU.mult, op1=ALU.add).then_inc(EV, 1)
            for j in range(2):
                b = take_bank(dve, "v")
                dve.tensor_tensor(ka[:, j, :], b[:, 0:L], sh[:, 4 + j, :], ALU.mult).then_inc(EV, 1)
            r = head_norm_vector(dve, 2)
            dve.tensor_tensor(rw_o, rw_o, r, ALU.mult)
            dve.drain()
            for j in range(2):
                dve.tensor_scalar(rw_o[:, j, :], rw_o[:, j, :], V("rw_gn_g_2", 2 * l + j), V("rw_gn_b_2", 2 * l + j),
                                  ALU.mult, ALU.add)
            dve.drain()
            dve.tensor_tensor(rw_o, rw_o, ka, ALU.add)
            dve.drain()
            dve.tensor_tensor(H[:, 0:2, :], rw_o, kdir, ALU.mult)

        def rwkv_scalar(act):
            act.activation(sh[:, 6, :], sh[:, 6, :], ACT.Tanh)
            act.activation(sh[:, 8, :], sh[:, 8, :], ACT.Sigmoid)
            act.drain().then_inc(aoperand_ready.sem, 1)
            act.wait_ge(for_scalar.sem, for_scalar.next())
            act.activation(rtmp, rtmp, ACT.Sqrt).then_inc(from_scalar.sem, 1)
            for d in range(2):
                act.wait_ge(for_scalar.sem, for_scalar.next())
                act.activation(lwa, lwa, ACT.Sigmoid)
                act.activation(ka, ka, ACT.Sigmoid)
                act.drain().then_inc(from_scalar.sem, 1)
                act.wait_ge(for_scalar.sem, for_scalar.next())
                act.activation(Kb, bR, ACT.Exp, scale=-1.0)
                act.activation(lwa, lwa, ACT.Exp)
                act.activation(rtmp, rtmp, ACT.Exp)
                act.drain()
                act.activation(bR, bR, ACT.Exp)
                act.drain().then_inc(from_scalar.sem, 1)
                for t in range(3):
                    rwkv_tile_scalar(act, t)
                act.drain().then_inc(aoperand_ready.sem, 1)
                for t in (range(3) if d == 0 else range(2, -1, -1)):
                    chunks = sorted(inter_chunks(d, t))
                    if chunks:
                        lo, hi, t0 = chunks[0] * CH, chunks[-1] * CH + CH, TILES[t][0]
                        b = take_bank(act, "a")
                        act.activation(s_inter[:, :, lo:hi],
                                       b[:, 0:2 * P].rearrange("p (j t) -> p j t", j=2)[:, :, lo - t0:hi - t0], ACT.Copy)\
                            .then_inc(EA, 1)
                act.drain().then_inc(from_scalar.sem, 1)
            head_norm_scalar(act, rw_o, 2, HD, eps_rwkv)

        def mix_out_tensor(pe):
            project_tensor(pe, D, KD, lambda k: H[:, k, :], L)

        def mix_out_vector(dve):
            for m in range(KD):
                b = take_bank(dve, "v")
                dve.tensor_tensor(X[:, m, :], X[:, m, :], b[:, 0:L], ALU.add).then_inc(EV, 1)
                dve.drain().then_inc(tile_ready.sem, 1)

        NE, CAP, FE = 16, 34, A["e_w1_2"].shape[3]
        KE = FE // P
        PAIRS = NE // 2
        xs = view(0, KD, NE * 64)
        T0 = KD * NE * 64
        utok = view(T0, 3, D)
        hot = view(T0 + 3 * D, 3, NE, CAP)
        E0 = T0 + 3 * D + 3 * NE * CAP
        aff, cum, mask = [view(E0 + 3 * NE * i, 3, NE) for i in range(3)]
        work = view(E0 + 9 * NE, L)
        top8 = view(E0 + 9 * NE + L, 8)
        ghot = view(E0 + 9 * NE + L + 8, NE, 64)
        G0 = E0 + 9 * NE + L + 8 + NE * 64
        hs, hid2 = view(G0, FE), view(G0 + FE, FE)
        hidT = view(G0 + 2 * FE, KE, P)
        gT = view(T0, PAIRS, L)
        h_flat = H[:, :, :].rearrange("p k t -> p (k t)")
        ys = [h_flat[:, 0:D], h_flat[:, D:2 * D], view(T0 + 3 * D, D), view(G0 - D, D)]
        assert PAIRS * L <= 3 * D and 2 * D <= G0 - (T0 + 3 * D)
        CHUNKS = ((0, 512), (512, 512), (1024, 384))
        KSPLIT = ((0, 4), (4, 4), (8, 3))
        silu_ready = signal("silu_ready")

        def moe_plan(l):
            load_plan(A["router_2"][l], 0, NE, 0, KD)
            for p in range(PAIRS):
                for w in ("e_w1_2", "e_w3_2"):
                    for c0, cw in CHUNKS:
                        for e in (2 * p, 2 * p + 1):
                            load_plan(A[w][l, e], c0, cw, 0, KD)
                for k0, nk in KSPLIT:
                    for e in (2 * p, 2 * p + 1):
                        load_plan(A["e_w2_2"][l, e], 0, D, k0, nk)

        def gather_tensor(pe, g):
            for k0 in range(0, KD, 2):
                b = fill_bank(pe, "v")
                o = b[:, :].rearrange("p (k e s) -> p k e s", k=2, e=4)
                for k in range(2):
                    for t, (t0, n) in enumerate(TILES):
                        mm = pe.matmul(o[:, k, :, 0:CAP], utok[0:n, t, (k0 + k) * P:(k0 + k + 1) * P],
                                       hot[0:n, t, 4 * g:4 * g + 4, :], start=(t == 0), stop=(t == 2))
                mm.then_inc(FV, 1)

        def gather_vector(dve, g):
            for k0 in range(0, KD, 2):
                b = take_bank(dve, "v")
                dve.tensor_copy(xs[:, k0:k0 + 2, 256 * g:256 * g + 256].rearrange("p k (e s) -> p k e s", e=4)[:, :, :, 0:CAP],
                                b[:, :].rearrange("p (k e s) -> p k e s", k=2, e=4)[:, :, :, 0:CAP]).then_inc(EV, 1)

        def gates_tensor(pe):
            for t, (t0, n) in enumerate(TILES):
                pe.wait_ge(operand_ready.sem, operand_ready.next())
                for half in range(2):
                    b = fill_bank(pe, "v")
                    for q in range(4):
                        p = 4 * half + q
                        mm = pe.transpose(b[:, q * P:q * P + n], ghot[0:n, 2 * p:2 * p + 2, :].rearrange("p e s -> p (e s)"),
                                          C("ident")[0:n, 0:n])
                    mm.then_inc(FV, 1)

        def gates_vector(dve):
            for t, (t0, n) in enumerate(TILES):
                dve.tensor_tensor(ghot[0:n, :, 0:CAP], hot[0:n, t, :, :], aff[0:n, t, :].unsqueeze(2).to_broadcast([n, NE, CAP]),
                                  ALU.mult)
                dve.drain().then_inc(operand_ready.sem, 1)
                for half in range(2):
                    b = take_bank(dve, "v")
                    dve.tensor_copy(gT[:, 4 * half:4 * half + 4, t0:t0 + n],
                                    b[:, :].rearrange("p (q t) -> p q t", q=4)[:, :, 0:n]).then_inc(EV, 1)

        pads_zeroed = signal("pads_zeroed")

        def moe_pool(pool):
            pool.memset(xs.rearrange("p k s -> p (k s)"), 0.0)
            pool.memset(ghot.rearrange("p e s -> p (e s)"), 0.0)
            pool.drain().then_inc(pads_zeroed.sem, 1)

        def moe_tensor(pe):
            W = next_slot(pe, KD, NE)
            b = fill_bank(pe, "v")
            for t, (t0, n) in enumerate(TILES):
                for k in range(KD):
                    if t == 0:
                        pe.wait_ge(h_ready.sem, h_ready.next())
                    mm = pe.matmul(b[0:n, t * NE:(t + 1) * NE], H[:, k, t0:t0 + n], W[:, k, :], start=(k == 0), stop=(k == KD - 1))
            mm.then_inc(FV, 1)
            read_with_bank()
            for t, (t0, n) in enumerate(TILES):
                for half in range(2):
                    b = fill_bank(pe, "a")
                    for m in range(4):
                        mm = pe.transpose(b[0:n, m * P:(m + 1) * P], H[:, 4 * half + m, t0:t0 + n], C("ident"))
                    mm.then_inc(FA, 1)
            pe.wait_ge(operand_ready.sem, operand_ready.next())
            b = fill_bank(pe, "v")
            for t, (t0, n) in enumerate(TILES):
                mm = pe.transpose(b[0:NE, t0:t0 + n], aff[0:n, t, :], C("ident")[0:n, 0:n])
            mm.then_inc(FV, 1)
            pe.wait_ge(operand_ready.sem, operand_ready.next())
            b = fill_bank(pe, "v")
            for t, (t0, n) in enumerate(TILES):
                mm = pe.transpose(b[0:n, t * NE:(t + 1) * NE], work[0:NE, t0:t0 + n], C("ident")[0:NE, 0:NE])
            mm.then_inc(FV, 1)
            pe.wait_ge(operand_ready.sem, operand_ready.next())
            b = fill_bank(pe, "v")
            for t, (t0, n) in enumerate(TILES):
                o = b[0:n, t * NE:(t + 1) * NE]
                for s_ in range(t):
                    pe.matmul(o, C("ones")[:, 0:n], mask[:, s_, :], start=(s_ == 0), stop=False)
                mm = pe.matmul(o, C("before")[0:n, 0:n], mask[0:n, t, :], start=(t == 0), stop=True)
            mm.then_inc(FV, 1)
            pe.wait_ge(operand_ready.sem, operand_ready.next())
            pe.wait_ge(aoperand_ready.sem, aoperand_ready.next())
            gather_tensor(pe, 0)
            pe.wait_ge(operand_ready.sem, operand_ready.next())
            for p in range(PAIRS):
                for which in ("a", "v"):
                    for c0, cw in CHUNKS:
                        W = [next_slot(pe, KD, cw) for _ in range(2)]
                        b = fill_bank(pe, which)
                        for k in range(KD):
                            for e in range(2):
                                x = xs[:, k, (2 * p + e) * 64:(2 * p + e + 1) * 64]
                                mm = pe.matmul(b[64 * e:64 * e + 64, 0:cw], x, W[e][:, k, :], start=(k == 0), stop=(k == KD - 1))
                                if k == KD - 1 and e == 0:
                                    read_alone(mm)
                        mm.then_inc(FA if which == "a" else FV, 1)
                        read_with_bank(which)
                pe.wait_ge(operand_ready.sem, operand_ready.next())
                for f0, nf in KSPLIT:
                    b = fill_bank(pe, "a")
                    for f in range(nf):
                        mm = pe.transpose(b[:, f * P:(f + 1) * P], hid2[:, (f0 + f) * P:(f0 + f + 1) * P], C("ident"))
                    mm.then_inc(FA, 1)
                pe.wait_ge(aoperand_ready.sem, aoperand_ready.next())
                b = [fill_bank(pe, "v") for _ in range(2)]
                for f0, nf in KSPLIT:
                    W = [next_slot(pe, nf, D) for _ in range(2)]
                    for f in range(nf):
                        for c in range(2):
                            for e in range(2):
                                mm = pe.matmul(b[c][64 * e:64 * e + 64, :], hidT[:, f0 + f, 64 * e:64 * e + 64],
                                               W[e][:, f, c * 512:(c + 1) * 512], start=(f0 + f == 0), stop=(f0 + f == KE - 1))
                                if f == nf - 1 and c == 1 and e == 0:
                                    read_alone(mm)
                            if f0 + f == KE - 1:
                                mm.then_inc(FV, 1)
                    if f0 + nf < KE:
                        read_alone(mm)
                    else:
                        read_with_bank("v")
                if p == 0:
                    gather_tensor(pe, 1)
                    gather_tensor(pe, 2)
                if p == 1:
                    gather_tensor(pe, 3)
                    gates_tensor(pe)
                    pe.wait_ge(operand_ready.sem, operand_ready.next())
                if p % 4 == 3:
                    pe.wait_ge(operand_ready.sem, operand_ready.next())
                    for m in range(KD):
                        b = fill_bank(pe, "v")
                        for q in range(4):
                            mm = pe.matmul(b[:, 0:L], ys[q][:, m * P:(m + 1) * P], gT[:, p - 3 + q, :], start=(q == 0), stop=(q == 3))
                        mm.then_inc(FV, 1)

        def moe_vector(dve, l):
            gain_norm_vector(dve, "norm2_g_2", l)
            dve.memset(aff.rearrange("p t e -> p (t e)"), 0.0)
            dve.drain()
            b = take_bank(dve, "v")
            for t, (t0, n) in enumerate(TILES):
                ins = dve.tensor_copy(aff[0:n, t, :], b[0:n, t * NE:(t + 1) * NE])
            ins.then_inc(EV, 1)
            dve.drain()
            mx, sm = small[:, 52:55], small[:, 56:59]
            bc = lambda x: x.unsqueeze(2).to_broadcast([P, 3, NE])
            dve.tensor_reduce(mx, aff, AX.X, ALU.max)
            dve.drain()
            dve.tensor_tensor(aff, aff, bc(mx), ALU.subtract)
            dve.drain().then_inc(for_scalar.sem, 1)
            dve.wait_ge(from_scalar.sem, from_scalar.next())
            dve.tensor_reduce(sm, aff, AX.X, ALU.add)
            dve.drain()
            dve.reciprocal(sm, sm)
            dve.drain()
            dve.tensor_tensor(aff, aff, bc(sm), ALU.mult)
            dve.drain().then_inc(operand_ready.sem, 1)
            b = take_bank(dve, "v")
            w = work[0:NE, :]
            dve.tensor_copy(w, b[0:NE, 0:L]).then_inc(EV, 1)
            dve.drain()
            for i in range(0, CAP, 8):
                dve.max(out=top8[0:NE, :], in_=w)
                dve.drain()
                if CAP - i < 8:
                    dve.memset(top8[0:NE, CAP - i:8], -1.0)
                    dve.drain()
                dve.match_replace(out=w, in_to_replace=top8[0:NE, :], in_values=w, imm_value=-1.0)
                dve.drain()
            dve.tensor_scalar(w, w, 0.0, None, ALU.is_lt)
            dve.drain().then_inc(operand_ready.sem, 1)
            b = take_bank(dve, "v")
            for t, (t0, n) in enumerate(TILES):
                ins = dve.tensor_copy(mask[0:n, t, :], b[0:n, t * NE:(t + 1) * NE])
            ins.then_inc(EV, 1)
            dve.drain().then_inc(operand_ready.sem, 1)
            b = take_bank(dve, "v")
            for t, (t0, n) in enumerate(TILES):
                ins = dve.scalar_tensor_tensor(out=cum[0:n, t, :], in0=mask[0:n, t, :], scalar=-1000.0,
                                               in1=b[0:n, t * NE:(t + 1) * NE], op0=ALU.mult, op1=ALU.add)
            ins.then_inc(EV, 1)
            dve.drain()
            for t, (t0, n) in enumerate(TILES):
                dve.tensor_scalar(cum[0:n, t, :], cum[0:n, t, :], 1000.0, None, ALU.add)
            dve.drain()
            for t, (t0, n) in enumerate(TILES):
                dve.tensor_tensor(hot[0:n, t, :, :], C("slot_no")[0:n, :].unsqueeze(1).to_broadcast([n, NE, CAP]),
                                  cum[0:n, t, :].unsqueeze(2).to_broadcast([n, NE, CAP]), ALU.is_equal)
            dve.drain().then_inc(operand_ready.sem, 1)
            dve.wait_ge(pads_zeroed.sem, pads_zeroed.next())
            gather_vector(dve, 0)
            dve.drain().then_inc(operand_ready.sem, 1)
            for p in range(PAIRS):
                for c0, cw in CHUNKS:
                    dve.wait_ge(silu_ready.sem, silu_ready.next())
                    b = take_bank(dve, "v")
                    dve.tensor_tensor(hid2[:, c0:c0 + cw], hs[:, c0:c0 + cw], b[:, 0:cw], ALU.mult).then_inc(EV, 1)
                dve.drain().then_inc(operand_ready.sem, 1)
                for c in range(2):
                    b = take_bank(dve, "v")
                    dve.tensor_copy(ys[p % 4][:, c * 512:(c + 1) * 512], b[:, :]).then_inc(EV, 1)
                if p == 0:
                    gather_vector(dve, 1)
                    gather_vector(dve, 2)
                if p == 1:
                    gather_vector(dve, 3)
                    gates_vector(dve)
                    dve.drain().then_inc(operand_ready.sem, 1)
                if p % 4 == 3:
                    dve.drain().then_inc(operand_ready.sem, 1)
                    for m in range(KD):
                        b = take_bank(dve, "v")
                        dve.tensor_tensor(X[:, m, :], X[:, m, :], b[:, 0:L], ALU.add).then_inc(EV, 1)
                        if p + 1 < PAIRS:
                            dve.drain()
                        else:
                            dve.drain().then_inc(tile_ready.sem, 1)

        def moe_scalar(act):
            for t, (t0, n) in enumerate(TILES):
                for half in range(2):
                    b = take_bank(act, "a")
                    act.activation(utok[0:n, t, 512 * half:512 * half + 512], b[0:n, :], ACT.Copy).then_inc(EA, 1)
            act.drain().then_inc(aoperand_ready.sem, 1)
            act.wait_ge(for_scalar.sem, for_scalar.next())
            act.activation(aff, aff, ACT.Exp).then_inc(from_scalar.sem, 1)
            for p in range(PAIRS):
                for c0, cw in CHUNKS:
                    b = take_bank(act, "a")
                    act.activation(hs[:, c0:c0 + cw], b[:, 0:cw], ACT.Silu).then_inc(EA, 1)
                    act.drain().then_inc(silu_ready.sem, 1)
                for f0, nf in KSPLIT:
                    b = take_bank(act, "a")
                    act.activation(hidT[:, f0:f0 + nf, :], b[:, 0:nf * P].rearrange("p (f s) -> p f s", s=P), ACT.Copy)\
                        .then_inc(EA, 1)
                act.drain().then_inc(aoperand_ready.sem, 1)

        def make_plan():
            for i in range(4):
                ada_plan(i)
            project_plan(A["ab_w_in"][0], 3072, KD)
            for i in range(4, 4 + LATER[0]):
                ada_plan(i)
            project_plan(A["ab_w_out"][0], D, KD)
            ffn_plan(0)
            odd_plan()
            ffn_plan(1)
            for l in range(DEPTH):
                second_in_plan(l)
                rwkv_plan(l)
                project_plan(A["w_out_2"][l], D, KD)
                moe_plan(l)
        make_plan()

        block = ctx.enter_context(nc.Block())

        @block.tensor
        def _(pe):
            start_tensor(pe)
            end_phase(pe, "pe")
            project_tensor(pe, 3072, KD, hrhs(SEQ), SEQ, fresh=True)
            turn_values_tensor(pe, 8)
            pe.wait_ge(aoperand_ready.sem, aoperand_ready.next())
            attend_tensor(pe, 16, head_rows(att_q), head_rows(att_k),
                          lambda h, t: att_v[:, t, h * HD:(h + 1) * HD], ada_beside_heads(later_ada_tensor, pe))
            pe.wait_ge(operand_ready.sem, operand_ready.next())
            project_tensor(pe, D, KD, lambda k: att_q[:, k, :], SEQ)
            norm_tensor(pe, KD, SEQ)
            norm_tensor(pe, KD, SEQ)
            end_phase(pe, "pe")
            ffn_tensor(pe, 0)
            norm_tensor(pe, KD, SEQ)
            norm_tensor(pe, KD, SEQ)
            end_phase(pe, "pe")
            odd_tensor(pe)
            norm_tensor(pe, KD, SEQ)
            norm_tensor(pe, KD, SEQ)
            end_phase(pe, "pe")
            ffn_tensor(pe, 1)
            norm_tensor(pe, KD, SEQ)
            norm_tensor(pe, KD, L)
            end_phase(pe, "pe")
            for l in range(DEPTH):
                second_in_tensor(pe)
                end_phase(pe, "pe")
                diff_tensor(pe)
                end_phase(pe, "pe")
                gla_tensor(pe, l)
                end_phase(pe, "pe")
                rwkv_tensor(pe, l)
                end_phase(pe, "pe")
                mix_out_tensor(pe)
                norm_tensor(pe, KD, L)
                end_phase(pe, "pe")
                moe_tensor(pe)
                norm_tensor(pe, KD, L)
                end_phase(pe, "pe")
            end_phase(pe, "pe")

        @block.vector
        def _(dve):
            start_vector(dve)
            end_phase(dve, "dve")
            pre_norm_vector(dve, 0, "mix_pre_g", 0, 1)
            project_vector(dve, 3072, even_put(dve))
            dve.drain().then_inc(operand_ready.sem, 1)
            dve.wait_ge(bias_loaded.sem, 16 * 16)
            attend_vector(dve, 16, 0.125, lambda h: att_b[:, h, :], head_rows(att_q), ada_beside_heads(later_ada_vector, dve))
            dve.drain().then_inc(operand_ready.sem, 1)
            project_y_vector(dve)
            post_norm_vector(dve, 0, "mix_post_g", 2)
            end_phase(dve, "dve")
            pre_norm_vector(dve, 0, "ffn_pre_g", 3, 4)
            ffn_first[0] = ntake["v"]
            ffn_vector(dve, 0)
            post_norm_vector(dve, 0, "ffn_post_g", 5)
            end_phase(dve, "dve")
            pre_norm_vector(dve, 1, "mix_pre_g", 0, 1)
            odd_vector(dve)
            post_norm_vector(dve, 1, "mix_post_g", 2)
            end_phase(dve, "dve")
            pre_norm_vector(dve, 1, "ffn_pre_g", 3, 4)
            ffn_first[1] = ntake["v"]
            ffn_vector(dve, 1)
            post_norm_vector(dve, 1, "ffn_post_g", 5)
            end_phase(dve, "dve")
            for l in range(DEPTH):
                second_in_vector(dve, l)
                end_phase(dve, "dve")
                diff_vector(dve, l)
                end_phase(dve, "dve")
                gla_vector(dve, l)
                end_phase(dve, "dve")
                rwkv_vector(dve, l)
                end_phase(dve, "dve")
                mix_out_vector(dve)
                end_phase(dve, "dve")
                moe_vector(dve, l)
                end_phase(dve, "dve")
            gain_norm_vector(dve, "final_g_2", 0)
            end_phase(dve, "dve")

        @block.scalar
        def _(act):
            start_scalar(act)
            norm_scalar(act, XB, KD, SEQ, D)
            end_phase(act, "act")
            turn_values_scalar(act, 8)
            attend_scalar(act, 16)
            norm_scalar(act, H[:, :, 0:SEQ], KD, SEQ, D, tiles=True)
            norm_scalar(act, XB, KD, SEQ, D, tiles=True)
            end_phase(act, "act")
            ffn_scalar(act, 0)
            norm_scalar(act, H[:, :, 0:SEQ], KD, SEQ, D, tiles=True)
            norm_scalar(act, XB, KD, SEQ, D, tiles=True)
            end_phase(act, "act")
            odd_scalar(act)
            norm_scalar(act, H[:, :, 0:SEQ], KD, SEQ, D, tiles=True)
            norm_scalar(act, XB, KD, SEQ, D, tiles=True)
            end_phase(act, "act")
            ffn_scalar(act, 1)
            norm_scalar(act, H[:, :, 0:SEQ], KD, SEQ, D, tiles=True)
            norm_scalar(act, X[:, :, :], KD, L, D, tiles=True)
            end_phase(act, "act")
            for l in range(DEPTH):
                end_phase(act, "act")
                diff_scalar(act)
                end_phase(act, "act")
                gla_scalar(act)
                end_phase(act, "act")
                rwkv_scalar(act)
                end_phase(act, "act")
                norm_scalar(act, X[:, :, :], KD, L, D, tiles=True)
                end_phase(act, "act")
                moe_scalar(act)
                norm_scalar(act, X[:, :, :], KD, L, D, tiles=True)
                end_phase(act, "act")
            end_phase(act, "act")

        @block.gpsimd
        def _(pool):
            ends["pool"] = 1
            pool.drain().then_inc(phase_end, 1)
            bias_pool(pool)
            for n in LATER:
                later_ada_pool(pool, n)
                end_phase(pool, "pool")
            end_phase(pool, "pool")
            for _ in range(DEPTH):
                for _ in range(5):
                    end_phase(pool, "pool")
                moe_pool(pool)
                end_phase(pool, "pool")
            end_phase(pool, "pool")

        @block.sync
        def _(sp):
            sp.dma_start(cst[:, :], A["consts"]).then_inc(loaded.sem, 16)
            sp.dma_start(vec[:, :], A["vectors"]).then_inc(loaded.sem, 16)
            sp.dma_start(X[:, :, META:L], A["xt"]).then_inc(loaded.sem, 16)
            sp.dma_start(X[:, :, 0:META], A["metat"]).then_inc(loaded.sem, 16)
            for i, (src, nk, w) in enumerate(plan):
                if i >= NSLOT:
                    sp.wait_ge(*slot_read[i - NSLOT])
                slot = ring[:, i % NSLOT, 0:nk * w].rearrange("p (k n) -> p k n", k=nk)
                parts = src if type(src) is list else [src]
                for j, part in enumerate(parts):
                    k = nk // len(parts)
                    sp.dma_start(slot[:, j * k:(j + 1) * k, :], part).then_inc(slot_filled[i % NSLOT].sem, 16)
            sp.wait_ge(phase_end, 4 * ends["dve"])
            sp.dma_start(out, H[:, :, :]).then_inc(stored.sem, 16)
            sp.wait_ge(stored.sem, 16)


SHARED = ["ada_w", "ab_w_in", "ab_w_out", "cd_w_in", "mla_w_uq", "mla_w_ukv", "cd_w_out", "ffn_w_up", "ffn_w_down",
          "w_in_2", "rw_w_up_2", "rw_a_up_2", "rw_g_up_2", "w_out_2", "router_2", "e_w1_2", "e_w3_2", "e_w2_2"]


def kernel(**inputs):
    import concourse.bacc as _bacc
    from concourse.bass_utils import run_bass_kernel_spmd as _run

    nc = _bacc.Bacc("TRN2", target_bir_lowering=False, num_devices=1)
    consts, cat = pack(shape_constants())
    vectors, vat = pack(vector_parts(inputs))
    arrays = {"consts": consts, "vectors": vectors}
    x = np.asarray(inputs["x"])[0]
    arrays["xt"] = np.ascontiguousarray(x.T.reshape(KD, P, SEQ).transpose(1, 0, 2))
    meta = np.asarray(inputs["meta_2"])
    arrays["metat"] = np.ascontiguousarray(meta.T.reshape(KD, P, META).transpose(1, 0, 2))
    for n in SHARED:
        arrays[n] = np.ascontiguousarray(inputs[n])
    A = {n: nc.dram_tensor(f"in_{n}", a.shape, FP32, kind="ExternalInput").ap() for n, a in arrays.items()}
    out = nc.dram_tensor("out_0", (P, KD, L), FP32, kind="ExternalOutput").ap()
    build(nc, A, cat, vat, out)
    r = _run(nc, [{f"in_{n}": a for n, a in arrays.items()}], core_ids=[0])
    got = r.results[0]["out_0"]
    return np.ascontiguousarray(got[:, :, META:L].transpose(2, 1, 0).reshape(1, SEQ, D))
```
